# Optimizing a Trainium2 kernel written in Bass

```python
import jax, jax.numpy as jnp
from jax import lax
import numpy as np

D_MODEL = 1024
BATCH = 1
SEQ = 1024
DEPTH = 1

MIX_WIDTH = D_MODEL
CONV_CH = MIX_WIDTH // 2
CONV_GROUPS = 8
CONV_WIDTH = 31
RWKV_HEAD = 64
RWKV_CH = MIX_WIDTH - CONV_CH
RWKV_HEADS = RWKV_CH // RWKV_HEAD
LORA_W = 32
LORA_A = 32
LORA_V = 32
LORA_G = 96
RWKV_IN = 3 * RWKV_CH + LORA_W + LORA_A + LORA_G
IN_COLS = 2 * CONV_CH + RWKV_IN
N_GROUPS = 4
EXPERTS_PER_GROUP = 8
N_EXPERTS = N_GROUPS * EXPERTS_PER_GROUP
TOP_K = 2
EXPERT_FF = 512
MOE_BLOCK = 512
PLE_DIM = 256
NORM_EPS = 1e-6
LN_EPS = 1e-5
GN_EPS = 64e-5

kernel_name = "hymba_conformer_rwkv7_hmoe"

def rms_norm(x, g):
    x32 = x.astype(jnp.float32)
    y = x32 * lax.rsqrt(jnp.mean(x32 * x32, axis=-1, keepdims=True) + NORM_EPS)
    return (y * g.astype(jnp.float32)).astype(x.dtype)

def token_shift(z):
    return jnp.pad(z, ((0, 0), (1, 0), (0, 0)))[:, :-1, :]

def conformer_conv(z, conv_w, conv_b, ln_g, ln_b):
    val, gate = jnp.split(z, 2, axis=-1)
    u = val * jax.nn.sigmoid(gate)
    u = lax.conv_general_dilated(
        u, conv_w[:, None, :].astype(u.dtype), window_strides=(1,),
        padding=[(CONV_WIDTH - 1, 0)],
        dimension_numbers=('NWC', 'WIO', 'NWC'),
        feature_group_count=CONV_CH) + conv_b
    u32 = u.astype(jnp.float32)
    mean = jnp.mean(u32, axis=-1, keepdims=True)
    var = jnp.mean(jnp.square(u32 - mean), axis=-1, keepdims=True)
    un = (u32 - mean) * lax.rsqrt(var + LN_EPS) * ln_g.astype(jnp.float32) + ln_b.astype(jnp.float32)
    return jax.nn.silu(un).astype(z.dtype)

def rwkv7_scan(r, w, k, v, a_vec, b_vec):
    Bb, Ss, H, N = r.shape

    def step(state, inp):
        r_t, w_t, k_t, v_t, a_t, b_t = inp
        sa = jnp.einsum('bhvk,bhk->bhv', state, a_t)
        state = (state * w_t[:, :, None, :]
                 + sa[..., None] * b_t[:, :, None, :]
                 + v_t[..., None] * k_t[:, :, None, :])
        y_t = jnp.einsum('bhvk,bhk->bhv', state, r_t)
        return state, y_t

    xs = tuple(jnp.moveaxis(t, 1, 0) for t in (r, w, k, v, a_vec, b_vec))
    s0 = jnp.zeros((Bb, H, N, N), jnp.float32)
    _, ys = lax.scan(step, s0, xs)
    return jnp.moveaxis(ys, 0, 1)

def rwkv7_time_mix(z, v_first, mu, w0, w2, a0, a2, g2, k_k, k_a, r_k, gn_g, gn_b, vres):
    Bb, Ss, _ = z.shape
    f32 = jnp.float32
    zs = z + (token_shift(z) - z) * mu
    r, k, v, w_lo, a_lo, g_lo = jnp.split(
        zs, [RWKV_CH, 2 * RWKV_CH, 3 * RWKV_CH, 3 * RWKV_CH + LORA_W,
             3 * RWKV_CH + LORA_W + LORA_A], axis=-1)
    w = -jax.nn.softplus(-(w0 + jnp.tanh(w_lo) @ w2)) - 0.5
    decay = jnp.exp(-jnp.exp(w.astype(f32)))
    if vres is None:
        v_first = v
    else:
        v0, v1, v2 = vres
        v = v + (v_first - v) * jax.nn.sigmoid(v0 + (v @ v1) @ v2)
    a = jax.nn.sigmoid(a0 + a_lo @ a2)
    g = jax.nn.sigmoid(g_lo) @ g2
    hs = (Bb, Ss, RWKV_HEADS, RWKV_HEAD)
    kk = (k * k_k).astype(f32).reshape(hs)
    kk = kk / jnp.maximum(jnp.sqrt(jnp.sum(kk * kk, axis=-1, keepdims=True)), 1e-12)
    k = k * (1.0 + (a - 1.0) * k_a)
    r_h = r.astype(f32).reshape(hs)
    k_h = k.astype(f32).reshape(hs)
    v_h = v.astype(f32).reshape(hs)
    a_h = a.astype(f32).reshape(hs)
    y = rwkv7_scan(r_h, decay.reshape(hs), k_h, v_h, -kk, kk * a_h)
    mean = jnp.mean(y, axis=-1, keepdims=True)
    var = jnp.mean(jnp.square(y - mean), axis=-1, keepdims=True)
    y = (y - mean) * lax.rsqrt(var + GN_EPS)
    y = y * gn_g.astype(f32).reshape(RWKV_HEADS, RWKV_HEAD) + gn_b.astype(f32).reshape(RWKV_HEADS, RWKV_HEAD)
    y = y + jnp.sum(r_h * k_h * r_k.astype(f32), axis=-1, keepdims=True) * v_h
    y = y.reshape(Bb, Ss, RWKV_CH).astype(z.dtype) * g
    return y, v_first

def hierarchical_moe(u, wg, bg, we, be, w_gate, w_up, w_down):
    Bb, Ss, D = u.shape
    t = u.reshape(-1, D)
    T = t.shape[0]
    glog = (t @ wg).astype(jnp.float32) + bg.astype(jnp.float32)
    gprob = jax.nn.softmax(glog, axis=-1)
    g_idx = jnp.argmax(glog, axis=-1)
    g_p = jnp.take_along_axis(gprob, g_idx[:, None], axis=1)[:, 0]
    elog_all = jnp.einsum('td,gde->tge', t, we).astype(jnp.float32) + be.astype(jnp.float32)
    elog = jnp.take_along_axis(elog_all, g_idx[:, None, None], axis=1)[:, 0]
    top_v, top_i = lax.top_k(elog, TOP_K)
    gate_w = jax.nn.softmax(top_v, axis=-1) * g_p[:, None]
    e_idx = g_idx[:, None].astype(jnp.int32) * EXPERTS_PER_GROUP + top_i.astype(jnp.int32)

    A = T * TOP_K
    n_blocks = -(-A // MOE_BLOCK) + N_EXPERTS
    P = n_blocks * MOE_BLOCK
    flat_e = e_idx.reshape(-1)
    order = jnp.argsort(flat_e)
    se = flat_e[order]
    tok = (order // TOP_K).astype(jnp.int32)
    gate = gate_w.reshape(-1)[order]
    counts = jnp.zeros((N_EXPERTS,), jnp.int32).at[flat_e].add(1)
    starts = jnp.cumsum(counts) - counts
    pcounts = (counts + MOE_BLOCK - 1) // MOE_BLOCK * MOE_BLOCK
    pend = jnp.cumsum(pcounts)
    pstarts = pend - pcounts
    dest = pstarts[se] + (jnp.arange(A, dtype=jnp.int32) - starts[se])
    buf_tok = jnp.full((P,), T, jnp.int32).at[dest].set(tok)
    buf_gate = jnp.zeros((P,), jnp.float32).at[dest].set(gate)
    blk_e = jnp.minimum(
        jnp.searchsorted(pend, jnp.arange(n_blocks, dtype=jnp.int32) * MOE_BLOCK, side='right'),
        N_EXPERTS - 1)
    t_pad = jnp.concatenate([t, jnp.zeros((1, D), t.dtype)], axis=0)
    xbuf = t_pad[buf_tok].reshape(n_blocks, MOE_BLOCK, D)

    def run_block(args):
        xb, e = args
        hid = jax.nn.silu(xb @ w_gate[e]) * (xb @ w_up[e])
        return hid @ w_down[e]

    ybuf = lax.map(run_block, (xbuf, blk_e)).reshape(P, D)
    ybuf = ybuf * buf_gate[:, None].astype(ybuf.dtype)
    out = jnp.zeros((T + 1, D), t.dtype).at[buf_tok].add(ybuf)[:T]
    return out.reshape(Bb, Ss, D)

def setup_inputs(seed: int = 0) -> dict:
    key = jax.random.key(seed)
    ks = iter(jax.random.split(key, 48))

    def nrm(shape, scale):
        return jax.random.normal(next(ks), shape, jnp.float32) * scale

    def gain(shape):
        return 1.0 + nrm(shape, 0.02)

    L = DEPTH
    Lv = DEPTH - 1
    return {
        "x": nrm((BATCH, SEQ, D_MODEL), 1.0),
        "p": nrm((DEPTH, BATCH, SEQ, PLE_DIM), 1.0),
        "mix_norm": gain((L, D_MODEL)),
        "w_in": nrm((L, D_MODEL, IN_COLS), D_MODEL ** -0.5),
        "conv_w": nrm((L, CONV_WIDTH, CONV_CH), CONV_WIDTH ** -0.5),
        "conv_b": nrm((L, CONV_CH), 0.01),
        "conv_ln_g": gain((L, CONV_CH)),
        "conv_ln_b": nrm((L, CONV_CH), 0.01),
        "rwkv_mu": jax.random.uniform(next(ks), (L, RWKV_IN), jnp.float32),
        "rwkv_w0": -1.5 + nrm((L, RWKV_CH), 0.5),
        "rwkv_w2": nrm((L, LORA_W, RWKV_CH), 0.1),
        "rwkv_a0": nrm((L, RWKV_CH), 0.1),
        "rwkv_a2": nrm((L, LORA_A, RWKV_CH), 0.1),
        "rwkv_g2": nrm((L, LORA_G, RWKV_CH), LORA_G ** -0.5),
        "rwkv_kk": 0.85 + nrm((L, RWKV_CH), 0.02),
        "rwkv_ka": 1.0 + nrm((L, RWKV_CH), 0.02),
        "rwkv_rk": nrm((L, RWKV_HEADS, RWKV_HEAD), 0.1),
        "rwkv_gn_g": gain((L, RWKV_CH)),
        "rwkv_gn_b": nrm((L, RWKV_CH), 0.01),
        "rwkv_v0": nrm((Lv, RWKV_CH), 0.1),
        "rwkv_v1": nrm((Lv, RWKV_CH, LORA_V), RWKV_CH ** -0.5),
        "rwkv_v2": nrm((Lv, LORA_V, RWKV_CH), 0.1),
        "w_out": nrm((L, MIX_WIDTH, D_MODEL), MIX_WIDTH ** -0.5),
        "ffn_norm": gain((L, D_MODEL)),
        "router_group_w": nrm((L, D_MODEL, N_GROUPS), D_MODEL ** -0.5),
        "router_group_b": nrm((L, N_GROUPS), 0.01),
        "router_expert_w": nrm((L, N_GROUPS, D_MODEL, EXPERTS_PER_GROUP), D_MODEL ** -0.5),
        "router_expert_b": nrm((L, N_GROUPS, EXPERTS_PER_GROUP), 0.01),
        "expert_w_gate": nrm((L, N_EXPERTS, D_MODEL, EXPERT_FF), D_MODEL ** -0.5),
        "expert_w_up": nrm((L, N_EXPERTS, D_MODEL, EXPERT_FF), D_MODEL ** -0.5),
        "expert_w_down": nrm((L, N_EXPERTS, EXPERT_FF, D_MODEL), EXPERT_FF ** -0.5),
        "ple_norm": gain((L, D_MODEL)),
        "ple_gate_w": nrm((L, D_MODEL, D_MODEL), D_MODEL ** -0.5),
        "ple_proj_w": nrm((L, PLE_DIM, D_MODEL), PLE_DIM ** -0.5),
        "final_norm": gain((D_MODEL,)),
    }

def reference(x, p, mix_norm, w_in, conv_w, conv_b, conv_ln_g, conv_ln_b,
              rwkv_mu, rwkv_w0, rwkv_w2, rwkv_a0, rwkv_a2, rwkv_g2, rwkv_kk, rwkv_ka,
              rwkv_rk, rwkv_gn_g, rwkv_gn_b, rwkv_v0, rwkv_v1, rwkv_v2, w_out,
              ffn_norm, router_group_w, router_group_b, router_expert_w, router_expert_b,
              expert_w_gate, expert_w_up, expert_w_down, ple_norm, ple_gate_w, ple_proj_w,
              final_norm):
    h = x
    v_first = None
    for i in range(DEPTH):
        u = rms_norm(h, mix_norm[i])
        z = u @ w_in[i]
        z_conv = z[..., :2 * CONV_CH]
        z_rwkv = z[..., 2 * CONV_CH:]
        y_conv = conformer_conv(z_conv, conv_w[i], conv_b[i], conv_ln_g[i], conv_ln_b[i])
        vres = None if i == 0 else (rwkv_v0[i - 1], rwkv_v1[i - 1], rwkv_v2[i - 1])
        y_rwkv, v_first = rwkv7_time_mix(
            z_rwkv, v_first, rwkv_mu[i], rwkv_w0[i], rwkv_w2[i], rwkv_a0[i], rwkv_a2[i],
            rwkv_g2[i], rwkv_kk[i], rwkv_ka[i], rwkv_rk[i], rwkv_gn_g[i], rwkv_gn_b[i], vres)
        h = h + jnp.concatenate([y_conv, y_rwkv], axis=-1) @ w_out[i]
        h = h + hierarchical_moe(rms_norm(h, ffn_norm[i]), router_group_w[i], router_group_b[i],
                                 router_expert_w[i], router_expert_b[i], expert_w_gate[i],
                                 expert_w_up[i], expert_w_down[i])
        gate = jax.nn.sigmoid(rms_norm(h, ple_norm[i]) @ ple_gate_w[i])
        h = h + gate * (p[i] @ ple_proj_w[i])
    return rms_norm(h, final_norm)


_drawn_inputs = setup_inputs


def setup_inputs(seed=0):
    import zlib

    import numpy as np

    out = dict(_drawn_inputs(seed))
    spreads = {}
    factors = {'conv_b': 3.213,
     'conv_ln_g': 3.378,
     'conv_ln_b': 5.113,
     'rwkv_kk': 8.0,
     'rwkv_ka': 4.146,
     'rwkv_gn_g': 3.844,
     'rwkv_gn_b': 8.0,
     'ffn_norm': 2.786,
     'router_group_b': 8.0,
     'router_expert_b': 3.954,
     'ple_norm': 8.0,
     'final_norm': 2.851}
    for name, (base, spread) in spreads.items():
        noise = np.random.default_rng([zlib.crc32(name.encode()), seed]).standard_normal(out[name].shape)
        drawn = base * np.exp(spread * noise) if base else spread * noise
        out[name] = __import__('jax').numpy.asarray(drawn.astype(out[name].dtype))
    for name, factor in factors.items():
        out[name] = (out[name] * factor).astype(out[name].dtype)
    return out
```

```python
from contextlib import ExitStack

import numpy as np
import concourse.bass as bass
from concourse import mybir

F32 = mybir.dt.float32
BF16 = mybir.dt.bfloat16
I32 = mybir.dt.int32
U32 = mybir.dt.uint32
ALU = mybir.AluOpType
ACT = mybir.ActivationFunctionType
AX_X = mybir.AxisListType.X

P = 128
T = 1024
D = 1024
KT = D // P
TT = T // P
HALF = 512
PAIRS = 4
HD = 64
C = 64
NCH = T // C
TAPS = 31
G = 4
EPG = 8
E = G * EPG
FF = 512
BLK = 128
ARENA = 192
OVF = 15
NBLK = E + OVF
ZEROS = NBLK + OVF
PLE = 256
DECAY = float(np.exp(-0.5)) / 2.0
LEVELS = (2, 4, 8, 16, 32)

_cols = [("mixg", KT), ("mu_r", 4), ("mu_k", 4), ("mu_v", 4), ("w0", 4), ("a0", 4), ("kk", 4), ("ka", 4),
         ("rk", 4), ("gng", 4), ("gnb", 4), ("convb", 4), ("lng", 4), ("lnb", 4), ("convw", 4 * TAPS),
         ("mu_wa", 1), ("mu_g", 1), ("pleg", KT)]
VCOL, _n = {}, 0
for _name, _w in _cols:
    VCOL[_name] = _n
    _n += _w
VEC = _n

_ccols = [("ident", 128), ("istack", 64), ("before", 128), ("ones", 128), ("bones", 128), ("sel2", 2),
          ("selT2", 128), ("strict", 64), ("strict2", 128), ("incl2", 128), ("first2", 128),
          ("levels2", 5 * 128), ("ebase", E), ("prefer4", 4), ("prefer8", 8), ("iotam", OVF)]
CCOL, _n = {}, 0
for _name, _w in _ccols:
    CCOL[_name] = _n
    _n += _w
CST = _n


def constants():
    c = np.zeros((P, CST), np.float32)

    def put(name, a):
        a = np.asarray(a, np.float32)
        c[:a.shape[0], CCOL[name]:CCOL[name] + a.shape[1]] = a

    j = np.arange(P)[:, None] % C
    hj = np.arange(P)[:, None] // C
    t = np.arange(C)[None, :]
    both = lambda m: np.concatenate([m * (hj == 0), m * (hj == 1)], axis=1)
    put("ident", np.eye(P))
    put("istack", j == t)
    put("before", np.arange(P)[:, None] < np.arange(P)[None, :])
    put("ones", np.ones((P, P)))
    put("bones", hj == np.arange(P)[None, :] // C)
    put("sel2", hj == np.arange(2)[None, :])
    c[64:66, CCOL["selT2"]:CCOL["selT2"] + P] = np.arange(2)[:, None] == np.arange(P)[None, :] // C
    put("strict", j < t)
    put("strict2", both(j < t))
    put("incl2", both(j <= t))
    put("first2", both((j // 2 == t // 2) & (j < t)))
    put("levels2", np.concatenate([both((j // (2 * s) == t // (2 * s)) & (j % (2 * s) < s) & (t % (2 * s) >= s))
                                   for s in LEVELS], axis=1))
    put("ebase", np.broadcast_to(BLK * np.arange(E)[None, :], (P, E)))
    put("prefer4", np.broadcast_to(8.0 - np.arange(4)[None, :], (P, 4)))
    put("prefer8", np.broadcast_to(8.0 - np.arange(8)[None, :], (P, 8)))
    put("iotam", np.broadcast_to(np.arange(OVF)[None, :], (P, OVF)))
    return c


class Chain:

    def __init__(self, eng, sem):
        self.eng, self.sem, self.base, self.n = eng, sem, 0, 0

    def link(self, ins):
        self.n += 1
        ins.then_inc(self.sem, 1)
        self.eng.wait_ge(self.sem, self.base + self.n)

    def enter(self, i, per):
        self.outer, self.per = self.base + self.n, per
        self.base, self.n = self.outer + i * per, 0

    def leave(self, count):
        assert self.n == self.per, (self.n, self.per)
        self.base, self.n = self.outer + count * self.per, 0


def program(nc, t):
    with ExitStack() as ctx:
        def sb(name, shape, dt=F32, where=ctx):
            return where.enter_context(nc.sbuf_tensor(name, shape, dt))

        def sem(name):
            return ctx.enter_context(nc.semaphore(name))

        ps = ctx.enter_context(nc.psum_tensor("ps", [P, 8, HALF], F32))

        vec = sb("vec", [P, VEC])
        cst = sb("cst", [P, CST])
        sg_lo = sb("sg_lo", [96, T])

        eps_rms = sb("eps_rms", [P, 1])
        eps_ln = sb("eps_ln", [P, 1])
        eps_gn = sb("eps_gn", [P, 1])
        w0h = sb("w0h", [P, PAIRS])
        a0h = sb("a0h", [P, PAIRS])
        lngh = sb("lngh", [P, PAIRS])
        lnbh = sb("lnbh", [P, PAIRS])
        convwh = sb("convwh", [P, PAIRS * TAPS])

        reset = sb("reset", [P, T], BF16)
        ssq, std, rstd, ssq2, std2, rstd2 = (sb(f"stat{q}", [P, TT]) for q in range(6))
        gate = [sb(f"gate{q}", [P, TT]) for q in range(2)]
        slot = [sb(f"slot{q}", [P, TT], U32) for q in range(2)]
        ctl = sb("ctl", [1, OVF + 1], I32)
        PCH = sb("PCH", [P, NCH, PAIRS])

        def V(name, i=0, n=1, rows=P):
            return vec[0:rows, VCOL[name] + i:VCOL[name] + i + n]

        def VD(name, i):
            return vec[:, bass.ds(i + VCOL[name], 1)]

        def flat(x):
            return x[:, :, :].rearrange("p a c -> p (a c)")

        def flat2(x):
            return x.rearrange("p a b c -> p (a b c)")

        def twice(x):
            return x.unsqueeze(2).to_broadcast([P, PAIRS, 2, C])

        def over_pairs(m):
            return m.unsqueeze(1).to_broadcast([P, PAIRS, C])

        def over_pairs2(m):
            return m.rearrange("p (a c) -> p a c", a=2).unsqueeze(1).to_broadcast([P, PAIRS, 2, C])

        def K(name, n=None, rows=P):
            w = dict(_ccols)[name]
            return cst[0:rows, CCOL[name]:CCOL[name] + (n or w)]

        arena = sb("arena", [P, ARENA * 256])

        class Region:

            def __init__(self, kib):
                self.at = int(kib * 256)

            def take(self, *shape, rows=P):
                n = int(np.prod(shape))
                x = arena[0:rows, self.at:self.at + n]
                self.at += n
                assert self.at <= ARENA * 256
                if len(shape) == 1:
                    return x
                names = "abcde"[:len(shape)]
                return x.rearrange(f"p ({' '.join(names)}) -> p {' '.join(names)}",
                                   **{q: w for q, w in zip(names[1:], shape[1:])})

        m = Region(0)
        pk = m.take(NCH, PAIRS, 5, C)

        m = Region(80)
        uT = m.take(KT, T)
        wz = [m.take(KT * P) for s in range(3)]
        wa2 = m.take(P, rows=2 * 32)
        zr, zk, zv = (m.take(T + 1) for _ in range(3))
        zval = m.take(T)
        b_ld = m.take(T)
        b_e1 = m.take(T)
        b_c = m.take(T)
        b_a = m.take(T)
        b_rs = m.take(T)
        b_ks = m.take(T)
        b_t = m.take(T)
        b_kk = m.take(T)
        b_sq = m.take(T)
        lora_nrm = m.take(T)
        lora = lora_nrm[0:64, :]
        nrm = lora_nrm[64:66, :]
        wl = lora
        glu = m.take(TAPS - 1 + T)
        yc = m.take(T)
        xin = [zr, zk]
        xn = [zv, zval]

        m = Region(80)
        Yall = m.take(NCH, PAIRS, HD)
        yconv = m.take(PAIRS, T)
        bdx = [m.take(PAIRS * 5, 2, C) for b in range(2)]
        ktb = [[m.take(PAIRS, P) for b in range(2)] for q in range(2)]
        vtk = [m.take(PAIRS, HD) for b in range(2)]
        aak, arb, ark = ([m.take(PAIRS, 2, C) for b in range(2)] for _ in range(3))
        LT = [m.take(PAIRS, C) for b in range(2)]
        Loff = [[m.take(PAIRS, 2, C) for q in range(2)] for b in range(2)]
        Ti2, TiT2, X2 = ([m.take(PAIRS, 2, C) for b in range(2)] for _ in range(3))
        R, U, S0, S1, Stmp = (m.take(PAIRS, HD) for _ in range(5))
        S = [S0, S1]
        zero = m.take(D)

        m = Region(112)
        yT = m.take(PAIRS, T)
        wout = m.take(KT, D)
        hb = [m.take(T) for _ in range(5)]
        squares = [hb[q] for q in (0, 1, 3, 4)]
        Ybd = m.take(NCH, 2, C)
        g2s = m.take(P, rows=96)
        bonesrk = m.take(P)
        gst = m.take(4, NCH)

        m = Region(0)
        h = m.take(TT, D)
        u2 = m.take(TT, D)
        yTs = [m.take(KT, P) for b in range(2)]
        xo = [m.take(D) for b in range(2)]
        u2s = [m.take(D) for b in range(2)]
        u2T = m.take(KT, P)
        fgain = m.take(D)
        m = Region(160)
        rw = m.take(KT, G + E)
        rbias = m.take(G + E)
        osq = m.take(D)
        lg = m.take(TT, G + E)
        r_a = m.take(TT, E)
        r_b = m.take(TT, E)
        O1, O2, Os, slotm, rank, tbase = (m.take(TT, E) for _ in range(6))
        og, gl1, gl2 = (m.take(TT, G) for _ in range(3))
        esel, e2nd, o1, o2, ew = (m.take(TT, EPG) for _ in range(5))
        gmax, gtop, gsum, gp, m1, m2, etop, dm = (m.take(TT) for _ in range(8))
        cnt, nb, incl, excl = (m.take(E) for _ in range(4))
        ovc = m.take(OVF, E)
        ov = m.take(OVF + 1)

        m = Region(32)
        xb = [m.take(D) for b in range(2)]
        xTs = m.take(KT, P)
        th = m.take(FF)
        hid = m.take(FF)
        hTs = m.take(FF // P, P)
        ys = [m.take(D) for b in range(2)]
        m = Region(96)
        wg, wu, wd = ([], [], [])
        for b in range(2):
            wg.append(m.take(KT, FF))
            wu.append(m.take(KT, FF))
            wd.append(m.take(FF // P, D))

        m = Region(64)
        plew = m.take(KT, D)
        m = Region(96)
        projw = m.take(PLE // P, D)
        yg = [[m.take(D) for k in range(2)] for b in range(2)]
        hs, ns, ob, oq, th2 = ([m.take(D) for b in range(2)] for _ in range(5))
        nT = m.take(KT, P)
        pin = [m.take(PLE) for b in range(2)]
        pT = m.take(PLE // P, P)
        lastg = m.take(D)

        s_const = sem("s_const")
        s_x = [sem(f"s_x{b}") for b in range(2)]
        s_std = sem("s_std"); s_xn = sem("s_xn"); s_xT = sem("s_xT"); s_uT = sem("s_uT")
        s_w = [sem(f"s_w{s}") for s in range(3)]
        s_zmm = [sem(f"s_zmm{s}") for s in range(3)]
        s_z = [sem(f"s_z{s}") for s in range(3)]
        s_wa2 = sem("s_wa2"); s_lora = sem("s_lora"); s_glo = sem("s_glo")
        s_dmm = sem("s_dmm"); s_dth = sem("s_dth"); s_amm = sem("s_amm"); s_ath = sem("s_ath")
        s_c = sem("s_c")
        s_exp = sem("s_exp"); s_kkr = sem("s_kkr"); s_sq = sem("s_sq")
        s_ssmm = sem("s_ssmm"); s_nrm = sem("s_nrm"); s_rn = sem("s_rn"); s_bcmm = sem("s_bcmm"); s_kk = sem("s_kk")
        s_pair = sem("s_pair"); s_yc = sem("s_yc"); s_ycst = sem("s_ycst"); s_prep = sem("s_prep")
        s_dve = sem("s_dve"); s_act = sem("s_act"); s_pool = sem("s_pool")
        s_bdz = sem("s_bdz")
        s_bdx = [sem(f"s_bdx{b}") for b in range(2)]
        s_gram = [sem(f"s_gram{b}") for b in range(2)]
        s_turn = [sem(f"s_turn{b}") for b in range(2)]
        s_msk = [sem(f"s_msk{b}") for b in range(2)]
        s_tok = [sem(f"s_tok{b}") for b in range(2)]
        s_loff = [sem(f"s_loff{b}") for b in range(2)]
        s_xmm = [sem(f"s_xmm{b}") for b in range(2)]
        s_x2 = [sem(f"s_x2{b}") for b in range(2)]
        s_tmm = [sem(f"s_tmm{b}") for b in range(2)]
        s_ti = [sem(f"s_ti{b}") for b in range(2)]
        s_tt = [sem(f"s_tt{b}") for b in range(2)]
        s_scan = sem("s_scan")
        s_ru = sem("s_ru")
        s_s = sem("s_s"); s_y = sem("s_y")
        s_ti0 = [sem(f"s_ti0{b}") for b in range(2)]

        s_zero = sem("s_zero"); s_zf = sem("s_zf"); s_ycl = sem("s_ycl"); s_wout = sem("s_wout"); s_g2 = sem("s_g2")
        s_lnm = sem("s_lnm"); s_lnc = sem("s_lnc"); s_lnsq = sem("s_lnsq"); s_lnq = sem("s_lnq"); s_lns = sem("s_lns")
        s_lnn = sem("s_lnn"); s_lnt = sem("s_lnt"); s_lny = sem("s_lny")
        s_gc = sem("s_gc"); s_gsq = sem("s_gsq"); s_gp = sem("s_gp"); s_gv = sem("s_gv"); s_gsd = sem("s_gsd")
        s_gy = sem("s_gy"); s_gt = sem("s_gt"); s_gs = sem("s_gs"); s_gmm = sem("s_gmm"); s_go = sem("s_go")
        s_xo = [sem(f"s_xo{b}") for b in range(2)]
        s_rw = sem("s_rw"); s_yts = sem("s_yts"); s_omm = sem("s_omm"); s_h = sem("s_h");
        s_sd2 = sem("s_sd2"); s_u2 = sem("s_u2"); s_u2c = sem("s_u2c"); s_t2 = sem("s_t2"); s_u2T = sem("s_u2T")
        s_lmm = sem("s_lmm"); s_lg = sem("s_lg"); s_rte = sem("s_rte"); s_rta = sem("s_rta"); s_cmm = sem("s_cmm")
        s_slot = sem("s_slot"); s_ctl = sem("s_ctl"); s_sc = sem("s_sc")
        s_wg, s_wu, s_wd, s_xb = ([sem(f"s_{q}{b}") for b in range(2)] for q in ("wg", "wu", "wd", "xb"))
        s_xtm = sem("s_xtm"); s_xts = sem("s_xts"); s_gu = sem("s_gu"); s_th = sem("s_th"); s_hid = sem("s_hid")
        s_htm = sem("s_htm"); s_hts = sem("s_hts"); s_dn = sem("s_dn"); s_ye = sem("s_ye")
        s_yst = [sem(f"s_yst{b}") for b in range(2)]
        s_pw = sem("s_pw"); s_yg = [sem(f"s_yg{b}") for b in range(2)]; s_pin = [sem(f"s_pin{b}") for b in range(2)]
        s_hs = sem("s_hs"); s_sd3 = sem("s_sd3"); s_ns = sem("s_ns"); s_ntm = sem("s_ntm")
        s_nT = sem("s_nT"); s_plm = sem("s_plm"); s_ptm = sem("s_ptm"); s_pT = sem("s_pT"); s_prm = sem("s_prm")
        s_th3 = sem("s_th3"); s_ob = sem("s_ob"); s_sd4 = sem("s_sd4"); s_of = sem("s_of")
        s_out = [sem(f"s_out{b}") for b in range(2)]

        NL = len(LEVELS)
        block = ctx.enter_context(nc.Block())

        @block.sync
        def _(sp):
            sp.sem_inc(s_ycst, 16)
            sp.dma_start(cst[:, :], t["cst"]).then_inc(s_const, 16)
            sp.dma_start(vec[:, :], t["vec"]).then_inc(s_const, 16)
            xv = t["x"].rearrange("(t p) d -> t p d", p=P)
            for b in range(2):
                sp.dma_start(xin[b][:, 0:D], xv[b]).then_inc(s_x[b], 16)
            sp.dma_start(wz[0][:, 0:KT * 64], t["w_wa"]).then_inc(s_w[0], 16)
            sp.dma_start(wz[1][:, 0:KT * 96], t["w_g"]).then_inc(s_w[1], 16)
            sp.dma_start(wz[2][:, :], t["w_rkv"][2]).then_inc(s_w[2], 16)
            sp.dma_start(wa2[:, :], t["wa2"][0]).then_inc(s_wa2, 16)
            with sp.Fori(1, TT // 2) as i:
                for b in range(2):
                    sp.wait_ge(s_xn, 2 * i + b - 1)
                    sp.dma_start(xin[b][:, 0:D], xv[2 * i + b]).then_inc(s_x[b], 16)
            for s, tile in ((0, 0), (1, 1)):
                sp.wait_ge(s_zmm[s], 1)
                sp.dma_start(wz[s][:, :], t["w_rkv"][tile]).then_inc(s_w[s], 16)
            with sp.Fori(0, PAIRS - 1) as j:
                for s in range(2):
                    sp.wait_ge(s_zmm[s], 2 * j + 2)
                    sp.dma_start(wz[s][:, :], t["w_conv"][2 * j + s]).then_inc(s_w[s], 16)
                sp.wait_ge(s_zmm[2], j + 2)
                sp.dma_start(wz[2][:, :], t["w_rkv"][3 * j + 5]).then_inc(s_w[2], 16)
                sp.wait_ge(s_amm, j + 1)
                sp.dma_start(wa2[:, :], t["wa2"][j + 1]).then_inc(s_wa2, 16)
                for s in range(2):
                    sp.wait_ge(s_zmm[s], 2 * j + 3)
                    sp.dma_start(wz[s][:, :], t["w_rkv"][3 * j + 3 + s]).then_inc(s_w[s], 16)
                sp.wait_ge(s_yc, j + 1)
                sp.dma_start(t["yconv"][j], yc[:, :]).then_inc(s_ycst, 16)
            for s in range(2):
                sp.wait_ge(s_zmm[s], 2 * PAIRS)
                sp.dma_start(wz[s][:, :], t["w_conv"][2 * (PAIRS - 1) + s]).then_inc(s_w[s], 16)
            sp.wait_ge(s_yc, PAIRS)
            sp.dma_start(t["yconv"][PAIRS - 1], yc[:, :]).then_inc(s_ycst, 16)
            sp.wait_ge(s_ycst, 16 * (PAIRS + 1))
            for j in range(PAIRS):
                sp.dma_start(yconv[:, j, :], t["yconv"][j]).then_inc(s_ycl, 16)
            sp.wait_ge(s_zero, 1)
            with sp.Fori(0, NBLK) as n:
                sp.dma_start(t["xbuf"][bass.ds(n * BLK, BLK), :], zero[:, :]).then_inc(s_zf, 16)
            with sp.Fori(E, NBLK) as n:
                sp.dma_start(t["ybuf"][bass.ds(n * BLK, BLK), :], zero[:, :]).then_inc(s_zf, 16)
            sp.wait_ge(s_zf, 16 * ZEROS)
            sp.wait_ge(s_y, NCH + 2)
            sp.wait_ge(s_s, NCH + 1)
            sp.dma_start(g2s[:, :], t["g2"][0]).then_inc(s_g2, 16)
            sp.dma_start(wout[:, :, :], t["w_out"].rearrange("(k p) d -> p k d", p=P)).then_inc(s_wout, 16)
            with sp.Fori(1, PAIRS) as p:
                sp.wait_ge(s_gmm, p)
                sp.dma_start(g2s[:, :], t["g2"][p]).then_inc(s_g2, 16)
            sp.wait_ge(s_go, PAIRS)
            for b in range(2):
                sp.dma_start(xo[b][:, :], xv[b]).then_inc(s_xo[b], 16)
            sp.dma_start(rw[:, :, :], t["rw"].rearrange("(k p) n -> p k n", p=P)).then_inc(s_rw, 16)
            sp.dma_start(rbias[:, :], t["rb"].partition_broadcast(P)).then_inc(s_rw, 16)
            sp.dma_start(fgain[:, :], t["ffg"].partition_broadcast(P)).then_inc(s_rw, 16)
            with sp.Fori(1, TT // 2) as i:
                for b in range(2):
                    sp.wait_ge(s_h, 2 * i + b + 1)
                    sp.dma_start(xo[b][:, :], xv[2 * i + b]).then_inc(s_xo[b], 16)

            def gate_up_weights(b, e):
                sp.dma_start(wg[b][:, :, :], t["wg"][e].rearrange("(k p) f -> p k f", p=P)).then_inc(s_wg[b], 16)
                sp.dma_start(wu[b][:, :, :], t["wu"][e].rearrange("(k p) f -> p k f", p=P)).then_inc(s_wu[b], 16)

            def down_weights(b, e):
                sp.dma_start(wd[b][:, :, :], t["wd"][e].rearrange("(k p) d -> p k d", p=P)).then_inc(s_wd[b], 16)

            def block_rows(b, n):
                sp.dma_start(xb[b][:, :], t["xbuf"][bass.ds(n * BLK, BLK), :]).then_inc(s_xb[b], 16)

            sp.wait_ge(s_slot, 2)
            sp.wait_ge(s_ctl, 1)
            for e in range(2):
                gate_up_weights(e, e)
                down_weights(e, e)
            sp.wait_ge(s_sc, 16 * 2 * TT)
            block_rows(0, 0)
            block_rows(1, 1)
            sp.dma_start(plew[:, :, :], t["plew"].rearrange("(k p) d -> p k d", p=P)).then_inc(s_pw, 16)
            with sp.Fori(0, E // 2 - 1) as i:
                for b in range(2):
                    e = 2 * i + b
                    sp.wait_ge(s_xtm, e + 1)
                    block_rows(b, e + 2)
                    sp.wait_ge(s_gu, e + 1)
                    gate_up_weights(b, e + 2)
                    sp.wait_ge(s_dn, e + 1)
                    down_weights(b, e + 2)
            novf = sp.value_load(ctl[0:1, OVF:OVF + 1], min_val=0, max_val=OVF)
            with sp.Fori(0, OVF) as n:
                with sp.If(novf > n):
                    e = sp.value_load(ctl[0:1, bass.ds(n, 1)], min_val=0, max_val=E - 1)
                    sp.wait_ge(s_xtm, n + E)
                    block_rows(0, n + E)
                    sp.wait_ge(s_gu, n + E)
                    sp.dma_start(wg[0][:, :, :], t["wg"][bass.ds(e, 1)].rearrange("o (k p) f -> p (o k) f", p=P))\
                        .then_inc(s_wg[0], 16)
                    sp.dma_start(wu[0][:, :, :], t["wu"][bass.ds(e, 1)].rearrange("o (k p) f -> p (o k) f", p=P))\
                        .then_inc(s_wu[0], 16)
                    sp.wait_ge(s_dn, n + E)
                    sp.dma_start(wd[0][:, :, :], t["wd"][bass.ds(e, 1)].rearrange("o (k p) d -> p (o k) d", p=P))\
                        .then_inc(s_wd[0], 16)
                    sp.nop()
                with sp.Else():
                    sp.nop()
            sp.wait_ge(s_dn, E + OVF)
            sp.dma_start(projw[:, :, :], t["projw"].rearrange("(k p) d -> p k d", p=P)).then_inc(s_pw, 16)
            sp.dma_start(lastg[:, :], t["lastg"].partition_broadcast(P)).then_inc(s_pw, 16)
            pv = t["p"].rearrange("(t p) d -> t p d", p=P)
            for b in range(2):
                sp.dma_start(pin[b][:, :], pv[b]).then_inc(s_pin[b], 16)
            with sp.Fori(1, TT // 2) as i:
                for b in range(2):
                    sp.wait_ge(s_ptm, 2 * i + b - 1)
                    sp.dma_start(pin[b][:, :], pv[2 * i + b]).then_inc(s_pin[b], 16)
            for b in range(2):
                sp.wait_ge(s_out[b], 16 * (TT // 2 + 1))

        @block.tensor
        def _(pe):
            pe.sem_inc(s_zmm[2], 1)
            pe.wait_ge(s_const, 32)
            ident = K("ident")
            with pe.Fori(0, TT // 2) as i:
                for b in range(2):
                    pe.wait_ge(s_xn, 2 * i + b + 1)
                    pe.wait_ge(s_uT, 2 * i + b + 1)
                    for k in range(KT):
                        last = pe.transpose(ps[:, 2 * b + k // 4, (k % 4) * P:(k % 4 + 1) * P],
                                            xn[b][:, k * P:(k + 1) * P], ident)
                    last.then_inc(s_xT, 1)
            pe.wait_ge(s_uT, TT + 2)

            def z_tile(s, n, cols=P):
                pe.wait_ge(s_w[s], 16 * (n + 1) if s < 2 else 16 * n)
                if not (isinstance(n, int) and n == 0):
                    pe.wait_ge(s_z[s], n)
                for h in range(2):
                    for k in range(KT):
                        last = pe.matmul(ps[0:cols, 2 * s + h, :], wz[s][:, k * cols:(k + 1) * cols],
                                         uT[:, k, h * HALF:(h + 1) * HALF], start=(k == 0), stop=(k == KT - 1))
                last.then_inc(s_zmm[s], 1)

            z_tile(0, 0, 64)
            z_tile(1, 0, 96)
            pe.wait_ge(s_lora, 2)
            with pe.Fori(0, PAIRS) as j:
                pe.wait_ge(s_wa2, 16 * j + 16)
                pe.wait_ge(s_kk, j + 1)
                for h in range(2):
                    last = pe.matmul(ps[:, 6 + h, :], wa2[0:32, :], wl[0:32, h * HALF:(h + 1) * HALF],
                                     start=True, stop=True)
                last.then_inc(s_dmm, 1)
                z_tile(0, 2 * j + 1)
                pe.wait_ge(s_dth, j + 1)
                for h in range(2):
                    last = pe.matmul(ps[:, 6 + h, :], wa2[32:64, :], wl[32:64, h * HALF:(h + 1) * HALF],
                                     start=True, stop=True)
                last.then_inc(s_amm, 1)
                z_tile(1, 2 * j + 1)
                z_tile(2, j + 1)
                z_tile(0, 2 * j + 2)
                pe.wait_ge(s_sq, j + 1)
                pe.wait_ge(s_ath, j + 1)
                for h in range(2):
                    last = pe.matmul(ps[64:66, 6 + h, :], K("sel2"), b_sq[:, h * HALF:(h + 1) * HALF],
                                     start=True, stop=True)
                last.then_inc(s_ssmm, 1)
                z_tile(1, 2 * j + 2)
                pe.wait_ge(s_rn, j + 1)
                for h in range(2):
                    last = pe.matmul(ps[:, 6 + h, :], cst[64:66, CCOL["selT2"]:CCOL["selT2"] + P], nrm[:, h * HALF:(h + 1) * HALF],
                                     start=True, stop=True)
                last.then_inc(s_bcmm, 1)

            pe.wait_ge(s_pair, PAIRS + 1)
            pe.wait_ge(s_z[1], 2 * PAIRS + 1)
            pe.wait_ge(s_z[0], 2 * PAIRS + 1)

            def bank(b, q, w):
                return ps[:, 3 * b + q, 0:PAIRS * w].rearrange("p (a w) -> p a w", a=PAIRS)

            scan6 = ps[:, 6, 0:PAIRS * HD].rearrange("p (a w) -> p a w", a=PAIRS)
            scan6u = ps[:, 6, 256:512].rearrange("p (a w) -> p a w", a=PAIRS)
            scan7 = ps[:, 7, 0:PAIRS * HD].rearrange("p (a w) -> p a w", a=PAIRS)

            def bd(b, p, kind):
                return bdx[b][:, 5 * p + kind, :, :].rearrange("p a c -> p (a c)")

            def two(x, p):
                return x[:, p, :, :].rearrange("p a c -> p (a c)")

            pe.wait_ge(s_s, 1)
            with pe.Fori(0, NCH // 2) as i:
                for b in range(2):
                    c = 2 * i + b
                    ar = [pk[:, bass.ds(c, 1), p, 0:2, :].rearrange("p o a c -> p (o a c)") for p in range(PAIRS)]
                    pe.wait_ge(s_bdx[b], i + 1)
                    for p in range(PAIRS):
                        last = pe.matmul(bank(b, 0, P)[:, p, :], bd(b, p, 2), ar[p], start=True, stop=True)
                    last.then_inc(s_gram[b], 1)
                    for p in range(PAIRS):
                        last = pe.matmul(bank(b, 1, P)[:, p, :], bd(b, p, 3), ar[p], start=True, stop=True)
                    last.then_inc(s_gram[b], 1)
                    for p in range(PAIRS):
                        last = pe.transpose(bank(b, 2, P)[:, p, :], bd(b, p, 2), ident)
                    last.then_inc(s_turn[b], 1)
                for b in range(2):
                    pe.wait_ge(s_msk[b], 3 * i + 2)
                    for p in range(PAIRS):
                        last = pe.transpose(bank(b, 0, P)[:, p, :], bd(b, p, 3), ident)
                    last.then_inc(s_turn[b], 1)
                    pe.wait_ge(s_msk[b], 3 * i + 3)
                    for p in range(PAIRS):
                        last = pe.matmul(bank(b, 1, HD)[:, p, :], bd(b, p, 4), K("istack"), start=True, stop=True)
                    last.then_inc(s_turn[b], 1)
                for b in range(2):
                    pe.wait_ge(s_tok[b], 3 * i + 1)
                    pe.wait_ge(s_ti0[b], i + 1)
                    for p in range(PAIRS):
                        last = pe.transpose(bank(b, 2, P)[:, p, :], two(TiT2[b], p), ident)
                    last.then_inc(s_tmm[b], 1)
                for lv in range(NL):
                    for b in range(2):
                        pe.wait_ge(s_loff[b], NL * i + lv + 1)
                        pe.wait_ge(s_ti[b], NL * i + lv + 1)
                        if lv == 0:
                            pe.wait_ge(s_tok[b], 3 * i + 3)
                        for p in range(PAIRS):
                            last = pe.matmul(bank(b, 0, P)[:, p, :], two(Loff[b][lv % 2], p), two(Ti2[b], p),
                                             start=True, stop=True)
                        last.then_inc(s_xmm[b], 1)
                    for b in range(2):
                        if lv > 0:
                            pe.wait_ge(s_tt[b], NL * i + lv)
                        pe.wait_ge(s_x2[b], NL * i + lv + 1)
                        if lv < NL - 1:
                            for p in range(PAIRS):
                                last = pe.matmul(bank(b, 1, P)[:, p, :], two(TiT2[b], p), two(X2[b], p),
                                                 start=True, stop=True)
                            last.then_inc(s_tmm[b], 1)
                        for p in range(PAIRS):
                            last = pe.matmul(bank(b, 2, P)[:, p, :], two(X2[b], p), two(TiT2[b], p),
                                             start=True, stop=True)
                        last.then_inc(s_tmm[b], 1)
                for b in range(2):
                    pe.wait_ge(s_tt[b], NL * i + NL)
                    pe.wait_ge(s_y, 2 * i + b + 2)
                    pe.wait_ge(s_s, 2 * i + b + 1)
                    for p in range(PAIRS):
                        pe.matmul(scan6[:, p, :], bd(b, p, 0), S[b][:, p, :], start=True, stop=False)
                        last = pe.matmul(scan6[:, p, :], two(aak[b], p), vtk[b][:, p, :], start=False, stop=True)
                    last.then_inc(s_scan, 1)
                    pe.wait_ge(s_ru, 4 * i + 2 * b + 1)
                    for p in range(PAIRS):
                        last = pe.matmul(scan6u[:, p, :], two(TiT2[b], p), R[:, p, :], start=True, stop=True)
                    last.then_inc(s_scan, 1)
                    pe.wait_ge(s_ru, 4 * i + 2 * b + 2)
                    for p in range(PAIRS):
                        pe.matmul(scan7[:, p, :], ktb[0][b][:, p, :], U[:, p, :], start=True, stop=False)
                        last = pe.matmul(scan7[:, p, :], ktb[1][b][:, p, :], vtk[b][:, p, :], start=False, stop=True)
                    last.then_inc(s_scan, 1)
                    for p in range(PAIRS):
                        pe.matmul(scan6[:, p, :], bd(b, p, 1), S[b][:, p, :], start=True, stop=False)
                        pe.matmul(scan6[:, p, :], two(arb[b], p), U[:, p, :], start=False, stop=False)
                        last = pe.matmul(scan6[:, p, :], two(ark[b], p), vtk[b][:, p, :], start=False, stop=True)
                    last.then_inc(s_scan, 1)

            pe.wait_ge(s_y, NCH + 2)
            pe.wait_ge(s_s, NCH + 1)
            pe.wait_ge(s_ycl, 16 * PAIRS)
            for h2 in range(2):
                for j in range(PAIRS):
                    last = pe.matmul(ps[:, 6 + h2, :], K("ones"), yconv[:, j, h2 * HALF:(h2 + 1) * HALF],
                                     start=(j == 0), stop=(j == PAIRS - 1))
            last.then_inc(s_lnm, 1)
            pe.wait_ge(s_lnc, PAIRS)
            for h2 in range(2):
                for j in range(PAIRS):
                    pe.wait_ge(s_lnsq, j + 1)
                    last = pe.matmul(ps[:, 6 + h2, :], K("ones"), squares[j][:, h2 * HALF:(h2 + 1) * HALF],
                                     start=(j == 0), stop=(j == PAIRS - 1))
            last.then_inc(s_lnq, 1)
            with pe.Fori(0, PAIRS) as p:
                pe.wait_ge(s_gp, p + 1)
                for h2 in range(2):
                    last = pe.matmul(ps[:, 2 + h2, :], bonesrk[:, :], hb[3][:, h2 * HALF:(h2 + 1) * HALF],
                                     start=True, stop=True)
                last.then_inc(s_gs, 1)
                pe.wait_ge(s_g2, 16 * p + 16)
                pe.wait_ge(s_glo, 3)
                for h2 in range(2):
                    last = pe.matmul(ps[:, 4 + h2, :], g2s[:, :], sg_lo[:, h2 * HALF:(h2 + 1) * HALF],
                                     start=True, stop=True)
                last.then_inc(s_gmm, 1)
                pe.wait_ge(s_gy, p + 1)
                for n in range(NCH):
                    last = pe.matmul(ps[:, n // 8, (n % 8) * C:(n % 8 + 1) * C],
                                     Ybd[:, n, :, :].rearrange("p a c -> p (a c)"), K("istack"), start=True, stop=True)
                last.then_inc(s_gt, 1)

            pe.sem_inc(s_omm, 2)
            pe.wait_ge(s_wout, 16)
            pe.wait_ge(s_go, PAIRS)
            pe.wait_ge(s_rw, 48)
            with pe.Fori(0, TT // 2) as i:
                for b in range(2):
                    n = 2 * i + b
                    pe.wait_ge(s_yts, n + 1)
                    pe.wait_ge(s_h, n + 1)
                    for h2 in range(2):
                        for k in range(KT):
                            last = pe.matmul(ps[:, 2 * b + h2, :], yTs[b][:, k, :], wout[:, k, h2 * HALF:(h2 + 1) * HALF],
                                             start=(k == 0), stop=(k == KT - 1))
                    last.then_inc(s_omm, 1)
                for b in range(2):
                    n = 2 * i + b
                    pe.wait_ge(s_u2, n + 1)
                    pe.wait_ge(s_u2T, n + 1)
                    for k in range(KT):
                        last = pe.transpose(ps[:, 4 + k // 4, (k % 4) * P:(k % 4 + 1) * P], u2s[b][:, k * P:(k + 1) * P],
                                            ident)
                    last.then_inc(s_t2, 1)
                    pe.wait_ge(s_u2T, n + 2)
                    pe.wait_ge(s_lg, n + 1)
                    for k in range(KT):
                        last = pe.matmul(ps[:, 6, 0:G + E], u2T[:, k, :], rw[:, k, :], start=(k == 0), stop=(k == KT - 1))
                    last.then_inc(s_lmm, 1)
            pe.wait_ge(s_rte, 3)
            pe.matmul(ps[:, 0, 0:TT * E], K("before"), flat(Os), start=True, stop=True)
            pe.matmul(ps[:, 1, 0:TT * E], K("ones"), flat(Os), start=True, stop=True).then_inc(s_cmm, 1)

            def turn_rows(n, b, q):
                pe.wait_ge(s_xb[b], 16 * q + 16)
                pe.wait_ge(s_xts, n + 1)
                for k in range(KT):
                    last = pe.transpose(ps[:, 4 + k // 4, (k % 4) * P:(k % 4 + 1) * P], xb[b][:, k * P:(k + 1) * P], ident)
                last.then_inc(s_xtm, 1)

            def gate_up(n, b, q):
                pe.wait_ge(s_xts, n + 2)
                pe.wait_ge(s_hid, n + 1)
                for o, (w, sw) in enumerate(((wg, s_wg), (wu, s_wu))):
                    pe.wait_ge(sw[b], 16 * q + 16)
                    for k in range(KT):
                        last = pe.matmul(ps[:, o, :], xTs[:, k, :], w[b][:, k, :], start=(k == 0), stop=(k == KT - 1))
                last.then_inc(s_gu, 1)

            def turn_hidden(n):
                pe.wait_ge(s_hid, n + 2)
                for k in range(FF // P):
                    last = pe.transpose(ps[:, 6, k * P:(k + 1) * P], hid[:, k * P:(k + 1) * P], ident)
                last.then_inc(s_htm, 1)

            def down(n, b, q):
                pe.wait_ge(s_hts, n + 1)
                pe.wait_ge(s_wd[b], 16 * q + 16)
                pe.wait_ge(s_ye, n + 1)
                for h2 in range(2):
                    for k in range(FF // P):
                        last = pe.matmul(ps[:, 2 + h2, :], hTs[:, k, :], wd[b][:, k, h2 * HALF:(h2 + 1) * HALF],
                                         start=(k == 0), stop=(k == FF // P - 1))
                last.then_inc(s_dn, 1)

            pe.wait_ge(s_ctl, 1)
            turn_rows(0, 0, 0)
            gate_up(0, 0, 0)
            with pe.Fori(0, E // 2 - 1) as i:
                for b in range(2):
                    n = 2 * i + b
                    turn_rows(n + 1, 1 - b, i + b)
                    turn_hidden(n)
                    gate_up(n + 1, 1 - b, i + b)
                    down(n, b, i)
            turn_rows(E - 1, 1, E // 2 - 1)
            turn_hidden(E - 2)
            gate_up(E - 1, 1, E // 2 - 1)
            down(E - 2, 0, E // 2 - 1)
            turn_hidden(E - 1)
            down(E - 1, 1, E // 2 - 1)
            novf = pe.value_load(ctl[0:1, OVF:OVF + 1], min_val=0, max_val=OVF)
            with pe.Fori(0, OVF) as m2:
                with pe.If(novf > m2):
                    turn_rows(m2 + E, 0, m2 + E // 2)
                    gate_up(m2 + E, 0, m2 + E // 2)
                    turn_hidden(m2 + E)
                    down(m2 + E, 0, m2 + E // 2)
                    pe.nop()
                with pe.Else():
                    pe.wait_ge(s_dn, m2 + E)
                    pe.sem_inc(s_dn, 1)

            pe.wait_ge(s_ye, E + OVF + 1)
            pe.wait_ge(s_pw, 48)
            def gate_tile(n, b, i):
                pe.wait_ge(s_ns, n + 1)
                pe.wait_ge(s_pT, n + 1)
                for k in range(KT):
                    last = pe.transpose(ps[:, k // 4, (k % 4) * P:(k % 4 + 1) * P], ns[b][:, k * P:(k + 1) * P], ident)
                last.then_inc(s_ntm, 1)
                pe.wait_ge(s_nT, n + 1)
                pe.wait_ge(s_pin[b], 16 * i + 16)
                for k in range(2):
                    last = pe.transpose(ps[:, 0, k * P:(k + 1) * P], pin[b][:, k * P:(k + 1) * P], ident)
                last.then_inc(s_ptm, 1)
                for h2 in range(2):
                    for k in range(KT):
                        last = pe.matmul(ps[:, 2 * b + 2 + h2, :], nT[:, k, :], plew[:, k, h2 * HALF:(h2 + 1) * HALF],
                                         start=(k == 0), stop=(k == KT - 1))
                last.then_inc(s_plm, 1)
                pe.wait_ge(s_pT, n + 2)
                pe.wait_ge(s_ob, n + 1)
                for h2 in range(2):
                    for k in range(2):
                        last = pe.matmul(ps[:, 6 + h2, :], pT[:, k, :], projw[:, k, h2 * HALF:(h2 + 1) * HALF],
                                         start=(k == 0), stop=(k == 1))
                last.then_inc(s_prm, 1)

            with pe.Fori(0, TT // 2) as i:
                for b in range(2):
                    gate_tile(2 * i + b, b, i)

        @block.scalar
        def _(act):
            act.sem_inc(s_z[2], 1)
            act.sem_inc(s_y, 2)
            act.wait_ge(s_const, 32)
            act.wait_ge(s_prep, 1)
            mine = Chain(act, s_act)
            with act.Fori(0, TT // 2) as i:
                mine.enter(i, 2)
                for b in range(2):
                    act.wait_ge(s_x[b], 16 * i + 16)
                    col = bass.ds(2 * i + b, 1)
                    mine.link(act.activation(b_e1[:, :], xin[b][:, 0:D], ACT.Square, accum_out=ssq[:, col]))
                    act.activation(std[:, col], ssq[:, col], ACT.Sqrt, scale=1.0 / D, bias=eps_rms[:, :]).then_inc(s_std, 1)

            mine.leave(TT // 2)

            def evac(s, n, out, func, rows=P, **kw):
                act.wait_ge(s_zmm[s], n + 1)
                act.activation(out, ps[0:rows, 2 * s:2 * s + 2, :].rearrange("p a c -> p (a c)"), func,
                               **kw).then_inc(s_z[s], 1)

            evac(0, 0, zr[0:64, 1:T + 1], ACT.Copy, 64)
            evac(1, 0, zk[0:96, 1:T + 1], ACT.Copy, 96)
            act.wait_ge(s_lora, 1)
            act.activation(lora[0:32, :], lora[0:32, :], ACT.Tanh).then_inc(s_lora, 1)
            act.wait_ge(s_glo, 1)
            act.activation(sg_lo[:, :], sg_lo[:, :], ACT.Tanh, scale=0.5).then_inc(s_glo, 1)
            low = ps[:, 6:8, :].rearrange("p a c -> p (a c)")
            with act.Fori(0, PAIRS) as j:
                act.wait_ge(s_dmm, j + 1)
                act.wait_ge(s_pair, j + 1)
                act.activation(b_ld[:, :], low, ACT.Tanh, scale=0.5, bias=w0h[:, bass.ds(j, 1)]).then_inc(s_dth, 1)
                evac(0, 2 * j + 1, zr[:, 1:T + 1], ACT.Copy)
                act.wait_ge(s_amm, j + 1)
                act.activation(b_a[:, :], low, ACT.Tanh, scale=0.5, bias=a0h[:, bass.ds(j, 1)]).then_inc(s_ath, 1)
                evac(1, 2 * j + 1, zk[:, 1:T + 1], ACT.Copy)
                evac(2, j + 1, zv[:, 1:T + 1], ACT.Copy)
                act.wait_ge(s_c, 2 * j + 1)
                act.activation(b_e1[:, :], b_c[:, :], ACT.Exp)
                act.wait_ge(s_c, 2 * j + 2)
                act.activation(b_ld[:, :], b_ld[:, :], ACT.Exp)
                act.activation(b_c[:, :], b_c[:, :], ACT.Exp, scale=-1.0).then_inc(s_exp, 1)
                act.wait_ge(s_kkr, j + 1)
                act.activation(b_sq[:, :], b_kk[:, :], ACT.Square).then_inc(s_sq, 1)
                evac(0, 2 * j + 2, zval[:, :], ACT.Copy)
                act.wait_ge(s_ssmm, j + 1)
                act.activation(nrm[:, :], ps[64:66, 6:8, :].rearrange("p a c -> p (a c)"), ACT.Sqrt).then_inc(s_nrm, 1)
                evac(1, 2 * j + 2, b_sq[:, :], ACT.Tanh, scale=0.5)


            def bank(b, q, w):
                return ps[:, 3 * b + q, 0:PAIRS * w]

            act.wait_ge(s_bdz, 2)
            with act.Fori(0, NCH // 2) as i:
                for b in range(2):
                    act.wait_ge(s_y, 2 * i + b + 1)
                    for hd in range(2):
                        rows = slice(64 * hd, 64 * hd + 64)
                        src = pk[rows, bass.ds(2 * i + b, 1), :, :, :].rearrange("p o a k c -> p (o a k) c")
                        last = act.activation(bdx[b][rows, :, hd, :], src, ACT.Copy)
                    last.then_inc(s_bdx[b], 1)
                for b in range(2):
                    act.wait_ge(s_turn[b], 3 * i + 1)
                    act.activation(flat(ktb[0][b]), bank(b, 2, P), ACT.Copy).then_inc(s_tok[b], 1)
                for b in range(2):
                    act.wait_ge(s_turn[b], 3 * i + 2)
                    act.activation(flat(ktb[1][b]), bank(b, 0, P), ACT.Copy).then_inc(s_tok[b], 1)
                    act.wait_ge(s_turn[b], 3 * i + 3)
                    act.activation(flat(vtk[b]), bank(b, 1, HD), ACT.Copy).then_inc(s_tok[b], 1)
                for lv in range(NL):
                    for b in range(2):
                        act.wait_ge(s_xmm[b], NL * i + lv + 1)
                        act.activation(flat2(X2[b]), bank(b, 0, P), ACT.Copy).then_inc(s_x2[b], 1)
                for b in range(2):
                    act.wait_ge(s_scan, 8 * i + 4 * b + 4)
                    act.activation(Yall[:, bass.ds(2 * i + b, 1), :, :].rearrange("p o a c -> p (o a c)"),
                                   ps[:, 6, 0:PAIRS * HD], ACT.Copy).then_inc(s_y, 1)

            for j in range(PAIRS):
                act.wait_ge(s_lnc, j + 1)
                act.activation(squares[j][:, :], yconv[:, j, :], ACT.Square).then_inc(s_lnsq, 1)
            act.wait_ge(s_lnq, 1)
            act.activation(hb[2][:, :], low, ACT.Sqrt, scale=1.0 / 512, bias=eps_ln[:, :]).then_inc(s_lns, 1)
            lin, tnh = (hb[3], hb[0]), (hb[4], hb[1])
            for j in range(PAIRS):
                act.wait_ge(s_lnn, j + 1)
                if j >= 2:
                    act.wait_ge(s_lny, j - 1)
                act.activation(lin[j % 2][:, :], yconv[:, j, :], ACT.Identity, scale=lngh[:, j:j + 1],
                               bias=lnbh[:, j:j + 1]).then_inc(s_lnt, 1)
                act.wait_ge(s_lnt, 2 * j + 1)
                act.activation(tnh[j % 2][:, :], lin[j % 2][:, :], ACT.Tanh).then_inc(s_lnt, 1)
            with act.Fori(0, PAIRS) as p:
                act.wait_ge(s_gc, p + 1)
                act.activation(hb[1][:, :], hb[0][:, :], ACT.Square).then_inc(s_gsq, 1)
                act.wait_ge(s_gv, p + 1)
                act.activation(gst[:, 2, :], gst[:, 1, :], ACT.Sqrt, scale=1.0 / HD, bias=eps_gn[:, :]).then_inc(s_gsd, 1)

            act.sem_inc(s_u2T, 1)
            act.wait_ge(s_go, PAIRS)
            act.wait_ge(s_lny, PAIRS)
            with act.Fori(0, TT // 2) as i:
                mine.enter(i, 2)
                for b in range(2):
                    n = 2 * i + b
                    act.wait_ge(s_omm, n + 1)
                    tok = bass.ds(256 * i + P * b, P)
                    act.activation(yTs[b][:, 0:PAIRS, :], yconv[:, :, tok], ACT.Copy)
                    act.activation(yTs[b][:, PAIRS:KT, :], yT[:, :, tok], ACT.Copy).then_inc(s_yts, 1)
                for b in range(2):
                    n = 2 * i + b
                    act.wait_ge(s_h, n + 3)
                    mine.link(act.activation(osq[:, :], h[:, bass.ds(n, 1), :].rearrange("p o d -> p (o d)"), ACT.Square,
                                             accum_out=ssq2[:, bass.ds(n, 1)]))
                    act.activation(std2[:, bass.ds(n, 1)], ssq2[:, bass.ds(n, 1)], ACT.Sqrt, scale=1.0 / D,
                                   bias=eps_rms[:, :]).then_inc(s_sd2, 1)
                for b in range(2):
                    act.wait_ge(s_t2, 2 * i + b + 1)
                    act.activation(flat(u2T), ps[:, 4:6, :].rearrange("p a c -> p (a c)"), ACT.Copy).then_inc(s_u2T, 1)
            mine.leave(TT // 2)
            act.wait_ge(s_rte, 1)
            act.activation(flat(gl2), flat(gl2), ACT.Exp).then_inc(s_rta, 1)
            act.wait_ge(s_rte, 2)
            act.activation(dm[:, :], dm[:, :], ACT.Exp).then_inc(s_rta, 1)

            act.sem_inc(s_xts, 1)
            act.sem_inc(s_ye, 1)
            for b in range(2):
                act.sem_inc(s_yst[b], 16)
            act.wait_ge(s_ctl, 1)

            def rows_turned(n):
                act.wait_ge(s_xtm, n + 1)
                act.activation(flat(xTs), ps[:, 4:6, :].rearrange("p a c -> p (a c)"), ACT.Copy).then_inc(s_xts, 1)

            def hidden_tanh(n):
                act.wait_ge(s_gu, n + 1)
                act.activation(th[:, :], ps[:, 0, :], ACT.Tanh, scale=0.5).then_inc(s_th, 1)

            def hidden_turned(n):
                act.wait_ge(s_htm, n + 1)
                act.activation(flat(hTs), ps[:, 6, :], ACT.Copy).then_inc(s_hts, 1)

            def rows_out(n, b, q):
                act.wait_ge(s_dn, n + 1)
                act.wait_ge(s_yst[b], 16 * q + 16)
                act.activation(ys[b][:, :], ps[:, 2:4, :].rearrange("p a c -> p (a c)"), ACT.Copy).then_inc(s_ye, 1)
                act.wait_ge(s_ye, n + 2)
                act.dma_start(t["ybuf"][bass.ds(n * BLK, BLK), :], ys[b][:, :]).then_inc(s_yst[b], 16)

            rows_turned(0)
            hidden_tanh(0)
            with act.Fori(0, E // 2 - 1) as i:
                for b in range(2):
                    n = 2 * i + b
                    rows_turned(n + 1)
                    hidden_turned(n)
                    hidden_tanh(n + 1)
                    rows_out(n, b, i)
            rows_turned(E - 1)
            hidden_turned(E - 2)
            hidden_tanh(E - 1)
            rows_out(E - 2, 0, E // 2 - 1)
            hidden_turned(E - 1)
            rows_out(E - 1, 1, E // 2 - 1)
            novf = act.value_load(ctl[0:1, OVF:OVF + 1], min_val=0, max_val=OVF)
            with act.Fori(0, OVF) as m2:
                with act.If(novf > m2):
                    rows_turned(m2 + E)
                    hidden_tanh(m2 + E)
                    hidden_turned(m2 + E)
                    rows_out(m2 + E, 0, m2 + E // 2)
                    act.nop()
                with act.Else():
                    act.sem_inc(s_ye, 1)
                    act.sem_inc(s_yst[0], 16)

            act.sem_inc(s_out[0], 16)
            act.sem_inc(s_out[1], 16)
            act.sem_inc(s_pT, 1)
            rows_of_out = t["out"].rearrange("(t p) d -> t p d", p=P)

            def moe_norm(n, b):
                col = bass.ds(n, 1)
                act.wait_ge(s_hs, 2 * n + 2)
                mine.link(act.activation(oq[b][:, :], hs[b][:, :], ACT.Square, accum_out=ssq[:, col]))
                act.activation(std[:, col], ssq[:, col], ACT.Sqrt, scale=1.0 / D, bias=eps_rms[:, :]).then_inc(s_sd3, 1)

            def embedding_turned(n):
                act.wait_ge(s_ptm, n + 1)
                act.activation(flat(pT), ps[:, 0, 0:PLE], ACT.Copy).then_inc(s_pT, 1)

            def gate_and_out(n, b):
                col = bass.ds(n, 1)
                act.wait_ge(s_plm, n + 1)
                act.activation(th2[b][:, :], ps[:, 2 * b + 2:2 * b + 4, :].rearrange("p a c -> p (a c)"), ACT.Tanh,
                               scale=0.5).then_inc(s_th3, 1)
                act.wait_ge(s_ob, n + 2)
                mine.link(act.activation(oq[b][:, :], ob[b][:, :], ACT.Square, accum_out=ssq2[:, col]))
                act.activation(std2[:, col], ssq2[:, col], ACT.Sqrt, scale=1.0 / D, bias=eps_rms[:, :]).then_inc(s_sd4, 1)
                act.wait_ge(s_of, n + 1)
                act.dma_start(rows_of_out[n], ob[b][:, :]).then_inc(s_out[b], 16)

            moe_norm(0, 0)
            with act.Fori(0, TT // 2 - 1) as i:
                mine.enter(i, 4)
                for b in range(2):
                    embedding_turned(2 * i + b)
                    moe_norm(2 * i + b + 1, 1 - b)
                    gate_and_out(2 * i + b, b)
            mine.leave(TT // 2 - 1)
            embedding_turned(TT - 2)
            moe_norm(TT - 1, 1)
            gate_and_out(TT - 2, 0)
            embedding_turned(TT - 1)
            gate_and_out(TT - 1, 1)

        @block.gpsimd
        def _(pool):
            pool.memset(glu[:, 0:TAPS - 1], 0.0).then_inc(s_pool, 1)
            pool.memset(reset[:, :], 1.0).then_inc(s_pool, 1)
            pool.wait_ge(s_pool, 2)
            pool.memset(reset[:, :].rearrange("p (n c) -> p n c", c=C)[:, :, 0:1], 0.0).then_inc(s_pool, 1)
            pool.wait_ge(s_pair, PAIRS + 1)
            pool.wait_ge(s_ycst, 16 * (PAIRS + 1))
            for b in range(2):
                pool.memset(bdx[b][:, :, :, :], 0.0).then_inc(s_bdz, 1)
            pool.memset(zero[:, :], 0.0).then_inc(s_zero, 1)
            pool.memset(S[0][:, :, :], 0.0).then_inc(s_s, 1)
            pool.wait_ge(s_bdz, 2)
            own = Chain(pool, s_pool)
            own.n = 3
            with pool.Fori(0, NCH // 2) as i:
                own.enter(i, 2)
                for b in range(2):
                    pool.wait_ge(s_msk[b], 3 * i + 1)
                    own.link(pool.tensor_tensor(TiT2[b], twice(LT[b][:, :, :]), over_pairs2(K("first2")), ALU.mult))
                    pool.tensor_tensor(TiT2[b], TiT2[b], over_pairs2(K("ident")), ALU.add).then_inc(s_ti0[b], 1)
                for lv in range(NL):
                    for b in range(2):
                        if lv >= 2:
                            pool.wait_ge(s_xmm[b], NL * i + lv - 1)
                        mask = cst[:, CCOL["levels2"] + lv * P:CCOL["levels2"] + (lv + 1) * P]
                        pool.tensor_tensor(Loff[b][lv % 2][:, :, :, :], twice(LT[b][:, :, :]), over_pairs2(mask),
                                           ALU.mult).then_inc(s_loff[b], 1)
            own.leave(NCH // 2)

            pool.sem_inc(s_u2c, 2)
            with pool.Fori(0, TT // 2) as i:
                for b in range(2):
                    pool.wait_ge(s_u2, 2 * i + b + 1)
                    pool.tensor_copy(u2[:, bass.ds(2 * i + b, 1), :].rearrange("p o d -> p (o d)"), u2s[b][:, :])\
                        .then_inc(s_u2c, 1)
            pool.wait_ge(s_slot, 2)
            pool.wait_ge(s_zf, 16 * ZEROS)
            pool.wait_ge(s_u2c, TT + 2)
            for n in range(TT):
                for k in range(2):
                    pool.indirect_dma_start(out=t["xbuf"][:, :], out_offset=bass.IndirectOffsetOnAxis(ap=slot[k][:, n:n + 1], axis=0),
                                            in_=u2[:, n, :], in_offset=None).then_inc(s_sc, 16)
            pool.wait_ge(s_yst[0], 16 * (E // 2 + OVF + 1))
            pool.wait_ge(s_yst[1], 16 * (E // 2 + 1))
            for n in range(TT):
                b = n % 2
                if n >= 2:
                    pool.wait_ge(s_hs, 2 * (n - 2) + 2)
                for k in range(2):
                    pool.indirect_dma_start(out=yg[b][k][:, :], out_offset=None, in_=t["ybuf"][:, :],
                                            in_offset=bass.IndirectOffsetOnAxis(ap=slot[k][:, n:n + 1], axis=0))\
                        .then_inc(s_yg[b], 16)

        @block.vector
        def _(dve):
            own = Chain(dve, s_dve)
            dve.sem_inc(s_uT, 2)
            dve.sem_inc(s_kk, 1)
            dve.sem_inc(s_pair, 1)
            dve.memset(eps_rms[:, :], 1e-6)
            dve.memset(eps_ln[:, :], 1e-5)
            dve.memset(eps_gn[:, :], 64e-5)
            dve.wait_ge(s_const, 32)
            for out, name, n in ((w0h, "w0", 4), (a0h, "a0", 4), (lngh, "lng", 4), (lnbh, "lnb", 4),
                                 (convwh, "convw", PAIRS * TAPS)):
                last = dve.tensor_scalar(out[:, :], V(name, 0, n), 0.5, None, ALU.mult)
            last.then_inc(s_prep, 1)
            with dve.Fori(0, TT // 2) as i:
                own.enter(i, 2)
                for b in range(2):
                    col = bass.ds(2 * i + b, 1)
                    dve.wait_ge(s_std, 2 * i + b + 1)
                    own.link(dve.reciprocal(rstd[:, col], std[:, col]))
                    dve.tensor_scalar(xn[b][:, 0:D], xin[b][:, 0:D], rstd[:, col], None, ALU.mult).then_inc(s_xn, 1)
                for b in range(2):
                    dve.wait_ge(s_xT, 2 * i + b + 1)
                    for q in range(2):
                        gain = V("mixg", 4 * q, 4).unsqueeze(2).to_broadcast([P, 4, P])
                        last = dve.tensor_tensor(uT[:, 4 * q:4 * q + 4, bass.ds(256 * i + P * b, P)],
                                                 ps[:, 2 * b + q, :].rearrange("p (k c) -> p k c", k=4), gain, ALU.mult)
                    last.then_inc(s_uT, 1)
            own.leave(TT // 2)
            for z in (zr, zk, zv):
                last = dve.memset(z[:, 0:1], 0.0)
            own.link(last)

            def shift(z, out, mu, rows=P):
                own.link(dve.tensor_tensor(out, z[0:rows, 0:T], z[0:rows, 1:T + 1], ALU.subtract))
                return dve.scalar_tensor_tensor(out=out, in0=out, scalar=mu, in1=z[0:rows, 1:T + 1],
                                                op0=ALU.mult, op1=ALU.add)

            dve.wait_ge(s_z[0], 1)
            shift(zr, lora[:, :], V("mu_wa", rows=64), 64).then_inc(s_lora, 1)
            dve.wait_ge(s_z[1], 1)
            shift(zk, sg_lo[:, :], V("mu_g", rows=96), 96).then_inc(s_glo, 1)
            dve.wait_ge(s_glo, 2)
            dve.tensor_scalar(sg_lo[:, :], sg_lo[:, :], 0.5, 0.5, ALU.mult, ALU.add).then_inc(s_glo, 1)

            dve.wait_ge(s_pool, 3)

            def chunked(x):
                return x.rearrange("p (n c) -> p n c", c=C)

            with dve.Fori(0, PAIRS) as j:
                own.enter(j, 43)

                def packed(kind):
                    return pk[:, :, bass.ds(j, 1), kind, :].rearrange("p n o c -> p n (o c)")

                dve.wait_ge(s_dth, j + 1)
                own.link(dve.tensor_scalar(b_ld[:, :], b_ld[:, :], -DECAY, -DECAY, ALU.mult, ALU.add))
                dve.tensor_tensor_scan(b_c[:, :], reset[:, :], b_ld[:, :], 0.0, ALU.mult, ALU.add).then_inc(s_c, 1)
                dve.wait_ge(s_c, 2 * j + 1)
                dve.tensor_tensor(b_ld[:, :], b_c[:, :], b_ld[:, :], ALU.subtract).then_inc(s_c, 1)
                dve.wait_ge(s_z[0], 2 * j + 2)
                own.link(shift(zr, b_rs[:, :], VD("mu_r", j)))
                dve.wait_ge(s_ath, j + 1)
                own.link(dve.tensor_scalar(b_a[:, :], b_a[:, :], 0.5, 0.5, ALU.mult, ALU.add))
                dve.wait_ge(s_z[1], 2 * j + 2)
                own.link(shift(zk, b_ks[:, :], VD("mu_k", j)))
                dve.tensor_scalar(b_kk[:, :], b_ks[:, :], VD("kk", j), None, ALU.mult).then_inc(s_kkr, 1)
                dve.wait_ge(s_z[2], j + 2)
                own.link(dve.tensor_tensor(b_t[:, :], zv[:, 0:T], zv[:, 1:T + 1], ALU.subtract))
                own.link(dve.scalar_tensor_tensor(out=packed(4), in0=chunked(b_t[:, :]), scalar=VD("mu_v", j),
                                                  in1=chunked(zv[:, 1:T + 1]), op0=ALU.mult, op1=ALU.add))
                own.link(dve.tensor_scalar(b_t[:, :], b_a[:, :], -1.0, VD("ka", j), ALU.add, ALU.mult))
                own.link(dve.scalar_tensor_tensor(out=b_t[:, :], in0=b_t[:, :], scalar=1.0, in1=b_ks[:, :],
                                                  op0=ALU.add, op1=ALU.mult))
                dve.wait_ge(s_exp, j + 1)
                dve.tensor_tensor(packed(1), chunked(b_rs[:, :]), chunked(b_e1[:, :]), ALU.mult)
                dve.tensor_tensor(packed(3), chunked(b_t[:, :]), chunked(b_c[:, :]), ALU.mult)
                dve.tensor_copy(PCH[:, :, bass.ds(j, 1)], chunked(b_e1[:, :])[:, :, C - 1:C])
                dve.wait_ge(s_nrm, j + 1)
                own.link(dve.tensor_scalar(nrm[:, :], nrm[:, :], 1e-12, None, ALU.max))
                dve.reciprocal(nrm[:, :], nrm[:, :]).then_inc(s_rn, 1)
                dve.wait_ge(s_bcmm, j + 1)
                dve.tensor_tensor(b_kk[:, :], b_kk[:, :], ps[:, 6:8, :].rearrange("p a c -> p (a c)"), ALU.mult)\
                    .then_inc(s_kk, 1)
                dve.wait_ge(s_kk, j + 2)
                own.link(dve.tensor_tensor(b_a[:, :], b_kk[:, :], b_a[:, :], ALU.mult))
                dve.tensor_tensor(packed(2), chunked(b_a[:, :]), chunked(b_c[:, :]), ALU.mult)
                dve.scalar_tensor_tensor(out=packed(0), in0=chunked(b_kk[:, :]), scalar=-1.0, in1=chunked(b_ld[:, :]),
                                         op0=ALU.mult, op1=ALU.mult).then_inc(s_pair, 1)
                dve.wait_ge(s_z[0], 2 * j + 3)
                dve.wait_ge(s_z[1], 2 * j + 3)
                own.link(dve.scalar_tensor_tensor(out=glu[:, TAPS - 1:TAPS - 1 + T], in0=b_sq[:, :], scalar=1.0,
                                                  in1=zval[:, :], op0=ALU.add, op1=ALU.mult))
                dve.wait_ge(s_ycst, 16 * j + 16)

                def tap(s):
                    return convwh[:, bass.ds(j * TAPS + s, 1)]

                own.link(dve.tensor_scalar(yc[:, :], glu[:, 0:T], tap(0), VD("convb", j), ALU.mult, ALU.add))
                for s in range(1, TAPS):
                    ins = dve.scalar_tensor_tensor(out=yc[:, :], in0=glu[:, s:s + T], scalar=tap(s), in1=yc[:, :],
                                                   op0=ALU.mult, op1=ALU.add)
                    if s < TAPS - 1:
                        own.link(ins)
                ins.then_inc(s_yc, 1)
            own.leave(PAIRS)

            dve.wait_ge(s_ycst, 16 * (PAIRS + 1))
            def bank(b, q, w):
                return ps[:, 3 * b + q, 0:PAIRS * w].rearrange("p (a w) -> p a w", a=PAIRS)

            with dve.Fori(0, NCH // 2) as i:
                own.enter(i, 2)
                for b in range(2):
                    dve.wait_ge(s_gram[b], 2 * i + 1)
                    g1, g2 = bank(b, 0, P), bank(b, 1, P)
                    dve.tensor_tensor(LT[b][:, :, :], g1[:, :, 0:C], over_pairs(K("strict")), ALU.mult)\
                        .then_inc(s_msk[b], 1)
                    dve.tensor_tensor(arb[b][:, :, :, :], twice(g1[:, :, C:P]), over_pairs2(K("incl2")), ALU.mult)\
                        .then_inc(s_msk[b], 1)
                    dve.wait_ge(s_gram[b], 2 * i + 2)
                    dve.tensor_tensor(aak[b][:, :, :, :], twice(g2[:, :, 0:C]), over_pairs2(K("strict2")), ALU.mult)
                    dve.tensor_tensor(ark[b][:, :, :, :], twice(g2[:, :, C:P]), over_pairs2(K("incl2")), ALU.mult)\
                        .then_inc(s_msk[b], 1)
                for b in range(2):
                    dve.wait_ge(s_tmm[b], 2 * NL * i + 1)
                    dve.tensor_copy(flat2(Ti2[b]), ps[:, 3 * b + 2, :]).then_inc(s_ti[b], 1)
                for lv in range(NL):
                    for b in range(2):
                        if lv < NL - 1:
                            dve.wait_ge(s_tmm[b], 2 * NL * i + 2 * lv + 2)
                            dve.tensor_tensor(flat2(Ti2[b]), flat2(Ti2[b]), ps[:, 3 * b + 1, :], ALU.add)\
                                .then_inc(s_ti[b], 1)
                        dve.wait_ge(s_tmm[b], 2 * NL * i + min(2 * lv + 3, 2 * NL))
                        dve.tensor_tensor(flat2(TiT2[b]), flat2(TiT2[b]), ps[:, 3 * b + 2, :], ALU.add)\
                            .then_inc(s_tt[b], 1)
                for b in range(2):
                    c = 2 * i + b
                    dve.wait_ge(s_scan, 4 * c + 1)
                    dve.tensor_copy(flat(R), ps[:, 6, 0:256]).then_inc(s_ru, 1)
                    dve.wait_ge(s_scan, 4 * c + 2)
                    dve.tensor_copy(flat(U), ps[:, 6, 256:512]).then_inc(s_ru, 1)
                    dve.wait_ge(s_scan, 4 * c + 3)
                    own.link(dve.tensor_tensor(flat(Stmp), ps[:, 7, 0:256], flat(S[b]), ALU.add))
                    decay = PCH[:, bass.ds(c, 1), :].rearrange("p o a -> p (o a)").unsqueeze(2)\
                        .to_broadcast([P, PAIRS, HD])
                    dve.tensor_tensor(S[1 - b][:, :, :], Stmp[:, :, :], decay, ALU.mult).then_inc(s_s, 1)
            own.leave(NCH // 2)

            dve.wait_ge(s_y, NCH + 2)
            dve.wait_ge(s_s, NCH + 1)
            dve.wait_ge(s_zf, 16 * ZEROS)
            own.link(dve.memset(Ybd[:, :, :, :], 0.0))
            low = ps[:, 6:8, :].rearrange("p a c -> p (a c)")
            dve.wait_ge(s_lnm, 1)
            for j in range(PAIRS):
                dve.scalar_tensor_tensor(out=yconv[:, j, :], in0=low, scalar=-1.0 / 512, in1=yconv[:, j, :],
                                         op0=ALU.mult, op1=ALU.add).then_inc(s_lnc, 1)
            dve.wait_ge(s_lns, 1)
            own.link(dve.reciprocal(hb[2][:, :], hb[2][:, :]))
            dve.wait_ge(s_lnc, PAIRS)
            dve.wait_ge(s_lnsq, PAIRS)
            for j in range(PAIRS):
                dve.tensor_tensor(yconv[:, j, :], yconv[:, j, :], hb[2][:, :], ALU.mult).then_inc(s_lnn, 1)
            lin, tnh = (hb[3], hb[0]), (hb[4], hb[1])
            for j in range(PAIRS):
                dve.wait_ge(s_lnt, 2 * j + 2)
                dve.scalar_tensor_tensor(out=yconv[:, j, :], in0=tnh[j % 2][:, :], scalar=1.0, in1=lin[j % 2][:, :],
                                         op0=ALU.add, op1=ALU.mult).then_inc(s_lny, 1)
            dve.wait_ge(s_lny, PAIRS)
            Yc, b1, b2 = hb[0], hb[2], hb[3]
            banks = lambda q: ps[:, q:q + 2, :].rearrange("p a c -> p (a c)")
            with dve.Fori(0, PAIRS) as p:
                own.enter(p, 6)
                yv = Yall[:, :, bass.ds(p, 1), :].rearrange("p n o c -> p n (o c)")
                one = lambda kind: pk[:, :, bass.ds(p, 1), kind, :].rearrange("p n o c -> p n (o c)")
                wide = lambda x: x.unsqueeze(2).to_broadcast([x.shape[0], NCH, HD])
                own.link(dve.tensor_reduce(gst[:, 0, :], yv, AX_X, ALU.add))
                own.link(dve.tensor_scalar(gst[:, 0, :], gst[:, 0, :], -1.0 / HD, None, ALU.mult))
                dve.tensor_tensor(chunked(Yc[:, :]), yv, wide(gst[:, 0, :]), ALU.add).then_inc(s_gc, 1)
                dve.tensor_scalar(bonesrk[:, :], K("bones"), VD("rk", p), None, ALU.mult)
                dve.tensor_tensor(chunked(b2[:, :]), one(1), one(3), ALU.mult).then_inc(s_gp, 1)
                dve.wait_ge(s_gsq, p + 1)
                dve.tensor_reduce(gst[:, 1, :], chunked(hb[1][:, :]), AX_X, ALU.add).then_inc(s_gv, 1)
                dve.wait_ge(s_gsd, p + 1)
                own.link(dve.reciprocal(gst[:, 3, :], gst[:, 2, :]))
                dve.wait_ge(s_gc, p + 1)
                for h2 in range(2):
                    rows = slice(64 * h2, 64 * h2 + 64)
                    last = dve.tensor_tensor(Ybd[rows, :, h2, :], chunked(Yc[rows, :]), wide(gst[rows, 3, :]), ALU.mult)
                last.then_inc(s_gy, 1)
                dve.wait_ge(s_gt, p + 1)
                own.link(dve.tensor_scalar(b1[:, :], banks(0), VD("gng", p), VD("gnb", p), ALU.mult, ALU.add))
                dve.wait_ge(s_gs, p + 1)
                own.link(dve.tensor_tensor(chunked(b2[:, :]), chunked(banks(2)), one(4), ALU.mult))
                own.link(dve.tensor_tensor(b1[:, :], b1[:, :], b2[:, :], ALU.add))
                dve.wait_ge(s_gmm, p + 1)
                dve.tensor_tensor(yT[:, bass.ds(p, 1), :].rearrange("p o d -> p (o d)"), b1[:, :], banks(4), ALU.mult)\
                    .then_inc(s_go, 1)
            own.leave(PAIRS)
            dve.sem_inc(s_h, 2)
            dve.sem_inc(s_lg, 1)


            dve.wait_ge(s_rw, 48)
            with dve.Fori(0, TT // 2) as i:
                own.enter(i, 2)
                for b in range(2):
                    n = 2 * i + b
                    dve.wait_ge(s_omm, n + 3)
                    dve.wait_ge(s_xo[b], 16 * i + 16)
                    dve.tensor_tensor(h[:, bass.ds(n, 1), :].rearrange("p o d -> p (o d)"), banks(2 * b), xo[b][:, :],
                                      ALU.add).then_inc(s_h, 1)
                for b in range(2):
                    n = 2 * i + b
                    dve.wait_ge(s_sd2, n + 1)
                    own.link(dve.reciprocal(rstd2[:, bass.ds(n, 1)], std2[:, bass.ds(n, 1)]))
                    dve.wait_ge(s_u2c, n + 1)
                    dve.scalar_tensor_tensor(out=u2s[b][:, :], in0=h[:, bass.ds(n, 1), :].rearrange("p o d -> p (o d)"),
                                             scalar=rstd2[:, bass.ds(n, 1)], in1=fgain[:, :],
                                             op0=ALU.mult, op1=ALU.mult).then_inc(s_u2, 1)
                for b in range(2):
                    n = 2 * i + b
                    dve.wait_ge(s_lmm, n + 1)
                    dve.tensor_tensor(lg[:, bass.ds(n, 1), :].rearrange("p o d -> p (o d)"), ps[:, 6, 0:G + E], rbias[:, :],
                                      ALU.add).then_inc(s_lg, 1)
            own.leave(TT // 2)
            dve.wait_ge(s_lg, TT + 1)

            def bc(x, n):
                return x.unsqueeze(2).to_broadcast([P, TT, n])

            def first_max(x, n, top, work, onehot, prefer):
                own.link(dve.tensor_reduce(top[:, :], x, AX_X, ALU.max))
                own.link(dve.tensor_tensor(work[:, :, :], x, bc(top, n), ALU.is_equal))
                own.link(dve.tensor_tensor(work[:, :, :], work[:, :, :], prefer.unsqueeze(1).to_broadcast([P, TT, n]),
                                           ALU.mult))
                own.link(dve.tensor_reduce(gtop[:, :], work[:, :, :], AX_X, ALU.max))
                own.link(dve.tensor_tensor(onehot[:, :, :], work[:, :, :], bc(gtop, n), ALU.is_equal))

            gl = lg[:, :, 0:G]
            el = lg[:, :, G:G + E].rearrange("p t (g e) -> p t g e", g=G)
            first_max(gl, G, gmax, gl1, og, K("prefer4"))
            dve.tensor_tensor(gl2[:, :, :], gl, bc(gmax, G), ALU.subtract).then_inc(s_rte, 1)
            four = lambda x: x.rearrange("p t (g e) -> p t g e", g=G)
            by_group = og.unsqueeze(3).to_broadcast([P, TT, G, EPG])
            by_expert = lambda x: x.unsqueeze(2).to_broadcast([P, TT, G, EPG])
            own.link(dve.tensor_tensor(four(r_a), el, by_group, ALU.mult))
            own.link(dve.tensor_reduce(esel[:, :, :], r_a.rearrange("p t (g e) -> p t e g", g=G), AX_X, ALU.add))
            first_max(esel, EPG, m1, ew, o1, K("prefer8"))
            own.link(dve.scalar_tensor_tensor(out=flat(e2nd), in0=flat(o1), scalar=-1e30, in1=flat(esel),
                                              op0=ALU.mult, op1=ALU.add))
            first_max(e2nd, EPG, m2, ew, o2, K("prefer8"))
            dve.tensor_tensor(dm[:, :], m2[:, :], m1[:, :], ALU.subtract).then_inc(s_rte, 1)
            dve.tensor_tensor(four(O1), by_group, by_expert(o1), ALU.mult)
            own.link(dve.tensor_tensor(four(O2), by_group, by_expert(o2), ALU.mult))
            dve.tensor_tensor(flat(Os), flat(O1), flat(O2), ALU.add).then_inc(s_rte, 1)
            dve.wait_ge(s_rta, 2)
            own.link(dve.tensor_reduce(gsum[:, :], gl2[:, :, :], AX_X, ALU.add))
            own.link(dve.reciprocal(gp[:, :], gsum[:, :]))
            own.link(dve.tensor_scalar(m1[:, :], dm[:, :], 1.0, None, ALU.add))
            own.link(dve.reciprocal(m2[:, :], m1[:, :]))
            own.link(dve.tensor_tensor(gate[0][:, :], m2[:, :], gp[:, :], ALU.mult))
            own.link(dve.tensor_tensor(gate[1][:, :], gate[0][:, :], dm[:, :], ALU.mult))
            dve.wait_ge(s_cmm, 1)
            own.link(dve.memset(tbase[:, 0, :], 0.0))
            own.link(dve.tensor_copy(flat(r_b), ps[:, 1, 0:TT * E]))
            for n in range(1, TT):
                own.link(dve.tensor_tensor(tbase[:, n, :], tbase[:, n - 1, :], r_b[:, n - 1, :], ALU.add))
            own.link(dve.tensor_tensor(cnt[:, :], tbase[:, TT - 1, :], r_b[:, TT - 1, :], ALU.add))
            own.link(dve.tensor_tensor(flat(rank), ps[:, 0, 0:TT * E], flat(tbase), ALU.add))
            own.link(dve.tensor_scalar(nb[:, :], cnt[:, :], float(BLK), None, ALU.is_gt))
            for q in range(2, T // BLK):
                own.link(dve.scalar_tensor_tensor(out=nb[:, :], in0=cnt[:, :], scalar=float(q * BLK), in1=nb[:, :],
                                                  op0=ALU.is_gt, op1=ALU.add))
            own.link(dve.tensor_tensor_scan(incl[:, :], K("ones", E), nb[:, :], 0.0, ALU.mult, ALU.add))
            own.link(dve.tensor_tensor(excl[:, :], incl[:, :], nb[:, :], ALU.subtract))
            own.link(dve.tensor_scalar(excl[:, :], excl[:, :], float(BLK), float((E - 1) * BLK), ALU.mult, ALU.add))
            own.link(dve.tensor_tensor(excl[:, :], excl[:, :], K("ebase"), ALU.subtract))
            over_tiles = lambda x: x.unsqueeze(1).to_broadcast([P, TT, E])
            own.link(dve.tensor_scalar(flat(r_a), flat(rank), float(BLK), None, ALU.is_ge))
            own.link(dve.tensor_tensor(r_a[:, :, :], r_a[:, :, :], over_tiles(excl), ALU.mult))
            own.link(dve.tensor_tensor(r_b[:, :, :], rank[:, :, :], over_tiles(K("ebase")), ALU.add))
            own.link(dve.tensor_tensor(flat(slotm), flat(r_a), flat(r_b), ALU.add))
            for k, O in enumerate((O1, O2)):
                own.link(dve.tensor_tensor(flat(r_a), flat(slotm), flat(O), ALU.mult))
                own.link(dve.tensor_reduce(gsum[:, :], r_a[:, :, :], AX_X, ALU.add))
                dve.tensor_copy(slot[k][:, :], gsum[:, :]).then_inc(s_slot, 1)
                dve.wait_ge(s_slot, k + 1)
            own.link(dve.tensor_tensor(ovc[0:1, :, :], incl[0:1, :].unsqueeze(1).to_broadcast([1, OVF, E]),
                                       cst[0:1, CCOL["iotam"]:CCOL["iotam"] + OVF].unsqueeze(2).to_broadcast([1, OVF, E]),
                                       ALU.is_le))
            own.link(dve.tensor_reduce(ov[0:1, 0:OVF], ovc[0:1, :, :], AX_X, ALU.add))
            own.link(dve.tensor_scalar(ov[0:1, 0:OVF], ov[0:1, 0:OVF], float(E - 1), None, ALU.min))
            own.link(dve.tensor_copy(ov[0:1, OVF:OVF + 1], incl[0:1, E - 1:E]))
            dve.tensor_copy(ctl[:, :], ov[0:1, :]).then_inc(s_ctl, 1)

            dve.sem_inc(s_hid, 1)
            dve.wait_ge(s_ctl, 1)
            novf = dve.value_load(ctl[0:1, OVF:OVF + 1], min_val=0, max_val=OVF)

            def hidden(n):
                dve.wait_ge(s_th, n + 1)
                own.link(dve.scalar_tensor_tensor(out=th[:, :], in0=th[:, :], scalar=1.0, in1=ps[:, 0, :],
                                                  op0=ALU.add, op1=ALU.mult))
                dve.scalar_tensor_tensor(out=hid[:, :], in0=th[:, :], scalar=0.5, in1=ps[:, 1, :],
                                         op0=ALU.mult, op1=ALU.mult).then_inc(s_hid, 1)

            with dve.Fori(0, E) as e:
                own.enter(e, 1)
                hidden(e)
            own.leave(E)
            with dve.Fori(0, OVF) as m2_:
                with dve.If(novf > m2_):
                    own.enter(m2_, 1)
                    hidden(m2_ + E)
                    dve.nop()
                with dve.Else():
                    dve.sem_inc(s_dve, 1)
            own.leave(OVF)

            dve.sem_inc(s_ob, 1)
            dve.wait_ge(s_ye, E + OVF + 1)
            dve.wait_ge(s_pw, 48)
            def add_experts(n, b, i):
                col = bass.ds(n, 1)
                dve.wait_ge(s_yg[b], 32 * i + 32)
                dve.scalar_tensor_tensor(out=hs[b][:, :], in0=yg[b][0][:, :], scalar=gate[0][:, col],
                                         in1=h[:, col, :].rearrange("p o d -> p (o d)"), op0=ALU.mult,
                                         op1=ALU.add).then_inc(s_hs, 1)
                dve.wait_ge(s_hs, 2 * n + 1)
                dve.scalar_tensor_tensor(out=hs[b][:, :], in0=yg[b][1][:, :], scalar=gate[1][:, col],
                                         in1=hs[b][:, :], op0=ALU.mult, op1=ALU.add).then_inc(s_hs, 1)
                dve.wait_ge(s_sd3, n + 1)
                own.link(dve.reciprocal(rstd[:, col], std[:, col]))
                dve.tensor_scalar(ns[b][:, :], hs[b][:, :], rstd[:, col], None, ALU.mult).then_inc(s_ns, 1)

            def turned(n):
                dve.wait_ge(s_ntm, n + 1)
                for q in range(2):
                    last = dve.tensor_tensor(nT[:, 4 * q:4 * q + 4, :], ps[:, q, :].rearrange("p (k c) -> p k c", k=4),
                                             V("pleg", 4 * q, 4).unsqueeze(2).to_broadcast([P, 4, P]), ALU.mult)
                last.then_inc(s_nT, 1)

            def finish(n, b, i):
                col = bass.ds(n, 1)
                dve.wait_ge(s_th3, n + 1)
                dve.wait_ge(s_prm, n + 1)
                own.link(dve.scalar_tensor_tensor(out=th2[b][:, :], in0=th2[b][:, :], scalar=1.0, in1=banks(6),
                                                  op0=ALU.add, op1=ALU.mult))
                dve.wait_ge(s_out[b], 16 * i + 16)
                dve.scalar_tensor_tensor(out=ob[b][:, :], in0=th2[b][:, :], scalar=0.5, in1=hs[b][:, :],
                                         op0=ALU.mult, op1=ALU.add).then_inc(s_ob, 1)
                dve.wait_ge(s_sd4, n + 1)
                own.link(dve.reciprocal(rstd2[:, col], std2[:, col]))
                dve.scalar_tensor_tensor(out=ob[b][:, :], in0=ob[b][:, :], scalar=rstd2[:, col], in1=lastg[:, :],
                                         op0=ALU.mult, op1=ALU.mult).then_inc(s_of, 1)

            add_experts(0, 0, 0)
            turned(0)
            with dve.Fori(0, TT // 2 - 1) as i:
                own.enter(i, 6)
                for b in range(2):
                    add_experts(2 * i + b + 1, 1 - b, i + b)
                    turned(2 * i + b + 1)
                    finish(2 * i + b, b, i)
            own.leave(TT // 2 - 1)
            add_experts(TT - 1, 1, TT // 2 - 1)
            turned(TT - 1)
            finish(TT - 2, 0, TT // 2 - 1)
            finish(TT - 1, 1, TT // 2 - 1)


def kernel(**inputs):
    import concourse.bacc as bacc
    from concourse.bass_utils import run_bass_kernel_spmd as run

    a = {k: np.ascontiguousarray(v) for k, v in inputs.items()}
    f = lambda x: np.ascontiguousarray(x)

    def cols(x):
        return x.reshape(-1, P).T

    def padded(x):
        out = np.zeros((P, x.shape[1]), x.dtype)
        out[:x.shape[0]] = x
        return out

    mu = a["rwkv_mu"][0]
    convw = a["conv_w"][0].reshape(TAPS, PAIRS, P).transpose(2, 1, 0).reshape(P, PAIRS * TAPS)
    parts = {"mixg": cols(a["mix_norm"][0]), "mu_r": cols(mu[0:512]), "mu_k": cols(mu[512:1024]),
             "mu_v": cols(mu[1024:1536]), "w0": cols(a["rwkv_w0"][0]), "a0": cols(a["rwkv_a0"][0]),
             "kk": cols(a["rwkv_kk"][0]), "ka": cols(a["rwkv_ka"][0]), "rk": cols(a["rwkv_rk"][0].reshape(-1)),
             "gng": cols(a["rwkv_gn_g"][0]), "gnb": cols(a["rwkv_gn_b"][0]), "convb": cols(a["conv_b"][0]),
             "lng": cols(a["conv_ln_g"][0]), "lnb": cols(a["conv_ln_b"][0]), "convw": convw,
             "mu_wa": padded(mu[1536:1600, None]), "mu_g": padded(mu[1600:1696, None]),
             "pleg": cols(a["ple_norm"][0])}
    vec = f(np.concatenate([parts[n] for n, _ in _cols], axis=1))

    def coltile(w):
        return w.reshape(KT, P, -1).transpose(1, 0, 2).reshape(P, -1)

    w_in = a["w_in"][0]
    z0 = D
    w_conv = f(np.stack([coltile(w_in[:, g * 512 + P * j:g * 512 + P * j + P]) for j in range(4) for g in range(2)]))
    w_rkv = f(np.stack([coltile(w_in[:, z0 + g * 512 + P * j:z0 + g * 512 + P * j + P])
                        for j in range(4) for g in range(3)]))
    arrays = {
        "x": a["x"][0], "cst": constants(), "vec": vec, "w_conv": w_conv, "w_rkv": w_rkv,
        "w_wa": f(coltile(w_in[:, z0 + 1536:z0 + 1600])), "w_g": f(coltile(w_in[:, z0 + 1600:z0 + 1696])),
        "wa2": f(np.concatenate([a["rwkv_w2"][0], a["rwkv_a2"][0]], axis=0).reshape(64, 4, P).transpose(1, 0, 2)),
    }
    arrays |= {
        "g2": f(a["rwkv_g2"][0].reshape(96, 4, P).transpose(1, 0, 2)), "w_out": a["w_out"][0],
        "rw": f(np.concatenate([a["router_group_w"][0], a["router_expert_w"][0].transpose(1, 0, 2).reshape(D, E)], axis=1)),
        "rb": f(np.concatenate([a["router_group_b"][0], a["router_expert_b"][0].reshape(E)])),
        "ffg": a["ffn_norm"][0], "wg": a["expert_w_gate"][0], "wu": a["expert_w_up"][0], "wd": a["expert_w_down"][0],
        "plew": a["ple_gate_w"][0], "projw": a["ple_proj_w"][0], "lastg": a["final_norm"], "p": a["p"][0, 0],
    }
    nc = bacc.Bacc("TRN2", target_bir_lowering=False, num_devices=1)
    t = {k: nc.dram_tensor("in_" + k, v.shape, mybir.dt.from_np(v.dtype), kind="ExternalInput").ap() for k, v in arrays.items()}
    t["out"] = nc.dram_tensor("out", (T, D), F32, kind="ExternalOutput").ap()
    t["yconv"] = nc.dram_tensor("dr_yconv", (PAIRS, P, T), F32, kind="Internal").ap()
    t["xbuf"] = nc.dram_tensor("dr_xbuf", (NBLK * BLK, D), F32, kind="Internal").ap()
    t["ybuf"] = nc.dram_tensor("dr_ybuf", (NBLK * BLK, D), F32, kind="Internal").ap()
    program(nc, t)
    r = run(nc, [{"in_" + k: v for k, v in arrays.items()}], core_ids=[0])
    return r.results[0]["out"].reshape(1, T, D)
```

```python
from contextlib import ExitStack

import numpy as np
import concourse.bass as bass
from concourse import mybir

F32 = mybir.dt.float32
BF16 = mybir.dt.bfloat16
I32 = mybir.dt.int32
U32 = mybir.dt.uint32
ALU = mybir.AluOpType
ACT = mybir.ActivationFunctionType
AX_X = mybir.AxisListType.X

P = 128
T = 1024
D = 1024
KT = D // P
TT = T // P
HALF = 512
PAIRS = 4
HD = 64
C = 64
NCH = T // C
TAPS = 31
G = 4
EPG = 8
E = G * EPG
FF = 512
BLK = 128
ARENA = 192
OVF = 15
OVF2 = (OVF + 1) // 2
NBLK = E + 2 * OVF2
ZEROS = NBLK + 2 * OVF2
PLE = 256
DECAY = float(np.exp(-0.5)) / 2.0
LEVELS = (2, 4, 8, 16, 32)

_cols = [("mixg", KT), ("mu_r", 4), ("mu_k", 4), ("mu_v", 4), ("w0", 4), ("a0", 4), ("kk", 4), ("ka", 4),
         ("rk", 4), ("gng", 4), ("gnb", 4), ("convb", 4), ("lng", 4), ("lnb", 4), ("convw", 4 * TAPS),
         ("mu_wa", 1), ("mu_g", 1), ("pleg", KT)]
VCOL, _n = {}, 0
for _name, _w in _cols:
    VCOL[_name] = _n
    _n += _w
VEC = _n

_ccols = [("ident", 128), ("istack", 64), ("before", 128), ("ones", 128), ("bones", 128), ("sel2", 2),
          ("selT2", 128), ("strict", 64), ("strict2", 128), ("incl2", 128), ("first2", 128),
          ("levels2", 5 * 128), ("ebase", E), ("prefer4", 4), ("prefer8", 8), ("iotam", OVF)]
CCOL, _n = {}, 0
for _name, _w in _ccols:
    CCOL[_name] = _n
    _n += _w
CST = _n


def constants():
    c = np.zeros((P, CST), np.float32)

    def put(name, a):
        a = np.asarray(a, np.float32)
        c[:a.shape[0], CCOL[name]:CCOL[name] + a.shape[1]] = a

    j = np.arange(P)[:, None] % C
    hj = np.arange(P)[:, None] // C
    t = np.arange(C)[None, :]
    both = lambda m: np.concatenate([m * (hj == 0), m * (hj == 1)], axis=1)
    put("ident", np.eye(P))
    put("istack", j == t)
    put("before", np.arange(P)[:, None] < np.arange(P)[None, :])
    put("ones", np.ones((P, P)))
    put("bones", hj == np.arange(P)[None, :] // C)
    put("sel2", hj == np.arange(2)[None, :])
    c[64:66, CCOL["selT2"]:CCOL["selT2"] + P] = np.arange(2)[:, None] == np.arange(P)[None, :] // C
    put("strict", j < t)
    put("strict2", both(j < t))
    put("incl2", both(j <= t))
    put("first2", both((j // 2 == t // 2) & (j < t)))
    put("levels2", np.concatenate([both((j // (2 * s) == t // (2 * s)) & (j % (2 * s) < s) & (t % (2 * s) >= s))
                                   for s in LEVELS], axis=1))
    put("ebase", np.broadcast_to(BLK * np.arange(E)[None, :], (P, E)))
    put("prefer4", np.broadcast_to(8.0 - np.arange(4)[None, :], (P, 4)))
    put("prefer8", np.broadcast_to(8.0 - np.arange(8)[None, :], (P, 8)))
    put("iotam", np.broadcast_to(np.arange(OVF)[None, :], (P, OVF)))
    return c


class Chain:

    def __init__(self, eng, sem):
        self.eng, self.sem, self.base, self.n = eng, sem, 0, 0

    def link(self, ins, back=0):
        self.n += 1
        ins.then_inc(self.sem, 1)
        self.eng.wait_ge(self.sem, self.base + self.n - back)

    def enter(self, i, per):
        self.outer, self.per = self.base + self.n, per
        self.base, self.n = self.outer + i * per, 0

    def leave(self, count):
        assert self.n == self.per, (self.n, self.per)
        self.base, self.n = self.outer + count * self.per, 0


def program(nc, t):
    with ExitStack() as ctx:
        def sb(name, shape, dt=F32, where=ctx):
            return where.enter_context(nc.sbuf_tensor(name, shape, dt))

        def sem(name):
            return ctx.enter_context(nc.semaphore(name))

        ps = ctx.enter_context(nc.psum_tensor("ps", [P, 8, HALF], F32))

        vec = sb("vec", [P, VEC])
        cst = sb("cst", [P, CST])
        sg_lo = sb("sg_lo", [96, T])

        omu = sb("omu", [P, 3 * PAIRS])
        ndecay = sb("ndecay", [P, 1])
        half = sb("half", [P, 1])
        eps_rms = sb("eps_rms", [P, 1])
        eps_ln = sb("eps_ln", [P, 1])
        eps_gn = sb("eps_gn", [P, 1])
        w0h = sb("w0h", [P, PAIRS])
        a0h = sb("a0h", [P, PAIRS])
        lngh = sb("lngh", [P, PAIRS])
        lnbh = sb("lnbh", [P, PAIRS])
        convwh = sb("convwh", [P, PAIRS * TAPS])

        reset = sb("reset", [P, T], BF16)
        ssq, std, rstd, ssq2, std2, rstd2 = (sb(f"stat{q}", [P, TT]) for q in range(6))
        gate = [sb(f"gate{q}", [P, TT]) for q in range(2)]
        slot = [sb(f"slot{q}", [P, TT], U32) for q in range(2)]
        ctl = sb("ctl", [1, OVF + 1], I32)
        PCH = sb("PCH", [P, NCH, PAIRS])

        def V(name, i=0, n=1, rows=P):
            return vec[0:rows, VCOL[name] + i:VCOL[name] + i + n]

        def VD(name, i):
            return vec[:, bass.ds(i + VCOL[name], 1)]

        def flat(x):
            return x[:, :, :].rearrange("p a c -> p (a c)")

        def flat2(x):
            return x.rearrange("p a b c -> p (a b c)")

        def twice(x):
            return x.unsqueeze(2).to_broadcast([P, PAIRS, 2, C])

        def over_pairs(m):
            return m.unsqueeze(1).to_broadcast([P, PAIRS, C])

        def over_pairs2(m):
            return m.rearrange("p (a c) -> p a c", a=2).unsqueeze(1).to_broadcast([P, PAIRS, 2, C])

        def K(name, n=None, rows=P):
            w = dict(_ccols)[name]
            return cst[0:rows, CCOL[name]:CCOL[name] + (n or w)]

        arena = sb("arena", [P, ARENA * 256])

        class Region:

            def __init__(self, kib):
                self.at = int(kib * 256)

            def take(self, *shape, rows=P):
                n = int(np.prod(shape))
                x = arena[0:rows, self.at:self.at + n]
                self.at += n
                assert self.at <= ARENA * 256
                if len(shape) == 1:
                    return x
                names = "abcde"[:len(shape)]
                return x.rearrange(f"p ({' '.join(names)}) -> p {' '.join(names)}",
                                   **{q: w for q, w in zip(names[1:], shape[1:])})

        m = Region(0)
        pk = m.take(NCH, PAIRS, 5, C)

        m = Region(80)
        uT = m.take(KT, T)
        wz = [m.take(KT * P) for s in range(3)]
        wa2 = m.take(P, rows=2 * 32)
        zr, zk, zv = (m.take(T + 1) for _ in range(3))
        zval = m.take(T)
        b_ld = m.take(T)
        b_e1 = m.take(T)
        b_c = m.take(T)
        b_a = m.take(T)
        b_rs = m.take(T)
        b_ks = m.take(T)
        b_t = m.take(T)
        b_kk = m.take(T)
        b_sq = m.take(T)
        lora_nrm = m.take(T)
        lora = lora_nrm[0:64, :]
        nrm = lora_nrm[64:66, :]
        wl = lora
        glu = m.take(TAPS - 1 + T)
        yc = m.take(T)
        xin = [zr, zk]
        xn = [zv, zval]

        Yall = pk[:, :, :, 0, :]
        m = Region(80)
        four = lambda *shape: [[m.take(*shape) for b in range(2)] for u in range(2)]
        bdar = four(PAIRS * 2, 2, C)
        bdbkv = [m.take(PAIRS * 3, 2, C) for b in range(2)]
        btk, ktk = four(PAIRS, P), four(PAIRS, P)
        vtk = four(PAIRS, HD)
        aak, arb, ark = four(PAIRS, 2, C), four(PAIRS, 2, C), four(PAIRS, 2, C)
        TiT2 = four(PAIRS, 2, C)
        LT = [m.take(PAIRS, C) for b in range(2)]
        Loff = [[m.take(PAIRS, 2, C) for q in range(2)] for b in range(2)]
        Ti, Xc = ([m.take(PAIRS, C) for b in range(2)] for _ in range(2))
        X2 = [m.take(PAIRS, 2, C) for b in range(2)]
        R, U, S0, S1, Stmp = (m.take(PAIRS, HD) for _ in range(5))
        S = [S0, S1]
        zero = m.take(D)

        m = Region(96)
        yconv = m.take(PAIRS, T)
        yT = m.take(PAIRS, T)
        wout = m.take(KT, D)
        Yc, ysq, bonus = ([m.take(T) for q in range(2)] for _ in range(3))
        b1 = m.take(T)
        g2s = m.take(PAIRS * P, rows=96)
        bonesrk = [m.take(P) for q in range(2)]
        gst = m.take(2, 4, NCH)
        m = Region(80)
        Ybd = [m.take(NCH, 2, C) for q in range(2)]
        m = Region(128)
        squares = [m.take(T) for j in range(PAIRS)]
        lnstd = m.take(T)

        m = Region(0)
        h = m.take(TT, D)
        u2 = m.take(TT, D)
        yTs = [m.take(KT, P) for b in range(2)]
        xo = [m.take(D) for b in range(2)]
        u2s = [m.take(D) for b in range(2)]
        u2T = m.take(KT, P)
        fgain = m.take(D)
        m = Region(160)
        rw = m.take(KT, G + E)
        rbias = m.take(G + E)
        osq = m.take(D)
        lg = m.take(TT, G + E)
        r_a = m.take(TT, E)
        r_b = m.take(TT, E)
        O1, O2, Os, slotm, rank, tbase = (m.take(TT, E) for _ in range(6))
        og, gl1, gl2 = (m.take(TT, G) for _ in range(3))
        esel, e2nd, o1, o2, ew = (m.take(TT, EPG) for _ in range(5))
        gmax, gtop, gsum, gp, m1, m2, etop, dm = (m.take(TT) for _ in range(8))
        cnt, nb, incl, excl = (m.take(E) for _ in range(4))
        ovc = m.take(OVF, E)
        ov = m.take(OVF + 1)

        m = Region(32)
        xb = [m.take(D) for b in range(2)]
        xTs = m.take(KT, P)
        th = m.take(FF)
        hid = m.take(FF)
        hTs = m.take(FF // P, P)
        ys = [m.take(D) for b in range(2)]
        m = Region(96)
        wd1, wd0 = m.take(FF // P, D), m.take(FF // P, D)
        wg0, wu0 = m.take(KT, FF), m.take(KT, FF)
        wg1, wu1 = m.take(KT, FF), m.take(KT, FF)
        wg, wu, wd = (wg0, wg1), (wu0, wu1), (wd0, wd1)

        m = Region(64)
        plew = m.take(KT, D)
        m = Region(96)
        projw = m.take(PLE // P, D)
        yg = [[m.take(D) for k in range(2)] for b in range(2)]
        hs, ns, ob, oq, th2 = ([m.take(D) for b in range(2)] for _ in range(5))
        nT = m.take(KT, P)
        pin = [m.take(PLE) for b in range(2)]
        pT = m.take(PLE // P, P)
        lastg = m.take(D)

        s_const = sem("s_const")
        s_x = [sem(f"s_x{b}") for b in range(2)]
        s_std = sem("s_std"); s_xn = sem("s_xn"); s_xT = sem("s_xT"); s_uT = sem("s_uT")
        s_w = [sem(f"s_w{s}") for s in range(3)]
        s_zmm = [sem(f"s_zmm{s}") for s in range(3)]
        s_z = [sem(f"s_z{s}") for s in range(3)]
        s_wa2 = sem("s_wa2"); s_lora = sem("s_lora"); s_glo = sem("s_glo")
        s_dmm = sem("s_dmm"); s_dth = sem("s_dth"); s_amm = sem("s_amm"); s_ath = sem("s_ath")
        s_c = sem("s_c")
        s_exp = sem("s_exp"); s_kkr = sem("s_kkr"); s_sq = sem("s_sq")
        s_ssmm = sem("s_ssmm"); s_nrm = sem("s_nrm"); s_rn = sem("s_rn"); s_bcmm = sem("s_bcmm"); s_kk = sem("s_kk")
        s_pair = sem("s_pair"); s_yc = sem("s_yc"); s_ycst = sem("s_ycst"); s_prep = sem("s_prep")
        s_dve = sem("s_dve"); s_act = sem("s_act"); s_pool = sem("s_pool")
        s_bdz = sem("s_bdz")
        s_bdx = [sem(f"s_bdx{b}") for b in range(2)]
        s_gram = [sem(f"s_gram{b}") for b in range(2)]
        s_turn = [sem(f"s_turn{b}") for b in range(2)]
        s_msk = [sem(f"s_msk{b}") for b in range(2)]
        s_tok = [sem(f"s_tok{b}") for b in range(2)]
        s_loff = [sem(f"s_loff{b}") for b in range(2)]
        s_xc = [sem(f"s_xc{b}") for b in range(2)]
        s_xmm = [sem(f"s_xmm{b}") for b in range(2)]
        s_x2 = [sem(f"s_x2{b}") for b in range(2)]
        s_tmm = [sem(f"s_tmm{b}") for b in range(2)]
        s_ti = [sem(f"s_ti{b}") for b in range(2)]
        s_tt = [sem(f"s_tt{b}") for b in range(2)]
        s_scan = sem("s_scan")
        s_ru = sem("s_ru")
        s_s = sem("s_s"); s_y = sem("s_y")
        s_ti0 = [sem(f"s_ti0{b}") for b in range(2)]

        s_zero = sem("s_zero"); s_zf = sem("s_zf"); s_ycl = sem("s_ycl"); s_wout = sem("s_wout"); s_g2 = sem("s_g2")
        s_lnm = sem("s_lnm"); s_lnc = sem("s_lnc"); s_lnsq = sem("s_lnsq"); s_lnq = sem("s_lnq"); s_lns = sem("s_lns")
        s_lnn = sem("s_lnn"); s_lnt = sem("s_lnt"); s_lny = sem("s_lny")
        s_gc = sem("s_gc"); s_gsq = sem("s_gsq"); s_gp = sem("s_gp"); s_gv = sem("s_gv"); s_gsd = sem("s_gsd")
        s_gy = sem("s_gy"); s_gt = sem("s_gt"); s_gs = sem("s_gs"); s_gmm = sem("s_gmm"); s_go = sem("s_go")
        s_xo = [sem(f"s_xo{b}") for b in range(2)]
        s_rw = sem("s_rw"); s_yts = sem("s_yts"); s_omm = sem("s_omm"); s_h = sem("s_h");
        s_sd2 = sem("s_sd2"); s_u2 = sem("s_u2"); s_u2c = sem("s_u2c"); s_t2 = sem("s_t2"); s_u2T = sem("s_u2T")
        s_lmm = sem("s_lmm"); s_lg = sem("s_lg"); s_rte = sem("s_rte"); s_rta = sem("s_rta"); s_cmm = sem("s_cmm")
        s_slot = sem("s_slot"); s_ctl = sem("s_ctl"); s_sc = sem("s_sc")
        s_wg, s_wu, s_wd, s_xb = ([sem(f"s_{q}{b}") for b in range(2)] for q in ("wg", "wu", "wd", "xb"))
        s_xtm = sem("s_xtm"); s_xts = sem("s_xts"); s_gu = sem("s_gu"); s_th = sem("s_th"); s_hid = sem("s_hid")
        s_htm = sem("s_htm"); s_hts = sem("s_hts"); s_dn = sem("s_dn"); s_ye = sem("s_ye")
        s_yst = [sem(f"s_yst{b}") for b in range(2)]
        s_pw = sem("s_pw"); s_yg = [sem(f"s_yg{b}") for b in range(2)]; s_pin = [sem(f"s_pin{b}") for b in range(2)]
        s_hs = sem("s_hs"); s_sd3 = sem("s_sd3"); s_ns = sem("s_ns"); s_ntm = sem("s_ntm")
        s_nT = sem("s_nT"); s_plm = sem("s_plm"); s_ptm = sem("s_ptm"); s_pT = sem("s_pT"); s_prm = sem("s_prm")
        s_th3 = sem("s_th3"); s_ob = sem("s_ob"); s_sd4 = sem("s_sd4"); s_of = sem("s_of")
        s_out = [sem(f"s_out{b}") for b in range(2)]

        NL = len(LEVELS)
        block = ctx.enter_context(nc.Block())

        @block.sync
        def _(sp):
            sp.sem_inc(s_ycst, 16)
            sp.dma_start(cst[:, :], t["cst"]).then_inc(s_const, 16)
            sp.dma_start(vec[:, :], t["vec"]).then_inc(s_const, 16)
            xv = t["x"].rearrange("(t p) d -> t p d", p=P)
            for b in range(2):
                sp.dma_start(xin[b][:, 0:D], xv[b]).then_inc(s_x[b], 16)
            sp.dma_start(wz[0][:, 0:KT * 64], t["w_wa"]).then_inc(s_w[0], 16)
            sp.dma_start(wz[1][:, 0:KT * 96], t["w_g"]).then_inc(s_w[1], 16)
            sp.dma_start(wz[2][:, :], t["w_rkv"][2]).then_inc(s_w[2], 16)
            sp.dma_start(wa2[:, :], t["wa2"][0]).then_inc(s_wa2, 16)
            with sp.Fori(1, TT // 2) as i:
                for b in range(2):
                    sp.wait_ge(s_xn, 2 * i + b - 1)
                    sp.dma_start(xin[b][:, 0:D], xv[2 * i + b]).then_inc(s_x[b], 16)
            for s in range(2):
                sp.wait_ge(s_zmm[s], 1)
                sp.dma_start(wz[s][:, :], t["w_conv"][s]).then_inc(s_w[s], 16)
            with sp.Fori(0, PAIRS - 1) as j:
                for s in range(2):
                    sp.wait_ge(s_zmm[s], 2 * j + 2)
                    sp.dma_start(wz[s][:, :], t["w_rkv"][3 * j + s]).then_inc(s_w[s], 16)
                sp.wait_ge(s_zmm[0], 2 * j + 3)
                sp.dma_start(wz[0][:, :], t["w_conv"][2 * j + 2]).then_inc(s_w[0], 16)
                sp.wait_ge(s_amm, j + 1)
                sp.dma_start(wa2[:, :], t["wa2"][j + 1]).then_inc(s_wa2, 16)
                sp.wait_ge(s_zmm[1], 2 * j + 3)
                sp.dma_start(wz[1][:, :], t["w_conv"][2 * j + 3]).then_inc(s_w[1], 16)
                sp.wait_ge(s_zmm[2], j + 2)
                sp.dma_start(wz[2][:, :], t["w_rkv"][3 * j + 5]).then_inc(s_w[2], 16)
                sp.wait_ge(s_yc, j + 1)
                sp.dma_start(t["yconv"][j], yc[:, :]).then_inc(s_ycst, 16)
            for s in range(2):
                sp.wait_ge(s_zmm[s], 2 * PAIRS)
                sp.dma_start(wz[s][:, :], t["w_rkv"][3 * (PAIRS - 1) + s]).then_inc(s_w[s], 16)
            sp.wait_ge(s_yc, PAIRS)
            sp.dma_start(t["yconv"][PAIRS - 1], yc[:, :]).then_inc(s_ycst, 16)
            sp.wait_ge(s_ycst, 16 * (PAIRS + 1))
            sp.wait_ge(s_zero, 1)
            with sp.Fori(0, NBLK) as n:
                sp.dma_start(t["xbuf"][bass.ds(n * BLK, BLK), :], zero[:, :]).then_inc(s_zf, 16)
            with sp.Fori(E, NBLK) as n:
                sp.dma_start(t["ybuf"][bass.ds(n * BLK, BLK), :], zero[:, :]).then_inc(s_zf, 16)
            sp.wait_ge(s_zf, 16 * ZEROS)
            sp.wait_ge(s_y, NCH + 2)
            sp.wait_ge(s_s, NCH + 1)
            sp.dma_start(g2s[:, :], t["g2"]).then_inc(s_g2, 16)
            for j in range(PAIRS):
                sp.dma_start(yconv[:, j, :], t["yconv"][j]).then_inc(s_ycl, 16)
            sp.wait_ge(s_lny, PAIRS)
            sp.dma_start(wout[:, :, :], t["w_out"].rearrange("(k p) d -> p k d", p=P)).then_inc(s_wout, 16)
            sp.wait_ge(s_go, PAIRS)
            for b in range(2):
                sp.dma_start(xo[b][:, :], xv[b]).then_inc(s_xo[b], 16)
            sp.dma_start(rw[:, :, :], t["rw"].rearrange("(k p) n -> p k n", p=P)).then_inc(s_rw, 16)
            sp.dma_start(rbias[:, :], t["rb"].partition_broadcast(P)).then_inc(s_rw, 16)
            sp.dma_start(fgain[:, :], t["ffg"].partition_broadcast(P)).then_inc(s_rw, 16)
            with sp.Fori(1, TT // 2) as i:
                for b in range(2):
                    sp.wait_ge(s_h, 2 * i + b + 1)
                    sp.dma_start(xo[b][:, :], xv[2 * i + b]).then_inc(s_xo[b], 16)

            def gate_up_weights(b, e):
                sp.dma_start(wg[b][:, :, :], t["wg"][e].rearrange("(k p) f -> p k f", p=P)).then_inc(s_wg[b], 16)
                sp.dma_start(wu[b][:, :, :], t["wu"][e].rearrange("(k p) f -> p k f", p=P)).then_inc(s_wu[b], 16)

            def down_weights(b, e):
                sp.dma_start(wd[b][:, :, :], t["wd"][e].rearrange("(k p) d -> p k d", p=P)).then_inc(s_wd[b], 16)

            def block_rows(b, n):
                sp.dma_start(xb[b][:, :], t["xbuf"][bass.ds(n * BLK, BLK), :]).then_inc(s_xb[b], 16)

            sp.wait_ge(s_omm, TT + 2)
            gate_up_weights(0, 0)
            down_weights(0, 0)
            sp.wait_ge(s_slot, 2)
            sp.wait_ge(s_ctl, 1)
            sp.wait_ge(s_sc, 16 * 2 * TT)
            block_rows(0, 0)
            block_rows(1, 1)
            gate_up_weights(1, 1)
            down_weights(1, 1)
            sp.dma_start(plew[:, :, :], t["plew"].rearrange("(k p) d -> p k d", p=P)).then_inc(s_pw, 16)
            with sp.Fori(0, E // 2 - 1) as i:
                for b in range(2):
                    e = 2 * i + b
                    sp.wait_ge(s_xtm, e + 1)
                    block_rows(b, e + 2)
                    sp.wait_ge(s_gu, e + 1)
                    gate_up_weights(b, e + 2)
                    sp.wait_ge(s_dn, e + 1)
                    down_weights(b, e + 2)
            novf = sp.value_load(ctl[0:1, OVF:OVF + 1], min_val=0, max_val=OVF)
            with sp.Fori(0, OVF2) as i:
                for b in range(2):
                    n = 2 * i + b
                    with sp.If(novf > n):
                        e = sp.value_load(ctl[0:1, bass.ds(n, 1)], min_val=0, max_val=E - 1)
                        row = bass.ds(e, 1)
                        sp.wait_ge(s_xtm, n + E - 1)
                        block_rows(b, n + E)
                        sp.wait_ge(s_gu, n + E - 1)
                        sp.dma_start(wg[b][:, :, :], t["wg"][row].rearrange("o (k p) f -> p (o k) f", p=P))\
                            .then_inc(s_wg[b], 16)
                        sp.dma_start(wu[b][:, :, :], t["wu"][row].rearrange("o (k p) f -> p (o k) f", p=P))\
                            .then_inc(s_wu[b], 16)
                        sp.wait_ge(s_dn, n + E - 1)
                        sp.dma_start(wd[b][:, :, :], t["wd"][row].rearrange("o (k p) d -> p (o k) d", p=P))\
                            .then_inc(s_wd[b], 16)
                        sp.nop()
                    with sp.Else():
                        sp.nop()
            sp.wait_ge(s_dn, E + 2 * OVF2)
            sp.dma_start(projw[:, :, :], t["projw"].rearrange("(k p) d -> p k d", p=P)).then_inc(s_pw, 16)
            sp.dma_start(lastg[:, :], t["lastg"].partition_broadcast(P)).then_inc(s_pw, 16)
            pv = t["p"].rearrange("(t p) d -> t p d", p=P)
            for b in range(2):
                sp.dma_start(pin[b][:, :], pv[b]).then_inc(s_pin[b], 16)
            with sp.Fori(1, TT // 2) as i:
                for b in range(2):
                    sp.wait_ge(s_ptm, 2 * i + b - 1)
                    sp.dma_start(pin[b][:, :], pv[2 * i + b]).then_inc(s_pin[b], 16)
            for b in range(2):
                sp.wait_ge(s_out[b], 16 * (TT // 2 + 1))

        @block.tensor
        def _(pe):
            pe.sem_inc(s_zmm[2], 1)
            pe.wait_ge(s_const, 32)
            ident = K("ident")
            with pe.Fori(0, TT // 2) as i:
                for b in range(2):
                    pe.wait_ge(s_xn, 2 * i + b + 1)
                    pe.wait_ge(s_uT, 2 * i + b + 1)
                    for k in range(KT):
                        last = pe.transpose(ps[:, 2 * b + k // 4, (k % 4) * P:(k % 4 + 1) * P],
                                            xn[b][:, k * P:(k + 1) * P], ident)
                    last.then_inc(s_xT, 1)
            pe.wait_ge(s_uT, TT + 2)

            def z_tile(s, n, cols=P):
                pe.wait_ge(s_w[s], 16 * (n + 1) if s < 2 else 16 * n)
                if not (isinstance(n, int) and n == 0):
                    pe.wait_ge(s_z[s], n)
                for h in range(2):
                    for k in range(KT):
                        last = pe.matmul(ps[0:cols, 2 * s + h, :], wz[s][:, k * cols:(k + 1) * cols],
                                         uT[:, k, h * HALF:(h + 1) * HALF], start=(k == 0), stop=(k == KT - 1))
                last.then_inc(s_zmm[s], 1)

            z_tile(0, 0, 64)
            z_tile(1, 0, 96)
            pe.wait_ge(s_lora, 2)

            def pair(j, more):
                pe.wait_ge(s_wa2, 16 * j + 16)
                pe.wait_ge(s_kk, j + 1)
                for h in range(2):
                    last = pe.matmul(ps[:, 6 + h, :], wa2[0:32, :], wl[0:32, h * HALF:(h + 1) * HALF],
                                     start=True, stop=True)
                last.then_inc(s_dmm, 1)
                z_tile(0, 2 * j + 2)
                pe.wait_ge(s_dth, j + 1)
                for h in range(2):
                    last = pe.matmul(ps[:, 6 + h, :], wa2[32:64, :], wl[32:64, h * HALF:(h + 1) * HALF],
                                     start=True, stop=True)
                last.then_inc(s_amm, 1)
                z_tile(1, 2 * j + 2)
                z_tile(2, j + 1)
                if more:
                    z_tile(0, 2 * j + 3)
                pe.wait_ge(s_sq, j + 1)
                pe.wait_ge(s_ath, j + 1)
                for h in range(2):
                    last = pe.matmul(ps[64:66, 6 + h, :], K("sel2"), b_sq[:, h * HALF:(h + 1) * HALF],
                                     start=True, stop=True)
                last.then_inc(s_ssmm, 1)
                if more:
                    z_tile(1, 2 * j + 3)
                pe.wait_ge(s_rn, j + 1)
                for h in range(2):
                    last = pe.matmul(ps[:, 6 + h, :], cst[64:66, CCOL["selT2"]:CCOL["selT2"] + P],
                                     nrm[:, h * HALF:(h + 1) * HALF], start=True, stop=True)
                last.then_inc(s_bcmm, 1)

            z_tile(0, 1)
            z_tile(1, 1)
            with pe.Fori(0, PAIRS - 1) as j:
                pair(j, True)
            pair(PAIRS - 1, False)

            pe.wait_ge(s_pair, PAIRS + 1)
            pe.wait_ge(s_z[1], 2 * PAIRS + 1)
            pe.wait_ge(s_z[0], 2 * PAIRS + 1)

            def bank(b, q, w):
                return ps[:, 3 * b + q, 0:PAIRS * w].rearrange("p (a w) -> p a w", a=PAIRS)

            scan6 = ps[:, 6, 0:PAIRS * HD].rearrange("p (a w) -> p a w", a=PAIRS)
            scan6u = ps[:, 6, 256:512].rearrange("p (a w) -> p a w", a=PAIRS)
            scan7 = ps[:, 7, 0:PAIRS * HD].rearrange("p (a w) -> p a w", a=PAIRS)

            def two(x, p):
                return x[:, p, :, :].rearrange("p a c -> p (a c)")

            def scan_r(i, u, b):
                c = 2 * i + b
                pe.wait_ge(s_tt[b], NL * i + NL)
                pe.wait_ge(s_y, c + 2)
                pe.wait_ge(s_s, c + 1)
                for p in range(PAIRS):
                    pe.matmul(scan6[:, p, :], two(bdar[u][b], 2 * p), S[b][:, p, :], start=True, stop=False)
                    last = pe.matmul(scan6[:, p, :], two(aak[u][b], p), vtk[u][b][:, p, :], start=False, stop=True)
                last.then_inc(s_scan, 1)

            def scan_u(i, u, b):
                pe.wait_ge(s_ru, 4 * i + 2 * b + 1)
                for p in range(PAIRS):
                    last = pe.matmul(scan6u[:, p, :], two(TiT2[u][b], p), R[:, p, :], start=True, stop=True)
                last.then_inc(s_scan, 1)

            def scan_sy(i, u, b):
                pe.wait_ge(s_ru, 4 * i + 2 * b + 2)
                for p in range(PAIRS):
                    pe.matmul(scan7[:, p, :], btk[u][b][:, p, :], U[:, p, :], start=True, stop=False)
                    last = pe.matmul(scan7[:, p, :], ktk[u][b][:, p, :], vtk[u][b][:, p, :], start=False, stop=True)
                last.then_inc(s_scan, 1)
                for p in range(PAIRS):
                    pe.matmul(scan6[:, p, :], two(bdar[u][b], 2 * p + 1), S[b][:, p, :], start=True, stop=False)
                    pe.matmul(scan6[:, p, :], two(arb[u][b], p), U[:, p, :], start=False, stop=False)
                    last = pe.matmul(scan6[:, p, :], two(ark[u][b], p), vtk[u][b][:, p, :], start=False, stop=True)
                last.then_inc(s_scan, 1)

            def prepare(i, u, scan):
                def step(f, b):
                    if scan:
                        f(i - 1, 1 - u, b)

                for b in range(2):
                    ar = [pk[:, bass.ds(2 * i + b, 1), p, 0:2, :].rearrange("p o a c -> p (o a c)") for p in range(PAIRS)]
                    pe.wait_ge(s_bdx[b], i + 1)
                    for p in range(PAIRS):
                        last = pe.matmul(bank(b, 0, P)[:, p, :], two(bdbkv[b], 3 * p), ar[p], start=True, stop=True)
                    last.then_inc(s_gram[b], 1)
                    for p in range(PAIRS):
                        last = pe.matmul(bank(b, 1, P)[:, p, :], two(bdbkv[b], 3 * p + 1), ar[p], start=True, stop=True)
                    last.then_inc(s_gram[b], 1)
                    if scan:
                        pe.wait_ge(s_tt[b], NL * i)
                    for p in range(PAIRS):
                        last = pe.transpose(bank(b, 2, P)[:, p, :], two(bdbkv[b], 3 * p), ident)
                    last.then_inc(s_turn[b], 1)
                step(scan_r, 0)
                for b in range(2):
                    pe.wait_ge(s_msk[b], 3 * i + 2)
                    for p in range(PAIRS):
                        last = pe.transpose(bank(b, 0, P)[:, p, :], two(bdbkv[b], 3 * p + 1), ident)
                    last.then_inc(s_turn[b], 1)
                    pe.wait_ge(s_msk[b], 3 * i + 3)
                    for p in range(PAIRS):
                        last = pe.matmul(bank(b, 1, HD)[:, p, :], two(bdbkv[b], 3 * p + 2), K("istack"),
                                         start=True, stop=True)
                    last.then_inc(s_turn[b], 1)
                for b in range(2):
                    pe.wait_ge(s_tok[b], 3 * i + 1)
                    pe.wait_ge(s_ti0[b], i + 1)
                    for p in range(PAIRS):
                        last = pe.matmul(bank(b, 2, C)[:, p, :], two(TiT2[u][b], p), K("istack"), start=True, stop=True)
                    last.then_inc(s_tmm[b], 1)
                step(scan_u, 0)
                for lv in range(NL):
                    for b in range(2):
                        pe.wait_ge(s_loff[b], NL * i + lv + 1)
                        pe.wait_ge(s_ti[b], NL * i + lv + 1)
                        if lv == 0:
                            pe.wait_ge(s_tok[b], 3 * i + 3)
                        for p in range(PAIRS):
                            last = pe.matmul(bank(b, 0, C)[:, p, :], two(Loff[b][lv % 2], p), Ti[b][:, p, :],
                                             start=True, stop=True)
                        last.then_inc(s_xmm[b], 1)
                    if lv < 3:
                        step((scan_sy, scan_r, scan_sy)[lv], (0, 1, 1)[lv])
                    for b in range(2):
                        if lv > 0:
                            pe.wait_ge(s_tt[b], NL * i + lv)
                        if lv < NL - 1:
                            pe.wait_ge(s_xc[b], (NL - 1) * i + lv + 1)
                            for p in range(PAIRS):
                                last = pe.matmul(bank(b, 1, C)[:, p, :], two(TiT2[u][b], p), Xc[b][:, p, :],
                                                 start=True, stop=True)
                            last.then_inc(s_tmm[b], 1)
                        pe.wait_ge(s_x2[b], NL * i + lv + 1)
                        for p in range(PAIRS):
                            last = pe.matmul(bank(b, 2, P)[:, p, :], two(X2[b], p), two(TiT2[u][b], p),
                                             start=True, stop=True)
                        last.then_inc(s_tmm[b], 1)
                    if lv == 1:
                        step(scan_u, 1)

            pe.wait_ge(s_s, 1)
            prepare(0, 0, False)
            with pe.Fori(0, NCH // 4 - 1) as i:
                prepare(2 * i + 1, 1, True)
                prepare(2 * i + 2, 0, True)
            prepare(NCH // 2 - 1, 1, True)
            for b in range(2):
                for f in (scan_r, scan_u, scan_sy):
                    f(NCH // 2 - 1, 1, b)

            def bonus_and_gate(p):
                pe.wait_ge(s_gp, p + 1)
                if p > 0:
                    pe.wait_ge(s_go, p)
                for h2 in range(2):
                    last = pe.matmul(ps[:, 2 + h2, :], bonesrk[p % 2][:, :],
                                     bonus[p % 2][:, h2 * HALF:(h2 + 1) * HALF], start=True, stop=True)
                last.then_inc(s_gs, 1)
                for h2 in range(2):
                    last = pe.matmul(ps[:, 4 + h2, :], g2s[:, p * P:(p + 1) * P], sg_lo[:, h2 * HALF:(h2 + 1) * HALF],
                                     start=True, stop=True)
                last.then_inc(s_gmm, 1)

            def heads_turned(p):
                pe.wait_ge(s_gy, p + 1)
                for n in range(NCH):
                    last = pe.matmul(ps[:, n // 8, (n % 8) * C:(n % 8 + 1) * C],
                                     Ybd[p % 2][:, n, :, :].rearrange("p a c -> p (a c)"), K("istack"),
                                     start=True, stop=True)
                last.then_inc(s_gt, 1)

            def conv_sums(x, ready, done):
                for h2 in range(2):
                    for j in range(PAIRS):
                        if ready:
                            pe.wait_ge(ready, j + 1)
                        last = pe.matmul(ps[:, 6 + h2, :], K("ones"), x(j)[:, h2 * HALF:(h2 + 1) * HALF],
                                         start=(j == 0), stop=(j == PAIRS - 1))
                last.then_inc(done, 1)

            pe.wait_ge(s_y, NCH + 2)
            pe.wait_ge(s_s, NCH + 1)
            pe.wait_ge(s_glo, 3)
            pe.wait_ge(s_g2, 16)
            bonus_and_gate(0)
            pe.wait_ge(s_ycl, 16 * PAIRS)
            conv_sums(lambda j: yconv[:, j, :], None, s_lnm)
            pe.wait_ge(s_lnc, PAIRS)
            conv_sums(lambda j: squares[j], s_lnsq, s_lnq)
            heads_turned(0)
            for p in range(1, PAIRS):
                bonus_and_gate(p)
                heads_turned(p)

            pe.sem_inc(s_omm, 2)
            pe.wait_ge(s_wout, 16)
            pe.wait_ge(s_go, PAIRS)

            def out_product(n, b):
                pe.wait_ge(s_yts, n + 1)
                pe.wait_ge(s_h, n + 1)
                for h2 in range(2):
                    for k in range(KT):
                        last = pe.matmul(ps[:, 2 * b + h2, :], yTs[b][:, k, :], wout[:, k, h2 * HALF:(h2 + 1) * HALF],
                                         start=(k == 0), stop=(k == KT - 1))
                last.then_inc(s_omm, 1)

            def logits(n, b):
                pe.wait_ge(s_u2, n + 1)
                pe.wait_ge(s_u2T, n + 1)
                for k in range(KT):
                    last = pe.transpose(ps[:, 4 + k // 4, (k % 4) * P:(k % 4 + 1) * P], u2s[b][:, k * P:(k + 1) * P],
                                        ident)
                last.then_inc(s_t2, 1)
                pe.wait_ge(s_u2T, n + 2)
                pe.wait_ge(s_lg, n + 1)
                for k in range(KT):
                    last = pe.matmul(ps[:, 6, 0:G + E], u2T[:, k, :], rw[:, k, :], start=(k == 0), stop=(k == KT - 1))
                last.then_inc(s_lmm, 1)

            out_product(0, 0)
            pe.wait_ge(s_rw, 48)
            with pe.Fori(0, TT // 2 - 1) as i:
                for b in range(2):
                    out_product(2 * i + b + 1, 1 - b)
                    logits(2 * i + b, b)
            out_product(TT - 1, 1)
            logits(TT - 2, 0)
            logits(TT - 1, 1)
            pe.wait_ge(s_rte, 3)
            pe.matmul(ps[:, 0, 0:TT * E], K("before"), flat(Os), start=True, stop=True)
            pe.matmul(ps[:, 1, 0:TT * E], K("ones"), flat(Os), start=True, stop=True).then_inc(s_cmm, 1)

            def turn_rows(n, b, q):
                pe.wait_ge(s_xb[b], 16 * q + 16)
                pe.wait_ge(s_xts, n + 1)
                for k in range(KT):
                    last = pe.transpose(ps[:, 4 + k // 4, (k % 4) * P:(k % 4 + 1) * P], xb[b][:, k * P:(k + 1) * P], ident)
                last.then_inc(s_xtm, 1)

            def gate_up(n, b, q):
                pe.wait_ge(s_xts, n + 2)
                pe.wait_ge(s_hid, n + 1)
                for o, (w, sw) in enumerate(((wg, s_wg), (wu, s_wu))):
                    pe.wait_ge(sw[b], 16 * q + 16)
                    for k in range(KT):
                        last = pe.matmul(ps[:, o, :], xTs[:, k, :], w[b][:, k, :], start=(k == 0), stop=(k == KT - 1))
                last.then_inc(s_gu, 1)

            def turn_hidden(n):
                pe.wait_ge(s_hid, n + 2)
                for k in range(FF // P):
                    last = pe.transpose(ps[:, 6, k * P:(k + 1) * P], hid[:, k * P:(k + 1) * P], ident)
                last.then_inc(s_htm, 1)

            def down(n, b, q):
                pe.wait_ge(s_hts, n + 1)
                pe.wait_ge(s_wd[b], 16 * q + 16)
                pe.wait_ge(s_ye, n + 1)
                for h2 in range(2):
                    for k in range(FF // P):
                        last = pe.matmul(ps[:, 2 + h2, :], hTs[:, k, :], wd[b][:, k, h2 * HALF:(h2 + 1) * HALF],
                                         start=(k == 0), stop=(k == FF // P - 1))
                last.then_inc(s_dn, 1)

            pe.wait_ge(s_ctl, 1)
            turn_rows(0, 0, 0)
            gate_up(0, 0, 0)
            turn_rows(1, 1, 0)
            with pe.Fori(0, E // 2 - 1) as i:
                for b in range(2):
                    n = 2 * i + b
                    turn_hidden(n)
                    gate_up(n + 1, 1 - b, i + b)
                    turn_rows(n + 2, b, i + 1)
                    down(n, b, i)
            turn_hidden(E - 2)
            gate_up(E - 1, 1, E // 2 - 1)
            down(E - 2, 0, E // 2 - 1)
            turn_hidden(E - 1)
            down(E - 1, 1, E // 2 - 1)
            novf = pe.value_load(ctl[0:1, OVF:OVF + 1], min_val=0, max_val=OVF)
            with pe.Fori(0, OVF2) as i:
                for b in range(2):
                    n = 2 * i + b + E
                    with pe.If(novf > 2 * i + b):
                        turn_rows(n, b, i + E // 2)
                        gate_up(n, b, i + E // 2)
                        turn_hidden(n)
                        down(n, b, i + E // 2)
                        pe.nop()
                    with pe.Else():
                        pe.wait_ge(s_dn, n)
                        pe.sem_inc(s_dn, 1)

            pe.wait_ge(s_ye, E + 2 * OVF2 + 1)
            pe.wait_ge(s_pw, 48)
            def gate_tile(n, b, i):
                pe.wait_ge(s_ns, n + 1)
                pe.wait_ge(s_pT, n + 1)
                for k in range(KT):
                    last = pe.transpose(ps[:, k // 4, (k % 4) * P:(k % 4 + 1) * P], ns[b][:, k * P:(k + 1) * P], ident)
                last.then_inc(s_ntm, 1)
                pe.wait_ge(s_nT, n + 1)
                pe.wait_ge(s_pin[b], 16 * i + 16)
                for k in range(2):
                    last = pe.transpose(ps[:, 0, k * P:(k + 1) * P], pin[b][:, k * P:(k + 1) * P], ident)
                last.then_inc(s_ptm, 1)
                for h2 in range(2):
                    for k in range(KT):
                        last = pe.matmul(ps[:, 2 * b + 2 + h2, :], nT[:, k, :], plew[:, k, h2 * HALF:(h2 + 1) * HALF],
                                         start=(k == 0), stop=(k == KT - 1))
                last.then_inc(s_plm, 1)
                pe.wait_ge(s_pT, n + 2)
                pe.wait_ge(s_ob, n + 1)
                for h2 in range(2):
                    for k in range(2):
                        last = pe.matmul(ps[:, 6 + h2, :], pT[:, k, :], projw[:, k, h2 * HALF:(h2 + 1) * HALF],
                                         start=(k == 0), stop=(k == 1))
                last.then_inc(s_prm, 1)

            with pe.Fori(0, TT // 2) as i:
                for b in range(2):
                    gate_tile(2 * i + b, b, i)

        @block.scalar
        def _(act):
            act.sem_inc(s_z[2], 1)
            act.sem_inc(s_y, 2)
            act.wait_ge(s_const, 32)
            act.wait_ge(s_prep, 1)
            mine = Chain(act, s_act)
            with act.Fori(0, TT // 2) as i:
                mine.enter(i, 2)
                for b in range(2):
                    act.wait_ge(s_x[b], 16 * i + 16)
                    col = bass.ds(2 * i + b, 1)
                    mine.link(act.activation(b_e1[:, :], xin[b][:, 0:D], ACT.Square, accum_out=ssq[:, col]))
                    act.activation(std[:, col], ssq[:, col], ACT.Sqrt, scale=1.0 / D, bias=eps_rms[:, :]).then_inc(s_std, 1)

            mine.leave(TT // 2)

            def evac(s, n, out, func, rows=P, **kw):
                act.wait_ge(s_zmm[s], n + 1)
                act.activation(out, ps[0:rows, 2 * s:2 * s + 2, :].rearrange("p a c -> p (a c)"), func,
                               **kw).then_inc(s_z[s], 1)

            evac(0, 0, zr[0:64, 1:T + 1], ACT.Copy, 64)
            evac(1, 0, zk[0:96, 1:T + 1], ACT.Copy, 96)
            act.wait_ge(s_lora, 1)
            act.activation(lora[0:32, :], lora[0:32, :], ACT.Tanh).then_inc(s_lora, 1)
            act.wait_ge(s_glo, 1)
            act.activation(sg_lo[:, :], sg_lo[:, :], ACT.Tanh, scale=0.5).then_inc(s_glo, 1)
            low = ps[:, 6:8, :].rearrange("p a c -> p (a c)")

            def evac_shift(s, n, z, out, q, j):
                act.wait_ge(s_zmm[s], n + 1)
                z_ps = ps[:, 2 * s:2 * s + 2, :].rearrange("p a c -> p (a c)")
                act.activation(z[:, 1:T + 1], z_ps, ACT.Copy)
                act.activation(out[:, :], z_ps, ACT.Copy, scale=omu[:, bass.ds(j + q * PAIRS, 1)]).then_inc(s_z[s], 1)

            def pair(j, more):
                act.wait_ge(s_dmm, j + 1)
                act.wait_ge(s_pair, j + 1)
                mine.link(act.activation(b_ld[:, :], low, ACT.Tanh, scale=0.5, bias=w0h[:, bass.ds(j, 1)]))
                act.activation(b_ld[:, :], b_ld[:, :], ACT.Identity, scale=-DECAY, bias=ndecay[:, :]).then_inc(s_dth, 1)
                evac_shift(0, 2 * j + 2, zr, b_rs, 0, j)
                act.wait_ge(s_amm, j + 1)
                mine.link(act.activation(b_a[:, :], low, ACT.Tanh, scale=0.5, bias=a0h[:, bass.ds(j, 1)]))
                act.activation(b_a[:, :], b_a[:, :], ACT.Identity, scale=0.5, bias=half[:, :]).then_inc(s_ath, 1)
                evac_shift(1, 2 * j + 2, zk, b_ks, 1, j)
                evac_shift(2, j + 1, zv, b_t, 2, j)
                act.wait_ge(s_c, 2 * j + 1)
                act.activation(b_e1[:, :], b_c[:, :], ACT.Exp)
                act.wait_ge(s_c, 2 * j + 2)
                act.activation(b_ld[:, :], b_ld[:, :], ACT.Exp)
                act.activation(b_c[:, :], b_c[:, :], ACT.Exp, scale=-1.0).then_inc(s_exp, 1)
                act.wait_ge(s_kkr, j + 1)
                act.activation(b_kk[:, :], b_ks[:, :], ACT.Copy, scale=VD("kk", j))
                act.activation(b_sq[:, :], b_ks[:, :], ACT.Square, scale=VD("kk", j)).then_inc(s_sq, 1)
                if more:
                    evac(0, 2 * j + 3, zval[:, :], ACT.Copy)
                act.wait_ge(s_ssmm, j + 1)
                act.activation(nrm[:, :], ps[64:66, 6:8, :].rearrange("p a c -> p (a c)"), ACT.Sqrt).then_inc(s_nrm, 1)
                if more:
                    evac(1, 2 * j + 3, b_sq[:, :], ACT.Tanh, scale=0.5)

            evac(0, 1, zval[:, :], ACT.Copy)
            evac(1, 1, b_sq[:, :], ACT.Tanh, scale=0.5)
            with act.Fori(0, PAIRS - 1) as j:
                mine.enter(j, 2)
                pair(j, True)
            mine.leave(PAIRS - 1)
            pair(PAIRS - 1, False)


            def bank(b, q, w):
                return ps[:, 3 * b + q, 0:PAIRS * w]

            def block_diagonal(i, u):
                for b in range(2):
                    for hd in range(2):
                        rows = slice(64 * hd, 64 * hd + 64)
                        for out, kinds in ((bdar[u][b], slice(0, 2)), (bdbkv[b], slice(2, 5))):
                            src = pk[rows, bass.ds(2 * i + b, 1), :, kinds, :].rearrange("p o a k c -> p (o a) k c")
                            out = out.rearrange("p (a k) h c -> p a k h c", a=PAIRS)
                            last = act.activation(out[rows, :, :, hd, :], src, ACT.Copy)
                    last.then_inc(s_bdx[b], 1)

            def y_out(i, b):
                act.wait_ge(s_scan, 8 * i + 4 * b + 4)
                act.activation(Yall[:, bass.ds(2 * i + b, 1), :, :].rearrange("p o a c -> p (o a) c"),
                               ps[:, 6, 0:PAIRS * HD].rearrange("p (a c) -> p a c", a=PAIRS), ACT.Copy).then_inc(s_y, 1)

            def prepare(i, u, scan, more):
                for b in range(2):
                    act.wait_ge(s_turn[b], 3 * i + 1)
                    act.activation(flat(btk[u][b]), bank(b, 2, P), ACT.Copy).then_inc(s_tok[b], 1)
                for b in range(2):
                    act.wait_ge(s_turn[b], 3 * i + 2)
                    act.activation(flat(ktk[u][b]), bank(b, 0, P), ACT.Copy).then_inc(s_tok[b], 1)
                    act.wait_ge(s_turn[b], 3 * i + 3)
                    act.activation(flat(vtk[u][b]), bank(b, 1, HD), ACT.Copy).then_inc(s_tok[b], 1)
                for lv in range(NL):
                    for b in range(2):
                        act.wait_ge(s_xmm[b], NL * i + lv + 1)
                        if lv < NL - 1:
                            act.activation(flat(Xc[b]), bank(b, 0, C), ACT.Copy).then_inc(s_xc[b], 1)
                        for hd in range(2):
                            rows = slice(64 * hd, 64 * hd + 64)
                            last = act.activation(X2[b][rows, :, hd, :],
                                                  ps[rows, 3 * b, 0:PAIRS * C].rearrange("p (a c) -> p a c", a=PAIRS),
                                                  ACT.Copy)
                        last.then_inc(s_x2[b], 1)
                    if scan and lv in (1, 3):
                        y_out(i - 1, (lv - 1) // 2)
                    if more and lv == 3:
                        block_diagonal(i + 1, 1 - u)

            act.wait_ge(s_bdz, 8)
            block_diagonal(0, 0)
            prepare(0, 0, False, True)
            with act.Fori(0, NCH // 4 - 1) as i:
                prepare(2 * i + 1, 1, True, True)
                prepare(2 * i + 2, 0, True, True)
            prepare(NCH // 2 - 1, 1, True, False)
            for b in range(2):
                y_out(NCH // 2 - 1, b)

            def y_squares(p):
                act.wait_ge(s_gc, p + 1)
                act.activation(ysq[p % 2][:, :], Yc[p % 2][:, :], ACT.Square).then_inc(s_gsq, 1)

            def y_deviation(p):
                act.wait_ge(s_gv, p + 1)
                act.activation(gst[:, p % 2, 2, :], gst[:, p % 2, 1, :], ACT.Sqrt, scale=1.0 / HD, bias=eps_gn[:, :])\
                    .then_inc(s_gsd, 1)

            y_squares(0)
            for j in range(PAIRS):
                act.wait_ge(s_lnc, j + 1)
                act.activation(squares[j][:, :], yconv[:, j, :], ACT.Square).then_inc(s_lnsq, 1)
            y_deviation(0)
            y_squares(1)
            act.wait_ge(s_lnq, 1)
            act.activation(lnstd[:, :], low, ACT.Sqrt, scale=1.0 / 512, bias=eps_ln[:, :]).then_inc(s_lns, 1)
            for j in range(PAIRS):
                act.wait_ge(s_lnn, j + 1)
                act.activation(yconv[:, j, :], yconv[:, j, :], ACT.Identity, scale=lngh[:, j:j + 1],
                               bias=lnbh[:, j:j + 1]).then_inc(s_lnt, 1)
                act.wait_ge(s_lnt, 2 * j + 1)
                act.activation(squares[j][:, :], yconv[:, j, :], ACT.Tanh).then_inc(s_lnt, 1)
            for p in range(1, PAIRS):
                y_deviation(p)
                if p + 1 < PAIRS:
                    y_squares(p + 1)

            act.sem_inc(s_u2T, 1)
            act.wait_ge(s_go, PAIRS)
            act.wait_ge(s_lny, PAIRS)

            def y_tile(n, b):
                act.wait_ge(s_omm, n + 1)
                tok = bass.ds(P * n, P)
                act.activation(yTs[b][:, 0:PAIRS, :], yconv[:, :, tok], ACT.Copy)
                act.activation(yTs[b][:, PAIRS:KT, :], yT[:, :, tok], ACT.Copy).then_inc(s_yts, 1)

            def h_norm(n):
                act.wait_ge(s_h, n + 3)
                mine.link(act.activation(osq[:, :], h[:, bass.ds(n, 1), :].rearrange("p o d -> p (o d)"), ACT.Square,
                                         accum_out=ssq2[:, bass.ds(n, 1)]))
                act.activation(std2[:, bass.ds(n, 1)], ssq2[:, bass.ds(n, 1)], ACT.Sqrt, scale=1.0 / D,
                               bias=eps_rms[:, :]).then_inc(s_sd2, 1)

            def u2_turned(n):
                act.wait_ge(s_t2, n + 1)
                act.activation(flat(u2T), ps[:, 4:6, :].rearrange("p a c -> p (a c)"), ACT.Copy).then_inc(s_u2T, 1)

            y_tile(0, 0)
            y_tile(1, 1)
            h_norm(0)
            y_tile(2, 0)
            with act.Fori(0, TT // 2 - 2) as i:
                mine.enter(i, 2)
                for b in range(2):
                    n = 2 * i + b + 1
                    u2_turned(n - 1)
                    h_norm(n)
                    y_tile(n + 2, 1 - b)
            mine.leave(TT // 2 - 2)
            u2_turned(TT - 4)
            h_norm(TT - 3)
            y_tile(TT - 1, 1)
            for n in (TT - 2, TT - 1):
                u2_turned(n - 1)
                h_norm(n)
            u2_turned(TT - 1)
            act.wait_ge(s_rte, 1)
            act.activation(flat(gl2), flat(gl2), ACT.Exp).then_inc(s_rta, 1)
            act.wait_ge(s_rte, 2)
            act.activation(dm[:, :], dm[:, :], ACT.Exp).then_inc(s_rta, 1)

            act.sem_inc(s_xts, 1)
            act.sem_inc(s_ye, 1)
            for b in range(2):
                act.sem_inc(s_yst[b], 16)
            act.wait_ge(s_ctl, 1)

            def rows_turned(n):
                act.wait_ge(s_xtm, n + 1)
                act.activation(flat(xTs), ps[:, 4:6, :].rearrange("p a c -> p (a c)"), ACT.Copy).then_inc(s_xts, 1)

            def hidden_tanh(n):
                act.wait_ge(s_gu, n + 1)
                act.activation(th[:, :], ps[:, 0, :], ACT.Tanh, scale=0.5).then_inc(s_th, 1)

            def hidden_turned(n):
                act.wait_ge(s_htm, n + 1)
                act.activation(flat(hTs), ps[:, 6, :], ACT.Copy).then_inc(s_hts, 1)

            def rows_out(n, b, q):
                act.wait_ge(s_dn, n + 1)
                act.wait_ge(s_yst[b], 16 * q + 16)
                act.activation(ys[b][:, :], ps[:, 2:4, :].rearrange("p a c -> p (a c)"), ACT.Copy).then_inc(s_ye, 1)
                act.wait_ge(s_ye, n + 2)
                act.dma_start(t["ybuf"][bass.ds(n * BLK, BLK), :], ys[b][:, :]).then_inc(s_yst[b], 16)

            rows_turned(0)
            hidden_tanh(0)
            rows_turned(1)
            with act.Fori(0, E // 2 - 1) as i:
                for b in range(2):
                    n = 2 * i + b
                    hidden_turned(n)
                    hidden_tanh(n + 1)
                    rows_turned(n + 2)
                    rows_out(n, b, i)
            hidden_turned(E - 2)
            hidden_tanh(E - 1)
            rows_out(E - 2, 0, E // 2 - 1)
            hidden_turned(E - 1)
            rows_out(E - 1, 1, E // 2 - 1)
            novf = act.value_load(ctl[0:1, OVF:OVF + 1], min_val=0, max_val=OVF)
            with act.Fori(0, OVF2) as i:
                for b in range(2):
                    n = 2 * i + b + E
                    with act.If(novf > 2 * i + b):
                        rows_turned(n)
                        hidden_tanh(n)
                        hidden_turned(n)
                        rows_out(n, b, i + E // 2)
                        act.nop()
                    with act.Else():
                        act.sem_inc(s_ye, 1)
                        act.sem_inc(s_yst[b], 16)

            act.sem_inc(s_out[0], 16)
            act.sem_inc(s_out[1], 16)
            act.sem_inc(s_pT, 1)
            rows_of_out = t["out"].rearrange("(t p) d -> t p d", p=P)

            def moe_norm(n, b):
                col = bass.ds(n, 1)
                act.wait_ge(s_hs, 2 * n + 2)
                mine.link(act.activation(oq[b][:, :], hs[b][:, :], ACT.Square, accum_out=ssq[:, col]))
                act.activation(std[:, col], ssq[:, col], ACT.Sqrt, scale=1.0 / D, bias=eps_rms[:, :]).then_inc(s_sd3, 1)

            def embedding_turned(n):
                act.wait_ge(s_ptm, n + 1)
                act.activation(flat(pT), ps[:, 0, 0:PLE], ACT.Copy).then_inc(s_pT, 1)

            def gate_and_out(n, b):
                col = bass.ds(n, 1)
                act.wait_ge(s_plm, n + 1)
                act.activation(th2[b][:, :], ps[:, 2 * b + 2:2 * b + 4, :].rearrange("p a c -> p (a c)"), ACT.Tanh,
                               scale=0.5).then_inc(s_th3, 1)
                act.wait_ge(s_ob, n + 2)
                mine.link(act.activation(oq[b][:, :], ob[b][:, :], ACT.Square, accum_out=ssq2[:, col]))
                act.activation(std2[:, col], ssq2[:, col], ACT.Sqrt, scale=1.0 / D, bias=eps_rms[:, :]).then_inc(s_sd4, 1)
                act.wait_ge(s_of, n + 1)
                act.dma_start(rows_of_out[n], ob[b][:, :]).then_inc(s_out[b], 16)

            moe_norm(0, 0)
            with act.Fori(0, TT // 2 - 1) as i:
                mine.enter(i, 4)
                for b in range(2):
                    embedding_turned(2 * i + b)
                    moe_norm(2 * i + b + 1, 1 - b)
                    gate_and_out(2 * i + b, b)
            mine.leave(TT // 2 - 1)
            embedding_turned(TT - 2)
            moe_norm(TT - 1, 1)
            gate_and_out(TT - 2, 0)
            embedding_turned(TT - 1)
            gate_and_out(TT - 1, 1)

        @block.gpsimd
        def _(pool):
            pool.memset(glu[:, 0:TAPS - 1], 0.0).then_inc(s_pool, 1)
            pool.memset(reset[:, :], 1.0).then_inc(s_pool, 1)
            pool.wait_ge(s_pool, 2)
            pool.memset(reset[:, :].rearrange("p (n c) -> p n c", c=C)[:, :, 0:1], 0.0).then_inc(s_pool, 1)
            pool.wait_ge(s_pair, PAIRS + 1)
            pool.wait_ge(s_ycst, 16 * (PAIRS + 1))
            for x in bdar[0] + X2 + bdar[1]:
                pool.memset(x, 0.0).then_inc(s_bdz, 1)
            pool.memset(zero[:, :], 0.0).then_inc(s_zero, 1)
            pool.memset(S[0][:, :, :], 0.0).then_inc(s_s, 1)
            own = Chain(pool, s_pool)
            own.n = 3

            def prepare(i, u):
                for b in range(2):
                    pool.wait_ge(s_msk[b], 3 * i + 1)
                    own.link(pool.tensor_tensor(TiT2[u][b], twice(LT[b][:, :, :]), over_pairs2(K("first2")), ALU.mult))
                    pool.tensor_tensor(TiT2[u][b], TiT2[u][b], over_pairs2(K("ident")), ALU.add).then_inc(s_ti0[b], 1)
                for lv in range(NL):
                    for b in range(2):
                        if lv >= 2:
                            pool.wait_ge(s_xmm[b], NL * i + lv - 1)
                        mask = cst[:, CCOL["levels2"] + lv * P:CCOL["levels2"] + (lv + 1) * P]
                        pool.tensor_tensor(Loff[b][lv % 2][:, :, :, :], twice(LT[b][:, :, :]), over_pairs2(mask),
                                           ALU.mult).then_inc(s_loff[b], 1)

            with pool.Fori(0, NCH // 4) as i:
                own.enter(i, 4)
                prepare(2 * i, 0)
                prepare(2 * i + 1, 1)
            own.leave(NCH // 4)
            pool.wait_ge(s_y, NCH + 2)
            pool.wait_ge(s_s, NCH + 1)
            for q in range(2):
                pool.memset(Ybd[q], 0.0).then_inc(s_bdz, 1)

            pool.sem_inc(s_u2c, 2)
            with pool.Fori(0, TT // 2) as i:
                for b in range(2):
                    pool.wait_ge(s_u2, 2 * i + b + 1)
                    pool.tensor_copy(u2[:, bass.ds(2 * i + b, 1), :].rearrange("p o d -> p (o d)"), u2s[b][:, :])\
                        .then_inc(s_u2c, 1)
            pool.wait_ge(s_slot, 2)
            pool.wait_ge(s_zf, 16 * ZEROS)
            pool.wait_ge(s_u2c, TT + 2)
            for n in range(TT):
                for k in range(2):
                    pool.indirect_dma_start(out=t["xbuf"][:, :], out_offset=bass.IndirectOffsetOnAxis(ap=slot[k][:, n:n + 1], axis=0),
                                            in_=u2[:, n, :], in_offset=None).then_inc(s_sc, 16)
            for b in range(2):
                pool.wait_ge(s_yst[b], 16 * (E // 2 + OVF2 + 1))
            for n in range(TT):
                b = n % 2
                if n >= 2:
                    pool.wait_ge(s_hs, 2 * (n - 2) + 2)
                for k in range(2):
                    pool.indirect_dma_start(out=yg[b][k][:, :], out_offset=None, in_=t["ybuf"][:, :],
                                            in_offset=bass.IndirectOffsetOnAxis(ap=slot[k][:, n:n + 1], axis=0))\
                        .then_inc(s_yg[b], 16)

        @block.vector
        def _(dve):
            own = Chain(dve, s_dve)
            dve.sem_inc(s_uT, 2)
            dve.sem_inc(s_kk, 1)
            dve.sem_inc(s_pair, 1)
            dve.memset(ndecay[:, :], -DECAY)
            dve.memset(half[:, :], 0.5)
            dve.memset(eps_rms[:, :], 1e-6)
            dve.memset(eps_ln[:, :], 1e-5)
            dve.memset(eps_gn[:, :], 64e-5)
            dve.wait_ge(s_const, 32)
            for out, name, n in ((w0h, "w0", 4), (a0h, "a0", 4), (lngh, "lng", 4), (lnbh, "lnb", 4),
                                 (convwh, "convw", PAIRS * TAPS)):
                dve.tensor_scalar(out[:, :], V(name, 0, n), 0.5, None, ALU.mult)
            last = dve.tensor_scalar(omu[:, :], V("mu_r", 0, 3 * PAIRS), -1.0, 1.0, ALU.mult, ALU.add)
            last.then_inc(s_prep, 1)
            with dve.Fori(0, TT // 2) as i:
                own.enter(i, 2)
                for b in range(2):
                    col = bass.ds(2 * i + b, 1)
                    dve.wait_ge(s_std, 2 * i + b + 1)
                    own.link(dve.reciprocal(rstd[:, col], std[:, col]))
                    dve.tensor_scalar(xn[b][:, 0:D], xin[b][:, 0:D], rstd[:, col], None, ALU.mult).then_inc(s_xn, 1)
                for b in range(2):
                    dve.wait_ge(s_xT, 2 * i + b + 1)
                    for q in range(2):
                        gain = V("mixg", 4 * q, 4).unsqueeze(2).to_broadcast([P, 4, P])
                        last = dve.tensor_tensor(uT[:, 4 * q:4 * q + 4, bass.ds(256 * i + P * b, P)],
                                                 ps[:, 2 * b + q, :].rearrange("p (k c) -> p k c", k=4), gain, ALU.mult)
                    last.then_inc(s_uT, 1)
            own.leave(TT // 2)
            for z in (zr, zk, zv):
                last = dve.memset(z[:, 0:1], 0.0)
            own.link(last)

            def shift(z, out, mu, rows=P):
                own.link(dve.tensor_tensor(out, z[0:rows, 0:T], z[0:rows, 1:T + 1], ALU.subtract))
                return dve.scalar_tensor_tensor(out=out, in0=out, scalar=mu, in1=z[0:rows, 1:T + 1],
                                                op0=ALU.mult, op1=ALU.add)

            dve.wait_ge(s_z[0], 1)
            shift(zr, lora[:, :], V("mu_wa", rows=64), 64).then_inc(s_lora, 1)
            dve.wait_ge(s_z[1], 1)
            shift(zk, sg_lo[:, :], V("mu_g", rows=96), 96).then_inc(s_glo, 1)
            dve.wait_ge(s_glo, 2)
            dve.tensor_scalar(sg_lo[:, :], sg_lo[:, :], 0.5, 0.5, ALU.mult, ALU.add).then_inc(s_glo, 1)

            dve.wait_ge(s_pool, 3)

            def chunked(x):
                return x.rearrange("p (n c) -> p n c", c=C)

            def pair(j):
                def packed(kind):
                    return pk[:, :, bass.ds(j, 1), kind, :].rearrange("p n o c -> p n (o c)")

                dve.wait_ge(s_dth, j + 1)
                dve.tensor_tensor_scan(b_c[:, :], reset[:, :], b_ld[:, :], 0.0, ALU.mult, ALU.add).then_inc(s_c, 1)
                dve.wait_ge(s_c, 2 * j + 1)
                dve.tensor_tensor(b_ld[:, :], b_c[:, :], b_ld[:, :], ALU.subtract).then_inc(s_c, 1)
                dve.wait_ge(s_z[0], 2 * j + 3)
                own.link(dve.scalar_tensor_tensor(out=b_rs[:, :], in0=zr[:, 0:T], scalar=VD("mu_r", j), in1=b_rs[:, :],
                                                  op0=ALU.mult, op1=ALU.add))
                dve.wait_ge(s_ath, j + 1)
                dve.wait_ge(s_z[1], 2 * j + 3)
                dve.scalar_tensor_tensor(out=b_ks[:, :], in0=zk[:, 0:T], scalar=VD("mu_k", j), in1=b_ks[:, :],
                                         op0=ALU.mult, op1=ALU.add).then_inc(s_kkr, 1)
                dve.wait_ge(s_kkr, j + 1)
                dve.wait_ge(s_z[2], j + 2)
                own.link(dve.scalar_tensor_tensor(out=packed(4), in0=chunked(zv[:, 0:T]), scalar=VD("mu_v", j),
                                                  in1=chunked(b_t[:, :]), op0=ALU.mult, op1=ALU.add))
                own.link(dve.tensor_scalar(b_t[:, :], b_a[:, :], -1.0, VD("ka", j), ALU.add, ALU.mult))
                own.link(dve.scalar_tensor_tensor(out=b_t[:, :], in0=b_t[:, :], scalar=1.0, in1=b_ks[:, :],
                                                  op0=ALU.add, op1=ALU.mult))
                dve.wait_ge(s_exp, j + 1)
                dve.tensor_tensor(packed(1), chunked(b_rs[:, :]), chunked(b_e1[:, :]), ALU.mult)
                dve.tensor_tensor(packed(3), chunked(b_t[:, :]), chunked(b_c[:, :]), ALU.mult)
                dve.tensor_copy(PCH[:, :, bass.ds(j, 1)], chunked(b_e1[:, :])[:, :, C - 1:C])
                dve.wait_ge(s_nrm, j + 1)
                own.link(dve.tensor_scalar(nrm[:, :], nrm[:, :], 1e-12, None, ALU.max))
                dve.reciprocal(nrm[:, :], nrm[:, :]).then_inc(s_rn, 1)
                dve.wait_ge(s_bcmm, j + 1)
                dve.tensor_tensor(b_kk[:, :], b_kk[:, :], ps[:, 6:8, :].rearrange("p a c -> p (a c)"), ALU.mult)\
                    .then_inc(s_kk, 1)
                dve.wait_ge(s_kk, j + 2)
                own.link(dve.tensor_tensor(b_a[:, :], b_kk[:, :], b_a[:, :], ALU.mult))
                dve.tensor_tensor(packed(2), chunked(b_a[:, :]), chunked(b_c[:, :]), ALU.mult)
                dve.scalar_tensor_tensor(out=packed(0), in0=chunked(b_kk[:, :]), scalar=-1.0, in1=chunked(b_ld[:, :]),
                                         op0=ALU.mult, op1=ALU.mult).then_inc(s_pair, 1)

            def conv(j):
                dve.wait_ge(s_z[0], 2 * j + 2)
                dve.wait_ge(s_z[1], 2 * j + 2)
                own.link(dve.scalar_tensor_tensor(out=glu[:, TAPS - 1:TAPS - 1 + T], in0=b_sq[:, :], scalar=1.0,
                                                  in1=zval[:, :], op0=ALU.add, op1=ALU.mult))
                dve.wait_ge(s_ycst, 16 * j + 16)

                def tap(s):
                    return convwh[:, bass.ds(j * TAPS + s, 1)]

                for k in range(TAPS):
                    for t0 in (0, HALF):
                        out, x = yc[:, t0:t0 + HALF], glu[:, k + t0:k + t0 + HALF]
                        if k == 0:
                            ins = dve.tensor_scalar(out, x, tap(0), VD("convb", j), ALU.mult, ALU.add)
                        else:
                            ins = dve.scalar_tensor_tensor(out=out, in0=x, scalar=tap(k), in1=out, op0=ALU.mult,
                                                           op1=ALU.add)
                        if k < TAPS - 1:
                            own.link(ins, 1)
                        elif t0 == 0:
                            own.link(ins, 0)
                ins.then_inc(s_yc, 1)

            conv(0)
            with dve.Fori(0, PAIRS - 1) as j:
                own.enter(j, 68)
                pair(j)
                conv(j + 1)
            own.leave(PAIRS - 1)
            pair(PAIRS - 1)

            dve.wait_ge(s_ycst, 16 * (PAIRS + 1))
            dve.wait_ge(s_pair, PAIRS + 1)
            for x in bdbkv:
                dve.memset(x, 0.0).then_inc(s_bdz, 1)
            def bank(b, q, w):
                return ps[:, 3 * b + q, 0:PAIRS * w].rearrange("p (a w) -> p a w", a=PAIRS)

            def scan_r(i, b):
                dve.wait_ge(s_scan, 8 * i + 4 * b + 1)
                dve.tensor_copy(flat(R), ps[:, 6, 0:256]).then_inc(s_ru, 1)

            def scan_u(i, b):
                dve.wait_ge(s_scan, 8 * i + 4 * b + 2)
                dve.tensor_copy(flat(U), ps[:, 6, 256:512]).then_inc(s_ru, 1)

            def scan_s(i, b):
                dve.wait_ge(s_scan, 8 * i + 4 * b + 3)
                own.link(dve.tensor_tensor(flat(Stmp), ps[:, 7, 0:256], flat(S[b]), ALU.add))
                decay = PCH[:, bass.ds(2 * i + b, 1), :].rearrange("p o a -> p (o a)").unsqueeze(2)\
                    .to_broadcast([P, PAIRS, HD])
                dve.tensor_tensor(S[1 - b][:, :, :], Stmp[:, :, :], decay, ALU.mult).then_inc(s_s, 1)

            def prepare(i, u, scan):
                def step(f, b):
                    if scan:
                        f(i - 1, b)

                for b in range(2):
                    dve.wait_ge(s_gram[b], 2 * i + 1)
                    g1, g2 = bank(b, 0, P), bank(b, 1, P)
                    dve.tensor_tensor(LT[b][:, :, :], g1[:, :, 0:C], over_pairs(K("strict")), ALU.mult)\
                        .then_inc(s_msk[b], 1)
                    dve.tensor_tensor(arb[u][b], twice(g1[:, :, C:P]), over_pairs2(K("incl2")), ALU.mult)\
                        .then_inc(s_msk[b], 1)
                    dve.wait_ge(s_gram[b], 2 * i + 2)
                    dve.tensor_tensor(aak[u][b], twice(g2[:, :, 0:C]), over_pairs2(K("strict2")), ALU.mult)
                    dve.tensor_tensor(ark[u][b], twice(g2[:, :, C:P]), over_pairs2(K("incl2")), ALU.mult)\
                        .then_inc(s_msk[b], 1)
                step(scan_r, 0)
                for b in range(2):
                    dve.wait_ge(s_tmm[b], 2 * NL * i + 1)
                    dve.tensor_copy(Ti[b][:, :, :], bank(b, 2, C)).then_inc(s_ti[b], 1)
                step(scan_u, 0)
                for lv in range(NL):
                    if lv == 2:
                        step(scan_u, 1)
                    for b in range(2):
                        if lv < NL - 1:
                            dve.wait_ge(s_tmm[b], 2 * NL * i + 2 * lv + 2)
                            dve.tensor_tensor(Ti[b][:, :, :], Ti[b][:, :, :], bank(b, 1, C), ALU.add)\
                                .then_inc(s_ti[b], 1)
                        dve.wait_ge(s_tmm[b], 2 * NL * i + min(2 * lv + 3, 2 * NL))
                        dve.tensor_tensor(flat2(TiT2[u][b]), flat2(TiT2[u][b]), ps[:, 3 * b + 2, :], ALU.add)\
                            .then_inc(s_tt[b], 1)
                    if lv < 3:
                        step((scan_s, scan_r, scan_s)[lv], (0, 1, 1)[lv])

            prepare(0, 0, False)
            with dve.Fori(0, NCH // 4 - 1) as i:
                own.enter(i, 4)
                prepare(2 * i + 1, 1, True)
                prepare(2 * i + 2, 0, True)
            own.leave(NCH // 4 - 1)
            prepare(NCH // 2 - 1, 1, True)
            for b in range(2):
                for f in (scan_r, scan_u, scan_s):
                    f(NCH // 2 - 1, b)

            low = ps[:, 6:8, :].rearrange("p a c -> p (a c)")
            banks = lambda q: ps[:, q:q + 2, :].rearrange("p a c -> p (a c)")
            one = lambda p, kind: pk[:, :, p, kind, :]
            wide = lambda x: x.unsqueeze(2).to_broadcast([x.shape[0], NCH, HD])

            def centre(p):
                q, yv = p % 2, Yall[:, :, p, :]
                own.link(dve.tensor_reduce(gst[:, q, 0, :], yv, AX_X, ALU.add))
                own.link(dve.tensor_scalar(gst[:, q, 0, :], gst[:, q, 0, :], -1.0 / HD, None, ALU.mult))
                dve.tensor_tensor(chunked(Yc[q][:, :]), yv, wide(gst[:, q, 0, :]), ALU.add).then_inc(s_gc, 1)
                dve.tensor_scalar(bonesrk[q][:, :], K("bones"), V("rk", p), None, ALU.mult)
                dve.tensor_tensor(chunked(bonus[q][:, :]), one(p, 1), one(p, 3), ALU.mult).then_inc(s_gp, 1)

            def normalise(p):
                q = p % 2
                dve.wait_ge(s_gsq, p + 1)
                dve.tensor_reduce(gst[:, q, 1, :], chunked(ysq[q][:, :]), AX_X, ALU.add).then_inc(s_gv, 1)
                dve.wait_ge(s_gsd, p + 1)
                own.link(dve.reciprocal(gst[:, q, 3, :], gst[:, q, 2, :]))
                dve.wait_ge(s_gc, p + 1)
                for h2 in range(2):
                    rows = slice(64 * h2, 64 * h2 + 64)
                    last = dve.tensor_tensor(Ybd[q][rows, :, h2, :], chunked(Yc[q][rows, :]), wide(gst[rows, q, 3, :]),
                                             ALU.mult)
                last.then_inc(s_gy, 1)

            def gated(p):
                b2 = bonus[p % 2]
                dve.wait_ge(s_gt, p + 1)
                own.link(dve.tensor_scalar(b1[:, :], banks(0), V("gng", p), V("gnb", p), ALU.mult, ALU.add))
                dve.wait_ge(s_gs, p + 1)
                own.link(dve.tensor_tensor(chunked(b2[:, :]), chunked(banks(2)), one(p, 4), ALU.mult))
                own.link(dve.tensor_tensor(b1[:, :], b1[:, :], b2[:, :], ALU.add))
                dve.wait_ge(s_gmm, p + 1)
                dve.tensor_tensor(yT[:, p, :], b1[:, :], banks(4), ALU.mult).then_inc(s_go, 1)

            dve.wait_ge(s_y, NCH + 2)
            dve.wait_ge(s_s, NCH + 1)
            dve.wait_ge(s_zf, 16 * ZEROS)
            centre(0)
            dve.wait_ge(s_lnm, 1)
            for j in range(PAIRS):
                dve.scalar_tensor_tensor(out=yconv[:, j, :], in0=low, scalar=-1.0 / 512, in1=yconv[:, j, :],
                                         op0=ALU.mult, op1=ALU.add).then_inc(s_lnc, 1)
            dve.wait_ge(s_bdz, 10)
            normalise(0)
            centre(1)
            dve.wait_ge(s_lns, 1)
            own.link(dve.reciprocal(lnstd[:, :], lnstd[:, :]))
            dve.wait_ge(s_lnc, PAIRS)
            dve.wait_ge(s_lnsq, PAIRS)
            for j in range(PAIRS):
                dve.tensor_tensor(yconv[:, j, :], yconv[:, j, :], lnstd[:, :], ALU.mult).then_inc(s_lnn, 1)
            gated(0)
            normalise(1)
            centre(2)
            for j in range(PAIRS):
                dve.wait_ge(s_lnt, 2 * j + 2)
                dve.scalar_tensor_tensor(out=yconv[:, j, :], in0=squares[j][:, :], scalar=1.0, in1=yconv[:, j, :],
                                         op0=ALU.add, op1=ALU.mult).then_inc(s_lny, 1)
            gated(1)
            normalise(2)
            centre(3)
            gated(2)
            normalise(3)
            gated(3)
            dve.sem_inc(s_h, 2)
            dve.sem_inc(s_lg, 1)


            dve.wait_ge(s_rw, 48)

            def residual(n, b, i):
                row = h[:, bass.ds(n, 1), :].rearrange("p o d -> p (o d)")
                dve.wait_ge(s_omm, n + 3)
                dve.wait_ge(s_xo[b], 16 * i + 16)
                dve.tensor_tensor(row, banks(2 * b), xo[b][:, :], ALU.add).then_inc(s_h, 1)
                dve.wait_ge(s_sd2, n + 1)
                own.link(dve.reciprocal(rstd2[:, bass.ds(n, 1)], std2[:, bass.ds(n, 1)]))
                dve.wait_ge(s_u2c, n + 1)
                dve.scalar_tensor_tensor(out=u2s[b][:, :], in0=row, scalar=rstd2[:, bass.ds(n, 1)], in1=fgain[:, :],
                                         op0=ALU.mult, op1=ALU.mult).then_inc(s_u2, 1)

            def keep_logits(n):
                dve.wait_ge(s_lmm, n + 1)
                dve.tensor_tensor(lg[:, bass.ds(n, 1), :].rearrange("p o d -> p (o d)"), ps[:, 6, 0:G + E], rbias[:, :],
                                  ALU.add).then_inc(s_lg, 1)

            residual(0, 0, 0)
            with dve.Fori(0, TT // 2 - 1) as i:
                own.enter(i, 2)
                for b in range(2):
                    residual(2 * i + b + 1, 1 - b, i + b)
                    keep_logits(2 * i + b)
            own.leave(TT // 2 - 1)
            residual(TT - 1, 1, TT // 2 - 1)
            keep_logits(TT - 2)
            keep_logits(TT - 1)
            dve.wait_ge(s_lg, TT + 1)

            def bc(x, n):
                return x.unsqueeze(2).to_broadcast([P, TT, n])

            def first_max(x, n, top, work, onehot, prefer):
                own.link(dve.tensor_reduce(top[:, :], x, AX_X, ALU.max))
                own.link(dve.tensor_tensor(work[:, :, :], x, bc(top, n), ALU.is_equal))
                own.link(dve.tensor_tensor(work[:, :, :], work[:, :, :], prefer.unsqueeze(1).to_broadcast([P, TT, n]),
                                           ALU.mult))
                own.link(dve.tensor_reduce(gtop[:, :], work[:, :, :], AX_X, ALU.max))
                own.link(dve.tensor_tensor(onehot[:, :, :], work[:, :, :], bc(gtop, n), ALU.is_equal))

            gl = lg[:, :, 0:G]
            el = lg[:, :, G:G + E].rearrange("p t (g e) -> p t g e", g=G)
            first_max(gl, G, gmax, gl1, og, K("prefer4"))
            dve.tensor_tensor(gl2[:, :, :], gl, bc(gmax, G), ALU.subtract).then_inc(s_rte, 1)
            four = lambda x: x.rearrange("p t (g e) -> p t g e", g=G)
            by_group = og.unsqueeze(3).to_broadcast([P, TT, G, EPG])
            by_expert = lambda x: x.unsqueeze(2).to_broadcast([P, TT, G, EPG])
            own.link(dve.tensor_tensor(four(r_a), el, by_group, ALU.mult))
            own.link(dve.tensor_reduce(esel[:, :, :], r_a.rearrange("p t (g e) -> p t e g", g=G), AX_X, ALU.add))
            first_max(esel, EPG, m1, ew, o1, K("prefer8"))
            own.link(dve.scalar_tensor_tensor(out=flat(e2nd), in0=flat(o1), scalar=-1e30, in1=flat(esel),
                                              op0=ALU.mult, op1=ALU.add))
            first_max(e2nd, EPG, m2, ew, o2, K("prefer8"))
            dve.tensor_tensor(dm[:, :], m2[:, :], m1[:, :], ALU.subtract).then_inc(s_rte, 1)
            dve.tensor_tensor(four(O1), by_group, by_expert(o1), ALU.mult)
            own.link(dve.tensor_tensor(four(O2), by_group, by_expert(o2), ALU.mult))
            dve.tensor_tensor(flat(Os), flat(O1), flat(O2), ALU.add).then_inc(s_rte, 1)
            dve.wait_ge(s_rta, 2)
            own.link(dve.tensor_reduce(gsum[:, :], gl2[:, :, :], AX_X, ALU.add))
            own.link(dve.reciprocal(gp[:, :], gsum[:, :]))
            own.link(dve.tensor_scalar(m1[:, :], dm[:, :], 1.0, None, ALU.add))
            own.link(dve.reciprocal(m2[:, :], m1[:, :]))
            own.link(dve.tensor_tensor(gate[0][:, :], m2[:, :], gp[:, :], ALU.mult))
            own.link(dve.tensor_tensor(gate[1][:, :], gate[0][:, :], dm[:, :], ALU.mult))
            dve.wait_ge(s_cmm, 1)
            own.link(dve.memset(tbase[:, 0, :], 0.0))
            own.link(dve.tensor_copy(flat(r_b), ps[:, 1, 0:TT * E]))
            for n in range(1, TT):
                own.link(dve.tensor_tensor(tbase[:, n, :], tbase[:, n - 1, :], r_b[:, n - 1, :], ALU.add))
            own.link(dve.tensor_tensor(cnt[:, :], tbase[:, TT - 1, :], r_b[:, TT - 1, :], ALU.add))
            own.link(dve.tensor_tensor(flat(rank), ps[:, 0, 0:TT * E], flat(tbase), ALU.add))
            own.link(dve.tensor_scalar(nb[:, :], cnt[:, :], float(BLK), None, ALU.is_gt))
            for q in range(2, T // BLK):
                own.link(dve.scalar_tensor_tensor(out=nb[:, :], in0=cnt[:, :], scalar=float(q * BLK), in1=nb[:, :],
                                                  op0=ALU.is_gt, op1=ALU.add))
            own.link(dve.tensor_tensor_scan(incl[:, :], K("ones", E), nb[:, :], 0.0, ALU.mult, ALU.add))
            own.link(dve.tensor_tensor(excl[:, :], incl[:, :], nb[:, :], ALU.subtract))
            own.link(dve.tensor_scalar(excl[:, :], excl[:, :], float(BLK), float((E - 1) * BLK), ALU.mult, ALU.add))
            own.link(dve.tensor_tensor(excl[:, :], excl[:, :], K("ebase"), ALU.subtract))
            over_tiles = lambda x: x.unsqueeze(1).to_broadcast([P, TT, E])
            own.link(dve.tensor_scalar(flat(r_a), flat(rank), float(BLK), None, ALU.is_ge))
            own.link(dve.tensor_tensor(r_a[:, :, :], r_a[:, :, :], over_tiles(excl), ALU.mult))
            own.link(dve.tensor_tensor(r_b[:, :, :], rank[:, :, :], over_tiles(K("ebase")), ALU.add))
            own.link(dve.tensor_tensor(flat(slotm), flat(r_a), flat(r_b), ALU.add))
            for k, O in enumerate((O1, O2)):
                own.link(dve.tensor_tensor(flat(r_a), flat(slotm), flat(O), ALU.mult))
                own.link(dve.tensor_reduce(gsum[:, :], r_a[:, :, :], AX_X, ALU.add))
                dve.tensor_copy(slot[k][:, :], gsum[:, :]).then_inc(s_slot, 1)
                dve.wait_ge(s_slot, k + 1)
            own.link(dve.tensor_tensor(ovc[0:1, :, :], incl[0:1, :].unsqueeze(1).to_broadcast([1, OVF, E]),
                                       cst[0:1, CCOL["iotam"]:CCOL["iotam"] + OVF].unsqueeze(2).to_broadcast([1, OVF, E]),
                                       ALU.is_le))
            own.link(dve.tensor_reduce(ov[0:1, 0:OVF], ovc[0:1, :, :], AX_X, ALU.add))
            own.link(dve.tensor_scalar(ov[0:1, 0:OVF], ov[0:1, 0:OVF], float(E - 1), None, ALU.min))
            own.link(dve.tensor_copy(ov[0:1, OVF:OVF + 1], incl[0:1, E - 1:E]))
            dve.tensor_copy(ctl[:, :], ov[0:1, :]).then_inc(s_ctl, 1)

            dve.sem_inc(s_hid, 1)
            dve.wait_ge(s_ctl, 1)
            novf = dve.value_load(ctl[0:1, OVF:OVF + 1], min_val=0, max_val=OVF)

            def hidden(n):
                dve.wait_ge(s_th, n + 1)
                own.link(dve.scalar_tensor_tensor(out=th[:, :], in0=th[:, :], scalar=1.0, in1=ps[:, 0, :],
                                                  op0=ALU.add, op1=ALU.mult))
                dve.scalar_tensor_tensor(out=hid[:, :], in0=th[:, :], scalar=0.5, in1=ps[:, 1, :],
                                         op0=ALU.mult, op1=ALU.mult).then_inc(s_hid, 1)

            with dve.Fori(0, E) as e:
                own.enter(e, 1)
                hidden(e)
            own.leave(E)
            with dve.Fori(0, OVF2) as i:
                own.enter(i, 2)
                for b in range(2):
                    with dve.If(novf > 2 * i + b):
                        hidden(2 * i + b + E)
                        dve.nop()
                    with dve.Else():
                        dve.sem_inc(s_dve, 1)
                        own.n = b + 1
            own.leave(OVF2)

            dve.sem_inc(s_ob, 1)
            dve.wait_ge(s_ye, E + 2 * OVF2 + 1)
            dve.wait_ge(s_pw, 48)
            def add_experts(n, b, i):
                col = bass.ds(n, 1)
                dve.wait_ge(s_yg[b], 32 * i + 32)
                dve.scalar_tensor_tensor(out=hs[b][:, :], in0=yg[b][0][:, :], scalar=gate[0][:, col],
                                         in1=h[:, col, :].rearrange("p o d -> p (o d)"), op0=ALU.mult,
                                         op1=ALU.add).then_inc(s_hs, 1)
                dve.wait_ge(s_hs, 2 * n + 1)
                dve.scalar_tensor_tensor(out=hs[b][:, :], in0=yg[b][1][:, :], scalar=gate[1][:, col],
                                         in1=hs[b][:, :], op0=ALU.mult, op1=ALU.add).then_inc(s_hs, 1)
                dve.wait_ge(s_sd3, n + 1)
                own.link(dve.reciprocal(rstd[:, col], std[:, col]))
                dve.tensor_scalar(ns[b][:, :], hs[b][:, :], rstd[:, col], None, ALU.mult).then_inc(s_ns, 1)

            def turned(n):
                dve.wait_ge(s_ntm, n + 1)
                for q in range(2):
                    last = dve.tensor_tensor(nT[:, 4 * q:4 * q + 4, :], ps[:, q, :].rearrange("p (k c) -> p k c", k=4),
                                             V("pleg", 4 * q, 4).unsqueeze(2).to_broadcast([P, 4, P]), ALU.mult)
                last.then_inc(s_nT, 1)

            def finish(n, b, i):
                col = bass.ds(n, 1)
                dve.wait_ge(s_th3, n + 1)
                dve.wait_ge(s_prm, n + 1)
                own.link(dve.scalar_tensor_tensor(out=th2[b][:, :], in0=th2[b][:, :], scalar=1.0, in1=banks(6),
                                                  op0=ALU.add, op1=ALU.mult))
                dve.wait_ge(s_out[b], 16 * i + 16)
                dve.scalar_tensor_tensor(out=ob[b][:, :], in0=th2[b][:, :], scalar=0.5, in1=hs[b][:, :],
                                         op0=ALU.mult, op1=ALU.add).then_inc(s_ob, 1)
                dve.wait_ge(s_sd4, n + 1)
                own.link(dve.reciprocal(rstd2[:, col], std2[:, col]))
                dve.scalar_tensor_tensor(out=ob[b][:, :], in0=ob[b][:, :], scalar=rstd2[:, col], in1=lastg[:, :],
                                         op0=ALU.mult, op1=ALU.mult).then_inc(s_of, 1)

            add_experts(0, 0, 0)
            turned(0)
            with dve.Fori(0, TT // 2 - 1) as i:
                own.enter(i, 6)
                for b in range(2):
                    add_experts(2 * i + b + 1, 1 - b, i + b)
                    turned(2 * i + b + 1)
                    finish(2 * i + b, b, i)
            own.leave(TT // 2 - 1)
            add_experts(TT - 1, 1, TT // 2 - 1)
            turned(TT - 1)
            finish(TT - 2, 0, TT // 2 - 1)
            finish(TT - 1, 1, TT // 2 - 1)


def kernel(**inputs):
    import concourse.bacc as bacc
    from concourse.bass_utils import run_bass_kernel_spmd as run

    a = {k: np.ascontiguousarray(v) for k, v in inputs.items()}
    f = lambda x: np.ascontiguousarray(x)

    def cols(x):
        return x.reshape(-1, P).T

    def padded(x):
        out = np.zeros((P, x.shape[1]), x.dtype)
        out[:x.shape[0]] = x
        return out

    mu = a["rwkv_mu"][0]
    convw = a["conv_w"][0].reshape(TAPS, PAIRS, P).transpose(2, 1, 0).reshape(P, PAIRS * TAPS)
    parts = {"mixg": cols(a["mix_norm"][0]), "mu_r": cols(mu[0:512]), "mu_k": cols(mu[512:1024]),
             "mu_v": cols(mu[1024:1536]), "w0": cols(a["rwkv_w0"][0]), "a0": cols(a["rwkv_a0"][0]),
             "kk": cols(a["rwkv_kk"][0]), "ka": cols(a["rwkv_ka"][0]), "rk": cols(a["rwkv_rk"][0].reshape(-1)),
             "gng": cols(a["rwkv_gn_g"][0]), "gnb": cols(a["rwkv_gn_b"][0]), "convb": cols(a["conv_b"][0]),
             "lng": cols(a["conv_ln_g"][0]), "lnb": cols(a["conv_ln_b"][0]), "convw": convw,
             "mu_wa": padded(mu[1536:1600, None]), "mu_g": padded(mu[1600:1696, None]),
             "pleg": cols(a["ple_norm"][0])}
    vec = f(np.concatenate([parts[n] for n, _ in _cols], axis=1))

    def coltile(w):
        return w.reshape(KT, P, -1).transpose(1, 0, 2).reshape(P, -1)

    w_in = a["w_in"][0]
    z0 = D
    w_conv = f(np.stack([coltile(w_in[:, g * 512 + P * j:g * 512 + P * j + P]) for j in range(4) for g in range(2)]))
    w_rkv = f(np.stack([coltile(w_in[:, z0 + g * 512 + P * j:z0 + g * 512 + P * j + P])
                        for j in range(4) for g in range(3)]))
    arrays = {
        "x": a["x"][0], "cst": constants(), "vec": vec, "w_conv": w_conv, "w_rkv": w_rkv,
        "w_wa": f(coltile(w_in[:, z0 + 1536:z0 + 1600])), "w_g": f(coltile(w_in[:, z0 + 1600:z0 + 1696])),
        "wa2": f(np.concatenate([a["rwkv_w2"][0], a["rwkv_a2"][0]], axis=0).reshape(64, 4, P).transpose(1, 0, 2)),
    }
    arrays |= {
        "g2": a["rwkv_g2"][0], "w_out": a["w_out"][0],
        "rw": f(np.concatenate([a["router_group_w"][0], a["router_expert_w"][0].transpose(1, 0, 2).reshape(D, E)], axis=1)),
        "rb": f(np.concatenate([a["router_group_b"][0], a["router_expert_b"][0].reshape(E)])),
        "ffg": a["ffn_norm"][0], "wg": a["expert_w_gate"][0], "wu": a["expert_w_up"][0], "wd": a["expert_w_down"][0],
        "plew": a["ple_gate_w"][0], "projw": a["ple_proj_w"][0], "lastg": a["final_norm"], "p": a["p"][0, 0],
    }
    nc = bacc.Bacc("TRN2", target_bir_lowering=False, num_devices=1)
    t = {k: nc.dram_tensor("in_" + k, v.shape, mybir.dt.from_np(v.dtype), kind="ExternalInput").ap() for k, v in arrays.items()}
    t["out"] = nc.dram_tensor("out", (T, D), F32, kind="ExternalOutput").ap()
    t["yconv"] = nc.dram_tensor("dr_yconv", (PAIRS, P, T), F32, kind="Internal").ap()
    t["xbuf"] = nc.dram_tensor("dr_xbuf", (NBLK * BLK, D), F32, kind="Internal").ap()
    t["ybuf"] = nc.dram_tensor("dr_ybuf", (NBLK * BLK, D), F32, kind="Internal").ap()
    program(nc, t)
    r = run(nc, [{"in_" + k: v for k, v in arrays.items()}], core_ids=[0])
    return r.results[0]["out"].reshape(1, T, D)
```

```python
from contextlib import ExitStack

import numpy as np
import concourse.bass as bass
from concourse import mybir

F32 = mybir.dt.float32
BF16 = mybir.dt.bfloat16
I32 = mybir.dt.int32
U32 = mybir.dt.uint32
ALU = mybir.AluOpType
ACT = mybir.ActivationFunctionType
AX_X = mybir.AxisListType.X

P = 128
T = 1024
D = 1024
KT = D // P
TT = T // P
HALF = 512
PAIRS = 4
HD = 64
C = 64
NCH = T // C
TAPS = 31
G = 4
EPG = 8
E = G * EPG
FF = 512
BLK = 128
ARENA = 192
OVF = 15
OVF2 = (OVF + 1) // 2
NBLK = E + 2 * OVF2
ZEROS = NBLK + 2 * OVF2
PLE = 256
DECAY = float(np.exp(-0.5)) / 2.0
LEVELS = (2, 4, 8, 16, 32)

_cols = [("mixg", KT), ("mu_r", 4), ("mu_k", 4), ("mu_v", 4), ("w0", 4), ("a0", 4), ("kk", 4), ("ka", 4),
         ("rk", 4), ("gng", 4), ("gnb", 4), ("convb", 4), ("lng", 4), ("lnb", 4), ("convw", 4 * TAPS),
         ("mu_wa", 1), ("mu_g", 1), ("pleg", KT)]
VCOL, _n = {}, 0
for _name, _w in _cols:
    VCOL[_name] = _n
    _n += _w
VEC = _n

_ccols = [("ident", 128), ("istack", 64), ("before", 128), ("ones", 128), ("bones", 128), ("sel2", 2),
          ("selT2", 128), ("strict", 64), ("strict2", 128), ("incl2", 128), ("first2", 128),
          ("levels2", 5 * 128), ("ebase", E), ("prefer4", 4), ("prefer8", 8), ("iotam", OVF)]
CCOL, _n = {}, 0
for _name, _w in _ccols:
    CCOL[_name] = _n
    _n += _w
CST = _n


def constants():
    c = np.zeros((P, CST), np.float32)

    def put(name, a):
        a = np.asarray(a, np.float32)
        c[:a.shape[0], CCOL[name]:CCOL[name] + a.shape[1]] = a

    j = np.arange(P)[:, None] % C
    hj = np.arange(P)[:, None] // C
    t = np.arange(C)[None, :]
    both = lambda m: np.concatenate([m * (hj == 0), m * (hj == 1)], axis=1)
    put("ident", np.eye(P))
    put("istack", j == t)
    put("before", np.arange(P)[:, None] < np.arange(P)[None, :])
    put("ones", np.ones((P, P)))
    put("bones", hj == np.arange(P)[None, :] // C)
    put("sel2", hj == np.arange(2)[None, :])
    c[64:66, CCOL["selT2"]:CCOL["selT2"] + P] = np.arange(2)[:, None] == np.arange(P)[None, :] // C
    put("strict", j < t)
    put("strict2", both(j < t))
    put("incl2", both(j <= t))
    put("first2", both((j // 2 == t // 2) & (j < t)))
    put("levels2", np.concatenate([both((j // (2 * s) == t // (2 * s)) & (j % (2 * s) < s) & (t % (2 * s) >= s))
                                   for s in LEVELS], axis=1))
    put("ebase", np.broadcast_to(BLK * np.arange(E)[None, :], (P, E)))
    put("prefer4", np.broadcast_to(8.0 - np.arange(4)[None, :], (P, 4)))
    put("prefer8", np.broadcast_to(8.0 - np.arange(8)[None, :], (P, 8)))
    put("iotam", np.broadcast_to(np.arange(OVF)[None, :], (P, OVF)))
    return c


class Chain:

    def __init__(self, eng, sem):
        self.eng, self.sem, self.base, self.n = eng, sem, 0, 0

    def link(self, ins, back=0):
        self.n += 1
        ins.then_inc(self.sem, 1)
        self.eng.wait_ge(self.sem, self.base + self.n - back)

    def enter(self, i, per):
        self.outer, self.per = self.base + self.n, per
        self.base, self.n = self.outer + i * per, 0

    def leave(self, count):
        assert self.n == self.per, (self.n, self.per)
        self.base, self.n = self.outer + count * self.per, 0


def program(nc, t):
    with ExitStack() as ctx:
        def sb(name, shape, dt=F32, where=ctx):
            return where.enter_context(nc.sbuf_tensor(name, shape, dt))

        def sem(name):
            return ctx.enter_context(nc.semaphore(name))

        ps = ctx.enter_context(nc.psum_tensor("ps", [P, 8, HALF], F32))

        vec = sb("vec", [P, VEC])
        cst = sb("cst", [P, CST])
        sg_lo = sb("sg_lo", [96, T])

        omu = sb("omu", [P, 3 * PAIRS])
        ndecay = sb("ndecay", [P, 1])
        half = sb("half", [P, 1])
        eps_rms = sb("eps_rms", [P, 1])
        eps_ln = sb("eps_ln", [P, 1])
        eps_gn = sb("eps_gn", [P, 1])
        w0h = sb("w0h", [P, PAIRS])
        a0h = sb("a0h", [P, PAIRS])
        lngh = sb("lngh", [P, PAIRS])
        lnbh = sb("lnbh", [P, PAIRS])
        convwh = sb("convwh", [P, PAIRS * TAPS])

        reset = sb("reset", [P, T], BF16)
        ssq, std, rstd, ssq2, std2, rstd2 = (sb(f"stat{q}", [P, TT]) for q in range(6))
        gate = [sb(f"gate{q}", [P, TT]) for q in range(2)]
        slot = [sb(f"slot{q}", [P, TT], U32) for q in range(2)]
        ctl = sb("ctl", [1, OVF + 1], I32)
        PCH = sb("PCH", [P, NCH, PAIRS])

        def V(name, i=0, n=1, rows=P):
            return vec[0:rows, VCOL[name] + i:VCOL[name] + i + n]

        def VD(name, i):
            return vec[:, bass.ds(i + VCOL[name], 1)]

        def flat(x):
            return x[:, :, :].rearrange("p a c -> p (a c)")

        def flat2(x):
            return x.rearrange("p a b c -> p (a b c)")

        def twice(x):
            return x.unsqueeze(2).to_broadcast([P, PAIRS, 2, C])

        def over_pairs(m):
            return m.unsqueeze(1).to_broadcast([P, PAIRS, C])

        def over_pairs2(m):
            return m.rearrange("p (a c) -> p a c", a=2).unsqueeze(1).to_broadcast([P, PAIRS, 2, C])

        def K(name, n=None, rows=P):
            w = dict(_ccols)[name]
            return cst[0:rows, CCOL[name]:CCOL[name] + (n or w)]

        arena = sb("arena", [P, ARENA * 256])

        class Region:

            def __init__(self, kib):
                self.at = int(kib * 256)

            def take(self, *shape, rows=P):
                n = int(np.prod(shape))
                x = arena[0:rows, self.at:self.at + n]
                self.at += n
                assert self.at <= ARENA * 256
                if len(shape) == 1:
                    return x
                names = "abcde"[:len(shape)]
                return x.rearrange(f"p ({' '.join(names)}) -> p {' '.join(names)}",
                                   **{q: w for q, w in zip(names[1:], shape[1:])})

        m = Region(0)
        pk = m.take(NCH, PAIRS, 5, C)

        xall = Region(0).take(TT, D)
        m = Region(80)
        uT = m.take(KT, T)
        wz = [m.take(KT * P) for s in range(3)]
        wa2 = m.take(P, rows=2 * 32)
        zr, zk, zv = (m.take(T + 1) for _ in range(3))
        zval = m.take(T)
        b_ld = m.take(T)
        b_e1 = m.take(T)
        b_c = m.take(T)
        b_a = m.take(T)
        b_rs = m.take(T)
        b_ks = m.take(T)
        b_t = m.take(T)
        b_kk = m.take(T)
        b_sq = m.take(T)
        lora_nrm = m.take(T)
        lora = lora_nrm[0:64, :]
        nrm = lora_nrm[64:66, :]
        glu = m.take(TAPS - 1 + T)
        yc = m.take(T)
        xn = [zv, zval]

        Yall = pk[:, :, :, 0, :]
        m = Region(80)
        four = lambda *shape: [[m.take(*shape) for b in range(2)] for u in range(2)]
        bdar = four(PAIRS * 2, 2, C)
        bdbkv = [m.take(PAIRS * 3, 2, C) for b in range(2)]
        btk, ktk = four(PAIRS, P), four(PAIRS, P)
        vtk = four(PAIRS, HD)
        aak, arb, ark = four(PAIRS, 2, C), four(PAIRS, 2, C), four(PAIRS, 2, C)
        TiT2 = four(PAIRS, 2, C)
        LT = [m.take(PAIRS, C) for b in range(2)]
        Loff = [[m.take(PAIRS, 2, C) for q in range(2)] for b in range(2)]
        Ti, Xc = ([m.take(PAIRS, C) for b in range(2)] for _ in range(2))
        X2 = [m.take(PAIRS, 2, C) for b in range(2)]
        R, U, S0, S1, Stmp = (m.take(PAIRS, HD) for _ in range(5))
        S = [S0, S1]
        zero = m.take(D)

        m = Region(96)
        yconv = m.take(PAIRS, T)
        yT = m.take(PAIRS, T)
        wout = m.take(KT, D)
        Yc, ysq, bonus = ([m.take(T) for q in range(2)] for _ in range(3))
        b1 = m.take(T)
        g2s = m.take(PAIRS * P, rows=96)
        bonesrk = [m.take(P) for q in range(2)]
        gst = m.take(2, 4, NCH)
        m = Region(80)
        Ybd = [m.take(NCH, 2, C) for q in range(2)]
        m = Region(128)
        squares = [m.take(T) for j in range(PAIRS)]
        lnstd = m.take(T)

        m = Region(0)
        h = m.take(TT, D)
        u2 = m.take(TT, D)
        yTs = [m.take(KT, P) for b in range(2)]
        xo = [m.take(D) for b in range(2)]
        u2s = [m.take(D) for b in range(2)]
        u2T = m.take(KT, P)
        fgain = m.take(D)
        m = Region(160)
        rw = m.take(KT, G + E)
        rbias = m.take(G + E)
        osq = m.take(D)
        lg = m.take(TT, G + E)
        r_a = m.take(TT, E)
        r_b = m.take(TT, E)
        O1, O2, Os, slotm, rank, tbase = (m.take(TT, E) for _ in range(6))
        og, gl1, gl2 = (m.take(TT, G) for _ in range(3))
        esel, e2nd, o1, o2, ew = (m.take(TT, EPG) for _ in range(5))
        gmax, gtop, gsum, gp, m1, m2, dm = (m.take(TT) for _ in range(7))
        cnt, nb, incl, excl = (m.take(E) for _ in range(4))
        ovc = m.take(OVF, E)
        ov = m.take(OVF + 1)

        m = Region(32)
        xb = [m.take(D) for b in range(2)]
        xTs = m.take(KT, P)
        th = m.take(FF)
        hid = m.take(FF)
        hTs = m.take(FF // P, P)
        ys = [m.take(D) for b in range(2)]
        m = Region(96)
        wd1, wd0 = m.take(FF // P, D), m.take(FF // P, D)
        wg0, wu0 = m.take(KT, FF), m.take(KT, FF)
        wg1, wu1 = m.take(KT, FF), m.take(KT, FF)
        wg, wu, wd = (wg0, wg1), (wu0, wu1), (wd0, wd1)

        m = Region(64)
        plew = m.take(KT, D)
        m = Region(96)
        projw = m.take(PLE // P, D)
        yg = [[m.take(D) for k in range(2)] for b in range(2)]
        hs, ns, ob, oq, th2 = ([m.take(D) for b in range(2)] for _ in range(5))
        nT = m.take(KT, P)
        pin = [m.take(PLE) for b in range(2)]
        pT = m.take(PLE // P, P)
        lastg = m.take(D)

        consts_loaded = sem("consts_loaded")
        x_loaded = [sem(f"x_loaded{q}") for q in range(TT // 2)]
        x_rms_ready = sem("x_rms_ready")
        x_scaled = sem("x_scaled")
        x_turned = sem("x_turned")
        u_ready = sem("u_ready")
        w_loaded = [sem(f"w_loaded{s}") for s in range(3)]
        z_product = [sem(f"z_product{s}") for s in range(3)]
        z_evacuated = [sem(f"z_evacuated{s}") for s in range(3)]
        wa2_loaded = sem("wa2_loaded")
        lora_ready = sem("lora_ready")
        gate_low_ready = sem("gate_low_ready")
        decay_product = sem("decay_product")
        decay_ready = sem("decay_ready")
        a_product = sem("a_product")
        a_ready = sem("a_ready")
        decay_sums = sem("decay_sums")
        exps_ready = sem("exps_ready")
        k_shifted = sem("k_shifted")
        kk_squared = sem("kk_squared")
        norm_sums = sem("norm_sums")
        norms_ready = sem("norms_ready")
        norms_inverted = sem("norms_inverted")
        norms_spread = sem("norms_spread")
        kk_ready = sem("kk_ready")
        pair_packed = sem("pair_packed")
        conv_done = sem("conv_done")
        conv_stored = sem("conv_stored")
        vectors_ready = sem("vectors_ready")
        dve_steps = sem("dve_steps")
        act_steps = sem("act_steps")
        pool_steps = sem("pool_steps")
        bd_zeroed = sem("bd_zeroed")
        bd_ready = [sem(f"bd_ready{b}") for b in range(2)]
        gram_products = [sem(f"gram_products{b}") for b in range(2)]
        turned_products = [sem(f"turned_products{b}") for b in range(2)]
        masked = [sem(f"masked{b}") for b in range(2)]
        token_major_ready = [sem(f"token_major_ready{b}") for b in range(2)]
        loff_ready = [sem(f"loff_ready{b}") for b in range(2)]
        xc_ready = [sem(f"xc_ready{b}") for b in range(2)]
        x_product = [sem(f"x_product{b}") for b in range(2)]
        x2_ready = [sem(f"x2_ready{b}") for b in range(2)]
        t_products = [sem(f"t_products{b}") for b in range(2)]
        ti_ready = [sem(f"ti_ready{b}") for b in range(2)]
        tit_ready = [sem(f"tit_ready{b}") for b in range(2)]
        scan_products = sem("scan_products")
        ru_ready = sem("ru_ready")
        state_ready = sem("state_ready")
        y_ready = sem("y_ready")
        tit_started = [sem(f"tit_started{b}") for b in range(2)]

        zeros_ready = sem("zeros_ready")
        zeros_stored = sem("zeros_stored")
        conv_loaded = sem("conv_loaded")
        wout_loaded = sem("wout_loaded")
        g2_loaded = sem("g2_loaded")
        ln_sums = sem("ln_sums")
        ln_centred = sem("ln_centred")
        ln_squared = sem("ln_squared")
        ln_square_sums = sem("ln_square_sums")
        ln_std_ready = sem("ln_std_ready")
        ln_normed = sem("ln_normed")
        ln_act_steps = sem("ln_act_steps")
        conv_half_ready = sem("conv_half_ready")
        gn_centred = sem("gn_centred")
        gn_squared = sem("gn_squared")
        bonus_ready = sem("bonus_ready")
        gn_vars = sem("gn_vars")
        gn_std_ready = sem("gn_std_ready")
        ybd_ready = sem("ybd_ready")
        heads_product = sem("heads_product")
        bonus_product = sem("bonus_product")
        gate_product = sem("gate_product")
        heads_half_ready = sem("heads_half_ready")
        xo_loaded = [sem(f"xo_loaded{b}") for b in range(2)]
        router_loaded = sem("router_loaded")
        y_tile_ready = sem("y_tile_ready")
        out_product_done = sem("out_product_done")
        h_ready = sem("h_ready")
        h_rms_ready = sem("h_rms_ready")
        u2_ready = sem("u2_ready")
        u2_kept = sem("u2_kept")
        u2_turned_psum = sem("u2_turned_psum")
        u2T_ready = sem("u2T_ready")
        logit_product = sem("logit_product")
        logits_ready = sem("logits_ready")
        route_steps = sem("route_steps")
        route_exps = sem("route_exps")
        count_products = sem("count_products")
        slots_ready = sem("slots_ready")
        ctl_ready = sem("ctl_ready")
        rows_scattered = sem("rows_scattered")
        wg_loaded, wu_loaded, wd_loaded, rows_loaded = ([sem(q + str(b)) for b in range(2)] for q in ("wg_loaded", "wu_loaded", "wd_loaded", "rows_loaded"))
        rows_turned_psum = sem("rows_turned_psum")
        xTs_ready = sem("xTs_ready")
        gate_up_product = sem("gate_up_product")
        tanh_ready = sem("tanh_ready")
        hidden_ready = sem("hidden_ready")
        hidden_turned_psum = sem("hidden_turned_psum")
        hTs_ready = sem("hTs_ready")
        down_product = sem("down_product")
        rows_evacuated = sem("rows_evacuated")
        rows_stored = [sem(f"rows_stored{b}") for b in range(2)]
        ple_loaded = sem("ple_loaded")
        rows_gathered = [sem(f"rows_gathered{b}") for b in range(2)]
        p_loaded = [sem(f"p_loaded{b}") for b in range(2)]
        hs_ready = sem("hs_ready")
        hs_rms_ready = sem("hs_rms_ready")
        ns_ready = sem("ns_ready")
        ns_turned = sem("ns_turned")
        nT_ready = sem("nT_ready")
        ple_gate_product = sem("ple_gate_product")
        p_turned = sem("p_turned")
        pT_ready = sem("pT_ready")
        p_product = sem("p_product")
        ple_tanh_ready = sem("ple_tanh_ready")
        sum_ready = sem("sum_ready")
        sum_rms_ready = sem("sum_rms_ready")
        out_rows_ready = sem("out_rows_ready")
        out_stored = [sem(f"out_stored{b}") for b in range(2)]

        NL = len(LEVELS)
        block = ctx.enter_context(nc.Block())

        @block.sync
        def _(sp):
            sp.sem_inc(conv_stored, 16)
            sp.dma_start(cst[:, :], t["cst"]).then_inc(consts_loaded, 16)
            sp.dma_start(vec[:, :], t["vec"]).then_inc(consts_loaded, 16)
            xv = t["x"].rearrange("(t p) d -> t p d", p=P)
            for q in range(TT // 2):
                sp.dma_start(xall[:, 2 * q:2 * q + 2, :], t["x"][256 * q:256 * q + 256, :].rearrange(
                    "(t p) d -> p t d", p=P)).then_inc(x_loaded[q], 16)
            sp.dma_start(wz[0][:, 0:KT * 64], t["w_wa"]).then_inc(w_loaded[0], 16)
            sp.dma_start(wz[1][:, 0:KT * 96], t["w_g"]).then_inc(w_loaded[1], 16)
            sp.dma_start(wz[2][:, :], t["w_rkv"][2]).then_inc(w_loaded[2], 16)
            sp.dma_start(wa2[:, :], t["wa2"][0]).then_inc(wa2_loaded, 16)
            for s in range(2):
                sp.wait_ge(z_product[s], 1)
                sp.dma_start(wz[s][:, :], t["w_conv"][s]).then_inc(w_loaded[s], 16)
            with sp.Fori(0, PAIRS - 1) as j:
                for s in range(2):
                    sp.wait_ge(z_product[s], 2 * j + 2)
                    sp.dma_start(wz[s][:, :], t["w_rkv"][3 * j + s]).then_inc(w_loaded[s], 16)
                sp.wait_ge(z_product[0], 2 * j + 3)
                sp.dma_start(wz[0][:, :], t["w_conv"][2 * j + 2]).then_inc(w_loaded[0], 16)
                sp.wait_ge(a_product, j + 1)
                sp.dma_start(wa2[:, :], t["wa2"][j + 1]).then_inc(wa2_loaded, 16)
                sp.wait_ge(z_product[1], 2 * j + 3)
                sp.dma_start(wz[1][:, :], t["w_conv"][2 * j + 3]).then_inc(w_loaded[1], 16)
                sp.wait_ge(z_product[2], j + 2)
                sp.dma_start(wz[2][:, :], t["w_rkv"][3 * j + 5]).then_inc(w_loaded[2], 16)
                sp.wait_ge(conv_done, j + 1)
                sp.dma_start(t["yconv"][j], yc[:, :]).then_inc(conv_stored, 16)
            for s in range(2):
                sp.wait_ge(z_product[s], 2 * PAIRS)
                sp.dma_start(wz[s][:, :], t["w_rkv"][3 * (PAIRS - 1) + s]).then_inc(w_loaded[s], 16)
            sp.wait_ge(conv_done, PAIRS)
            sp.dma_start(t["yconv"][PAIRS - 1], yc[:, :]).then_inc(conv_stored, 16)
            sp.wait_ge(conv_stored, 16 * (PAIRS + 1))
            sp.wait_ge(zeros_ready, 1)
            with sp.Fori(0, NBLK) as n:
                sp.dma_start(t["xbuf"][bass.ds(n * BLK, BLK), :], zero[:, :]).then_inc(zeros_stored, 16)
            with sp.Fori(E, NBLK) as n:
                sp.dma_start(t["ybuf"][bass.ds(n * BLK, BLK), :], zero[:, :]).then_inc(zeros_stored, 16)
            sp.wait_ge(zeros_stored, 16 * ZEROS)
            sp.wait_ge(y_ready, NCH + 2)
            sp.wait_ge(state_ready, NCH + 1)
            sp.dma_start(g2s[:, :], t["g2"]).then_inc(g2_loaded, 16)
            for j in range(PAIRS):
                sp.dma_start(yconv[:, j, :], t["yconv"][j]).then_inc(conv_loaded, 16)
            sp.wait_ge(conv_half_ready, PAIRS)
            sp.dma_start(wout[:, :, :], t["w_out"].rearrange("(k p) d -> p k d", p=P)).then_inc(wout_loaded, 16)
            sp.wait_ge(heads_half_ready, PAIRS)
            for b in range(2):
                sp.dma_start(xo[b][:, :], xv[b]).then_inc(xo_loaded[b], 16)
            sp.dma_start(rw[:, :, :], t["rw"].rearrange("(k p) n -> p k n", p=P)).then_inc(router_loaded, 16)
            sp.dma_start(rbias[:, :], t["rb"].partition_broadcast(P)).then_inc(router_loaded, 16)
            sp.dma_start(fgain[:, :], t["ffg"].partition_broadcast(P)).then_inc(router_loaded, 16)
            with sp.Fori(1, TT // 2) as i:
                for b in range(2):
                    sp.wait_ge(h_ready, 2 * i + b + 1)
                    sp.dma_start(xo[b][:, :], xv[2 * i + b]).then_inc(xo_loaded[b], 16)

            def gate_up_weights(b, e):
                sp.dma_start(wg[b][:, :, :], t["wg"][e].rearrange("(k p) f -> p k f", p=P)).then_inc(wg_loaded[b], 16)
                sp.dma_start(wu[b][:, :, :], t["wu"][e].rearrange("(k p) f -> p k f", p=P)).then_inc(wu_loaded[b], 16)

            def down_weights(b, e):
                sp.dma_start(wd[b][:, :, :], t["wd"][e].rearrange("(k p) d -> p k d", p=P)).then_inc(wd_loaded[b], 16)

            def block_rows(b, n):
                sp.dma_start(xb[b][:, :], t["xbuf"][bass.ds(n * BLK, BLK), :]).then_inc(rows_loaded[b], 16)

            sp.wait_ge(out_product_done, TT + 2)
            gate_up_weights(0, 0)
            down_weights(0, 0)
            sp.wait_ge(slots_ready, 2)
            sp.wait_ge(ctl_ready, 1)
            sp.wait_ge(rows_scattered, 16 * 2 * TT)
            block_rows(0, 0)
            block_rows(1, 1)
            gate_up_weights(1, 1)
            down_weights(1, 1)
            sp.dma_start(plew[:, :, :], t["plew"].rearrange("(k p) d -> p k d", p=P)).then_inc(ple_loaded, 16)
            with sp.Fori(0, E // 2 - 1) as i:
                for b in range(2):
                    e = 2 * i + b
                    sp.wait_ge(rows_turned_psum, e + 1)
                    block_rows(b, e + 2)
                    sp.wait_ge(gate_up_product, e + 1)
                    gate_up_weights(b, e + 2)
                    sp.wait_ge(down_product, e + 1)
                    down_weights(b, e + 2)
            novf = sp.value_load(ctl[0:1, OVF:OVF + 1], min_val=0, max_val=OVF)
            with sp.Fori(0, OVF2) as i:
                for b in range(2):
                    n = 2 * i + b
                    with sp.If(novf > n):
                        e = sp.value_load(ctl[0:1, bass.ds(n, 1)], min_val=0, max_val=E - 1)
                        row = bass.ds(e, 1)
                        sp.wait_ge(rows_turned_psum, n + E - 1)
                        block_rows(b, n + E)
                        sp.wait_ge(gate_up_product, n + E - 1)
                        sp.dma_start(wg[b][:, :, :], t["wg"][row].rearrange("o (k p) f -> p (o k) f", p=P))\
                            .then_inc(wg_loaded[b], 16)
                        sp.dma_start(wu[b][:, :, :], t["wu"][row].rearrange("o (k p) f -> p (o k) f", p=P))\
                            .then_inc(wu_loaded[b], 16)
                        sp.wait_ge(down_product, n + E - 1)
                        sp.dma_start(wd[b][:, :, :], t["wd"][row].rearrange("o (k p) d -> p (o k) d", p=P))\
                            .then_inc(wd_loaded[b], 16)
                        sp.nop()
                    with sp.Else():
                        sp.nop()
            sp.wait_ge(down_product, E + 2 * OVF2)
            sp.dma_start(projw[:, :, :], t["projw"].rearrange("(k p) d -> p k d", p=P)).then_inc(ple_loaded, 16)
            sp.dma_start(lastg[:, :], t["lastg"].partition_broadcast(P)).then_inc(ple_loaded, 16)
            pv = t["p"].rearrange("(t p) d -> t p d", p=P)
            for b in range(2):
                sp.dma_start(pin[b][:, :], pv[b]).then_inc(p_loaded[b], 16)
            with sp.Fori(1, TT // 2) as i:
                for b in range(2):
                    sp.wait_ge(p_turned, 2 * i + b - 1)
                    sp.dma_start(pin[b][:, :], pv[2 * i + b]).then_inc(p_loaded[b], 16)
            for b in range(2):
                sp.wait_ge(out_stored[b], 16 * (TT // 2 + 1))

        @block.tensor
        def _(pe):
            pe.sem_inc(z_product[2], 1)
            pe.wait_ge(consts_loaded, 32)
            ident = K("ident")
            with pe.Fori(0, TT // 2) as i:
                for b in range(2):
                    pe.wait_ge(x_scaled, 2 * i + b + 1)
                    pe.wait_ge(u_ready, 2 * i + b + 1)
                    for k in range(KT):
                        last = pe.transpose(ps[:, 2 * b + k // 4, (k % 4) * P:(k % 4 + 1) * P],
                                            xn[b][:, k * P:(k + 1) * P], ident)
                    last.then_inc(x_turned, 1)
            pe.wait_ge(u_ready, TT + 2)

            def z_tile(s, n, cols=P):
                pe.wait_ge(w_loaded[s], 16 * (n + 1) if s < 2 else 16 * n)
                if not (isinstance(n, int) and n == 0):
                    pe.wait_ge(z_evacuated[s], n)
                for h in range(2):
                    for k in range(KT):
                        last = pe.matmul(ps[0:cols, 2 * s + h, :], wz[s][:, k * cols:(k + 1) * cols],
                                         uT[:, k, h * HALF:(h + 1) * HALF], start=(k == 0), stop=(k == KT - 1))
                last.then_inc(z_product[s], 1)

            z_tile(0, 0, 64)
            z_tile(1, 0, 96)
            pe.wait_ge(lora_ready, 2)

            def pair(j, more):
                pe.wait_ge(wa2_loaded, 16 * j + 16)
                pe.wait_ge(kk_ready, j + 1)
                for h in range(2):
                    last = pe.matmul(ps[:, 6 + h, :], wa2[0:32, :], lora[0:32, h * HALF:(h + 1) * HALF],
                                     start=True, stop=True)
                last.then_inc(decay_product, 1)
                z_tile(0, 2 * j + 2)
                pe.wait_ge(decay_ready, j + 1)
                for h in range(2):
                    last = pe.matmul(ps[:, 6 + h, :], wa2[32:64, :], lora[32:64, h * HALF:(h + 1) * HALF],
                                     start=True, stop=True)
                last.then_inc(a_product, 1)
                z_tile(1, 2 * j + 2)
                z_tile(2, j + 1)
                if more:
                    z_tile(0, 2 * j + 3)
                pe.wait_ge(kk_squared, j + 1)
                pe.wait_ge(a_ready, j + 1)
                for h in range(2):
                    last = pe.matmul(ps[64:66, 6 + h, :], K("sel2"), b_sq[:, h * HALF:(h + 1) * HALF],
                                     start=True, stop=True)
                last.then_inc(norm_sums, 1)
                if more:
                    z_tile(1, 2 * j + 3)
                pe.wait_ge(norms_inverted, j + 1)
                for h in range(2):
                    last = pe.matmul(ps[:, 6 + h, :], cst[64:66, CCOL["selT2"]:CCOL["selT2"] + P],
                                     nrm[:, h * HALF:(h + 1) * HALF], start=True, stop=True)
                last.then_inc(norms_spread, 1)

            z_tile(0, 1)
            z_tile(1, 1)
            with pe.Fori(0, PAIRS - 1) as j:
                pair(j, True)
            pair(PAIRS - 1, False)

            pe.wait_ge(pair_packed, PAIRS + 1)
            pe.wait_ge(z_evacuated[1], 2 * PAIRS + 1)
            pe.wait_ge(z_evacuated[0], 2 * PAIRS + 1)

            def bank(b, q, w):
                return ps[:, 3 * b + q, 0:PAIRS * w].rearrange("p (a w) -> p a w", a=PAIRS)

            scan6 = ps[:, 6, 0:PAIRS * HD].rearrange("p (a w) -> p a w", a=PAIRS)
            scan6u = ps[:, 6, 256:512].rearrange("p (a w) -> p a w", a=PAIRS)
            scan7 = ps[:, 7, 0:PAIRS * HD].rearrange("p (a w) -> p a w", a=PAIRS)

            def two(x, p):
                return x[:, p, :, :].rearrange("p a c -> p (a c)")

            def scan_r(i, u, b):
                c = 2 * i + b
                pe.wait_ge(tit_ready[b], NL * i + NL)
                pe.wait_ge(y_ready, c + 2)
                pe.wait_ge(state_ready, c + 1)
                for p in range(PAIRS):
                    pe.matmul(scan6[:, p, :], two(bdar[u][b], 2 * p), S[b][:, p, :], start=True, stop=False)
                    last = pe.matmul(scan6[:, p, :], two(aak[u][b], p), vtk[u][b][:, p, :], start=False, stop=True)
                last.then_inc(scan_products, 1)

            def scan_u(i, u, b):
                pe.wait_ge(ru_ready, 4 * i + 2 * b + 1)
                for p in range(PAIRS):
                    last = pe.matmul(scan6u[:, p, :], two(TiT2[u][b], p), R[:, p, :], start=True, stop=True)
                last.then_inc(scan_products, 1)

            def scan_sy(i, u, b):
                pe.wait_ge(ru_ready, 4 * i + 2 * b + 2)
                for p in range(PAIRS):
                    pe.matmul(scan7[:, p, :], btk[u][b][:, p, :], U[:, p, :], start=True, stop=False)
                    last = pe.matmul(scan7[:, p, :], ktk[u][b][:, p, :], vtk[u][b][:, p, :], start=False, stop=True)
                last.then_inc(scan_products, 1)
                for p in range(PAIRS):
                    pe.matmul(scan6[:, p, :], two(bdar[u][b], 2 * p + 1), S[b][:, p, :], start=True, stop=False)
                    pe.matmul(scan6[:, p, :], two(arb[u][b], p), U[:, p, :], start=False, stop=False)
                    last = pe.matmul(scan6[:, p, :], two(ark[u][b], p), vtk[u][b][:, p, :], start=False, stop=True)
                last.then_inc(scan_products, 1)

            def prepare(i, u, scan):
                def step(f, b):
                    if scan:
                        f(i - 1, 1 - u, b)

                for b in range(2):
                    ar = [pk[:, bass.ds(2 * i + b, 1), p, 0:2, :].rearrange("p o a c -> p (o a c)") for p in range(PAIRS)]
                    pe.wait_ge(bd_ready[b], i + 1)
                    for p in range(PAIRS):
                        last = pe.matmul(bank(b, 0, P)[:, p, :], two(bdbkv[b], 3 * p), ar[p], start=True, stop=True)
                    last.then_inc(gram_products[b], 1)
                    for p in range(PAIRS):
                        last = pe.matmul(bank(b, 1, P)[:, p, :], two(bdbkv[b], 3 * p + 1), ar[p], start=True, stop=True)
                    last.then_inc(gram_products[b], 1)
                    if scan:
                        pe.wait_ge(tit_ready[b], NL * i)
                    for p in range(PAIRS):
                        last = pe.transpose(bank(b, 2, P)[:, p, :], two(bdbkv[b], 3 * p), ident)
                    last.then_inc(turned_products[b], 1)
                step(scan_r, 0)
                for b in range(2):
                    pe.wait_ge(masked[b], 3 * i + 2)
                    for p in range(PAIRS):
                        last = pe.transpose(bank(b, 0, P)[:, p, :], two(bdbkv[b], 3 * p + 1), ident)
                    last.then_inc(turned_products[b], 1)
                    pe.wait_ge(masked[b], 3 * i + 3)
                    for p in range(PAIRS):
                        last = pe.matmul(bank(b, 1, HD)[:, p, :], two(bdbkv[b], 3 * p + 2), K("istack"),
                                         start=True, stop=True)
                    last.then_inc(turned_products[b], 1)
                for b in range(2):
                    pe.wait_ge(token_major_ready[b], 3 * i + 1)
                    pe.wait_ge(tit_started[b], i + 1)
                    for p in range(PAIRS):
                        last = pe.matmul(bank(b, 2, C)[:, p, :], two(TiT2[u][b], p), K("istack"), start=True, stop=True)
                    last.then_inc(t_products[b], 1)
                step(scan_u, 0)
                for lv in range(NL):
                    for b in range(2):
                        pe.wait_ge(loff_ready[b], NL * i + lv + 1)
                        pe.wait_ge(ti_ready[b], NL * i + lv + 1)
                        if lv == 0:
                            pe.wait_ge(token_major_ready[b], 3 * i + 3)
                        for p in range(PAIRS):
                            last = pe.matmul(bank(b, 0, C)[:, p, :], two(Loff[b][lv % 2], p), Ti[b][:, p, :],
                                             start=True, stop=True)
                        last.then_inc(x_product[b], 1)
                    if lv < 3:
                        step((scan_sy, scan_r, scan_sy)[lv], (0, 1, 1)[lv])
                    for b in range(2):
                        if lv > 0:
                            pe.wait_ge(tit_ready[b], NL * i + lv)
                        if lv < NL - 1:
                            pe.wait_ge(xc_ready[b], (NL - 1) * i + lv + 1)
                            for p in range(PAIRS):
                                last = pe.matmul(bank(b, 1, C)[:, p, :], two(TiT2[u][b], p), Xc[b][:, p, :],
                                                 start=True, stop=True)
                            last.then_inc(t_products[b], 1)
                        pe.wait_ge(x2_ready[b], NL * i + lv + 1)
                        for p in range(PAIRS):
                            last = pe.matmul(bank(b, 2, P)[:, p, :], two(X2[b], p), two(TiT2[u][b], p),
                                             start=True, stop=True)
                        last.then_inc(t_products[b], 1)
                    if lv == 1:
                        step(scan_u, 1)

            pe.wait_ge(state_ready, 1)
            prepare(0, 0, False)
            with pe.Fori(0, NCH // 4 - 1) as i:
                prepare(2 * i + 1, 1, True)
                prepare(2 * i + 2, 0, True)
            prepare(NCH // 2 - 1, 1, True)
            for b in range(2):
                for f in (scan_r, scan_u, scan_sy):
                    f(NCH // 2 - 1, 1, b)

            def bonus_and_gate(p):
                pe.wait_ge(bonus_ready, p + 1)
                if p > 0:
                    pe.wait_ge(heads_half_ready, p)
                for h2 in range(2):
                    last = pe.matmul(ps[:, 2 + h2, :], bonesrk[p % 2][:, :],
                                     bonus[p % 2][:, h2 * HALF:(h2 + 1) * HALF], start=True, stop=True)
                last.then_inc(bonus_product, 1)
                for h2 in range(2):
                    last = pe.matmul(ps[:, 4 + h2, :], g2s[:, p * P:(p + 1) * P], sg_lo[:, h2 * HALF:(h2 + 1) * HALF],
                                     start=True, stop=True)
                last.then_inc(gate_product, 1)

            def heads_turned(p):
                pe.wait_ge(ybd_ready, p + 1)
                for n in range(NCH):
                    last = pe.matmul(ps[:, n // 8, (n % 8) * C:(n % 8 + 1) * C],
                                     Ybd[p % 2][:, n, :, :].rearrange("p a c -> p (a c)"), K("istack"),
                                     start=True, stop=True)
                last.then_inc(heads_product, 1)

            def conv_sums(x, ready, done):
                for h2 in range(2):
                    for j in range(PAIRS):
                        if ready:
                            pe.wait_ge(ready, j + 1)
                        last = pe.matmul(ps[:, 6 + h2, :], K("ones"), x(j)[:, h2 * HALF:(h2 + 1) * HALF],
                                         start=(j == 0), stop=(j == PAIRS - 1))
                last.then_inc(done, 1)

            pe.wait_ge(y_ready, NCH + 2)
            pe.wait_ge(state_ready, NCH + 1)
            pe.wait_ge(gate_low_ready, 3)
            pe.wait_ge(g2_loaded, 16)
            bonus_and_gate(0)
            pe.wait_ge(conv_loaded, 16 * PAIRS)
            conv_sums(lambda j: yconv[:, j, :], None, ln_sums)
            pe.wait_ge(ln_centred, PAIRS)
            conv_sums(lambda j: squares[j], ln_squared, ln_square_sums)
            heads_turned(0)
            for p in range(1, PAIRS):
                bonus_and_gate(p)
                heads_turned(p)

            pe.sem_inc(out_product_done, 2)
            pe.wait_ge(wout_loaded, 16)
            pe.wait_ge(heads_half_ready, PAIRS)

            def out_product(n, b):
                pe.wait_ge(y_tile_ready, n + 1)
                pe.wait_ge(h_ready, n + 1)
                for h2 in range(2):
                    for k in range(KT):
                        last = pe.matmul(ps[:, 2 * b + h2, :], yTs[b][:, k, :], wout[:, k, h2 * HALF:(h2 + 1) * HALF],
                                         start=(k == 0), stop=(k == KT - 1))
                last.then_inc(out_product_done, 1)

            def logits(n, b):
                pe.wait_ge(u2_ready, n + 1)
                pe.wait_ge(u2T_ready, n + 1)
                for k in range(KT):
                    last = pe.transpose(ps[:, 4 + k // 4, (k % 4) * P:(k % 4 + 1) * P], u2s[b][:, k * P:(k + 1) * P],
                                        ident)
                last.then_inc(u2_turned_psum, 1)
                pe.wait_ge(u2T_ready, n + 2)
                pe.wait_ge(logits_ready, n + 1)
                for k in range(KT):
                    last = pe.matmul(ps[:, 6, 0:G + E], u2T[:, k, :], rw[:, k, :], start=(k == 0), stop=(k == KT - 1))
                last.then_inc(logit_product, 1)

            out_product(0, 0)
            pe.wait_ge(router_loaded, 48)
            with pe.Fori(0, TT // 2 - 1) as i:
                for b in range(2):
                    out_product(2 * i + b + 1, 1 - b)
                    logits(2 * i + b, b)
            out_product(TT - 1, 1)
            logits(TT - 2, 0)
            logits(TT - 1, 1)
            pe.wait_ge(route_steps, 3)
            pe.matmul(ps[:, 0, 0:TT * E], K("before"), flat(Os), start=True, stop=True)
            pe.matmul(ps[:, 1, 0:TT * E], K("ones"), flat(Os), start=True, stop=True).then_inc(count_products, 1)

            def turn_rows(n, b, q):
                pe.wait_ge(rows_loaded[b], 16 * q + 16)
                pe.wait_ge(xTs_ready, n + 1)
                for k in range(KT):
                    last = pe.transpose(ps[:, 4 + k // 4, (k % 4) * P:(k % 4 + 1) * P], xb[b][:, k * P:(k + 1) * P], ident)
                last.then_inc(rows_turned_psum, 1)

            def gate_up(n, b, q):
                pe.wait_ge(xTs_ready, n + 2)
                pe.wait_ge(hidden_ready, n + 1)
                for o, (w, sw) in enumerate(((wg, wg_loaded), (wu, wu_loaded))):
                    pe.wait_ge(sw[b], 16 * q + 16)
                    for k in range(KT):
                        last = pe.matmul(ps[:, o, :], xTs[:, k, :], w[b][:, k, :], start=(k == 0), stop=(k == KT - 1))
                last.then_inc(gate_up_product, 1)

            def turn_hidden(n):
                pe.wait_ge(hidden_ready, n + 2)
                for k in range(FF // P):
                    last = pe.transpose(ps[:, 6, k * P:(k + 1) * P], hid[:, k * P:(k + 1) * P], ident)
                last.then_inc(hidden_turned_psum, 1)

            def down(n, b, q):
                pe.wait_ge(hTs_ready, n + 1)
                pe.wait_ge(wd_loaded[b], 16 * q + 16)
                pe.wait_ge(rows_evacuated, n + 1)
                for h2 in range(2):
                    for k in range(FF // P):
                        last = pe.matmul(ps[:, 2 + h2, :], hTs[:, k, :], wd[b][:, k, h2 * HALF:(h2 + 1) * HALF],
                                         start=(k == 0), stop=(k == FF // P - 1))
                last.then_inc(down_product, 1)

            pe.wait_ge(ctl_ready, 1)
            turn_rows(0, 0, 0)
            gate_up(0, 0, 0)
            turn_rows(1, 1, 0)
            with pe.Fori(0, E // 2 - 1) as i:
                for b in range(2):
                    n = 2 * i + b
                    turn_hidden(n)
                    gate_up(n + 1, 1 - b, i + b)
                    turn_rows(n + 2, b, i + 1)
                    down(n, b, i)
            turn_hidden(E - 2)
            gate_up(E - 1, 1, E // 2 - 1)
            down(E - 2, 0, E // 2 - 1)
            turn_hidden(E - 1)
            down(E - 1, 1, E // 2 - 1)
            novf = pe.value_load(ctl[0:1, OVF:OVF + 1], min_val=0, max_val=OVF)
            with pe.Fori(0, OVF2) as i:
                for b in range(2):
                    n = 2 * i + b + E
                    with pe.If(novf > 2 * i + b):
                        turn_rows(n, b, i + E // 2)
                        gate_up(n, b, i + E // 2)
                        turn_hidden(n)
                        down(n, b, i + E // 2)
                        pe.nop()
                    with pe.Else():
                        pe.wait_ge(down_product, n)
                        pe.sem_inc(down_product, 1)

            pe.wait_ge(rows_evacuated, E + 2 * OVF2 + 1)
            pe.wait_ge(ple_loaded, 48)
            def gate_tile(n, b, i):
                pe.wait_ge(ns_ready, n + 1)
                pe.wait_ge(pT_ready, n + 1)
                for k in range(KT):
                    last = pe.transpose(ps[:, k // 4, (k % 4) * P:(k % 4 + 1) * P], ns[b][:, k * P:(k + 1) * P], ident)
                last.then_inc(ns_turned, 1)
                pe.wait_ge(nT_ready, n + 1)
                pe.wait_ge(p_loaded[b], 16 * i + 16)
                for k in range(2):
                    last = pe.transpose(ps[:, 0, k * P:(k + 1) * P], pin[b][:, k * P:(k + 1) * P], ident)
                last.then_inc(p_turned, 1)
                for h2 in range(2):
                    for k in range(KT):
                        last = pe.matmul(ps[:, 2 * b + 2 + h2, :], nT[:, k, :], plew[:, k, h2 * HALF:(h2 + 1) * HALF],
                                         start=(k == 0), stop=(k == KT - 1))
                last.then_inc(ple_gate_product, 1)
                pe.wait_ge(pT_ready, n + 2)
                pe.wait_ge(sum_ready, n + 1)
                for h2 in range(2):
                    for k in range(2):
                        last = pe.matmul(ps[:, 6 + h2, :], pT[:, k, :], projw[:, k, h2 * HALF:(h2 + 1) * HALF],
                                         start=(k == 0), stop=(k == 1))
                last.then_inc(p_product, 1)

            with pe.Fori(0, TT // 2) as i:
                for b in range(2):
                    gate_tile(2 * i + b, b, i)

        @block.scalar
        def _(act):
            act.sem_inc(z_evacuated[2], 1)
            act.sem_inc(y_ready, 2)
            act.wait_ge(consts_loaded, 32)
            act.wait_ge(vectors_ready, 1)
            mine = Chain(act, act_steps)
            for q in range(TT // 2):
                act.wait_ge(x_loaded[q], 16)
                for n in (2 * q, 2 * q + 1):
                    mine.link(act.activation(b_e1[:, :], xall[:, n, :], ACT.Square, accum_out=ssq[:, n:n + 1]))
                if q % 2 == 1:
                    cols = slice(2 * q - 2, 2 * q + 2)
                    act.activation(std[:, cols], ssq[:, cols], ACT.Sqrt, scale=1.0 / D, bias=eps_rms[:, :])\
                        .then_inc(x_rms_ready, 1)

            def evac(s, n, out, func, rows=P, **kw):
                act.wait_ge(z_product[s], n + 1)
                act.activation(out, ps[0:rows, 2 * s:2 * s + 2, :].rearrange("p a c -> p (a c)"), func,
                               **kw).then_inc(z_evacuated[s], 1)

            evac(0, 0, zr[0:64, 1:T + 1], ACT.Copy, 64)
            evac(1, 0, zk[0:96, 1:T + 1], ACT.Copy, 96)
            act.wait_ge(lora_ready, 1)
            act.activation(lora[0:32, :], lora[0:32, :], ACT.Tanh).then_inc(lora_ready, 1)
            act.wait_ge(gate_low_ready, 1)
            act.activation(sg_lo[:, :], sg_lo[:, :], ACT.Tanh, scale=0.5).then_inc(gate_low_ready, 1)
            low = ps[:, 6:8, :].rearrange("p a c -> p (a c)")

            def evac_shift(s, n, z, out, q, j):
                act.wait_ge(z_product[s], n + 1)
                z_ps = ps[:, 2 * s:2 * s + 2, :].rearrange("p a c -> p (a c)")
                act.activation(z[:, 1:T + 1], z_ps, ACT.Copy)
                act.activation(out[:, :], z_ps, ACT.Copy, scale=omu[:, bass.ds(j + q * PAIRS, 1)]).then_inc(z_evacuated[s], 1)

            def pair(j, more):
                act.wait_ge(decay_product, j + 1)
                act.wait_ge(pair_packed, j + 1)
                mine.link(act.activation(b_ld[:, :], low, ACT.Tanh, scale=0.5, bias=w0h[:, bass.ds(j, 1)]))
                act.activation(b_ld[:, :], b_ld[:, :], ACT.Identity, scale=-DECAY, bias=ndecay[:, :]).then_inc(decay_ready, 1)
                evac_shift(0, 2 * j + 2, zr, b_rs, 0, j)
                act.wait_ge(a_product, j + 1)
                mine.link(act.activation(b_a[:, :], low, ACT.Tanh, scale=0.5, bias=a0h[:, bass.ds(j, 1)]))
                act.activation(b_a[:, :], b_a[:, :], ACT.Identity, scale=0.5, bias=half[:, :]).then_inc(a_ready, 1)
                evac_shift(1, 2 * j + 2, zk, b_ks, 1, j)
                evac_shift(2, j + 1, zv, b_t, 2, j)
                act.wait_ge(decay_sums, 2 * j + 1)
                act.activation(b_e1[:, :], b_c[:, :], ACT.Exp)
                act.wait_ge(decay_sums, 2 * j + 2)
                act.activation(b_ld[:, :], b_ld[:, :], ACT.Exp)
                act.activation(b_c[:, :], b_c[:, :], ACT.Exp, scale=-1.0).then_inc(exps_ready, 1)
                act.wait_ge(k_shifted, j + 1)
                act.activation(b_kk[:, :], b_ks[:, :], ACT.Copy, scale=VD("kk", j))
                act.activation(b_sq[:, :], b_ks[:, :], ACT.Square, scale=VD("kk", j)).then_inc(kk_squared, 1)
                if more:
                    evac(0, 2 * j + 3, zval[:, :], ACT.Copy)
                act.wait_ge(norm_sums, j + 1)
                act.activation(nrm[:, :], ps[64:66, 6:8, :].rearrange("p a c -> p (a c)"), ACT.Sqrt).then_inc(norms_ready, 1)
                if more:
                    evac(1, 2 * j + 3, b_sq[:, :], ACT.Tanh, scale=0.5)

            evac(0, 1, zval[:, :], ACT.Copy)
            evac(1, 1, b_sq[:, :], ACT.Tanh, scale=0.5)
            with act.Fori(0, PAIRS - 1) as j:
                mine.enter(j, 2)
                pair(j, True)
            mine.leave(PAIRS - 1)
            pair(PAIRS - 1, False)


            def bank(b, q, w):
                return ps[:, 3 * b + q, 0:PAIRS * w]

            def block_diagonal(i, u):
                for b in range(2):
                    for hd in range(2):
                        rows = slice(64 * hd, 64 * hd + 64)
                        for out, kinds in ((bdar[u][b], slice(0, 2)), (bdbkv[b], slice(2, 5))):
                            src = pk[rows, bass.ds(2 * i + b, 1), :, kinds, :].rearrange("p o a k c -> p (o a) k c")
                            out = out.rearrange("p (a k) h c -> p a k h c", a=PAIRS)
                            last = act.activation(out[rows, :, :, hd, :], src, ACT.Copy)
                    last.then_inc(bd_ready[b], 1)

            def y_out(i, b):
                act.wait_ge(scan_products, 8 * i + 4 * b + 4)
                act.activation(Yall[:, bass.ds(2 * i + b, 1), :, :].rearrange("p o a c -> p (o a) c"),
                               ps[:, 6, 0:PAIRS * HD].rearrange("p (a c) -> p a c", a=PAIRS), ACT.Copy).then_inc(y_ready, 1)

            def prepare(i, u, scan, more):
                for b in range(2):
                    act.wait_ge(turned_products[b], 3 * i + 1)
                    act.activation(flat(btk[u][b]), bank(b, 2, P), ACT.Copy).then_inc(token_major_ready[b], 1)
                for b in range(2):
                    act.wait_ge(turned_products[b], 3 * i + 2)
                    act.activation(flat(ktk[u][b]), bank(b, 0, P), ACT.Copy).then_inc(token_major_ready[b], 1)
                    act.wait_ge(turned_products[b], 3 * i + 3)
                    act.activation(flat(vtk[u][b]), bank(b, 1, HD), ACT.Copy).then_inc(token_major_ready[b], 1)
                for lv in range(NL):
                    for b in range(2):
                        act.wait_ge(x_product[b], NL * i + lv + 1)
                        if lv < NL - 1:
                            act.activation(flat(Xc[b]), bank(b, 0, C), ACT.Copy).then_inc(xc_ready[b], 1)
                        for hd in range(2):
                            rows = slice(64 * hd, 64 * hd + 64)
                            last = act.activation(X2[b][rows, :, hd, :],
                                                  ps[rows, 3 * b, 0:PAIRS * C].rearrange("p (a c) -> p a c", a=PAIRS),
                                                  ACT.Copy)
                        last.then_inc(x2_ready[b], 1)
                    if scan and lv in (1, 3):
                        y_out(i - 1, (lv - 1) // 2)
                    if more and lv == 3:
                        block_diagonal(i + 1, 1 - u)

            act.wait_ge(bd_zeroed, 8)
            block_diagonal(0, 0)
            prepare(0, 0, False, True)
            with act.Fori(0, NCH // 4 - 1) as i:
                prepare(2 * i + 1, 1, True, True)
                prepare(2 * i + 2, 0, True, True)
            prepare(NCH // 2 - 1, 1, True, False)
            for b in range(2):
                y_out(NCH // 2 - 1, b)

            def y_squares(p):
                act.wait_ge(gn_centred, p + 1)
                act.activation(ysq[p % 2][:, :], Yc[p % 2][:, :], ACT.Square).then_inc(gn_squared, 1)

            def y_deviation(p):
                act.wait_ge(gn_vars, p + 1)
                act.activation(gst[:, p % 2, 2, :], gst[:, p % 2, 1, :], ACT.Sqrt, scale=1.0 / HD, bias=eps_gn[:, :])\
                    .then_inc(gn_std_ready, 1)

            y_squares(0)
            for j in range(PAIRS):
                act.wait_ge(ln_centred, j + 1)
                act.activation(squares[j][:, :], yconv[:, j, :], ACT.Square).then_inc(ln_squared, 1)
            y_deviation(0)
            y_squares(1)
            act.wait_ge(ln_square_sums, 1)
            act.activation(lnstd[:, :], low, ACT.Sqrt, scale=1.0 / 512, bias=eps_ln[:, :]).then_inc(ln_std_ready, 1)
            for j in range(PAIRS):
                act.wait_ge(ln_normed, j + 1)
                act.activation(yconv[:, j, :], yconv[:, j, :], ACT.Identity, scale=lngh[:, j:j + 1],
                               bias=lnbh[:, j:j + 1]).then_inc(ln_act_steps, 1)
                act.wait_ge(ln_act_steps, 2 * j + 1)
                act.activation(squares[j][:, :], yconv[:, j, :], ACT.Tanh).then_inc(ln_act_steps, 1)
            for p in range(1, PAIRS):
                y_deviation(p)
                if p + 1 < PAIRS:
                    y_squares(p + 1)

            act.sem_inc(u2T_ready, 1)
            act.wait_ge(heads_half_ready, PAIRS)
            act.wait_ge(conv_half_ready, PAIRS)

            def y_tile(n, b):
                act.wait_ge(out_product_done, n + 1)
                tok = bass.ds(P * n, P)
                act.activation(yTs[b][:, 0:PAIRS, :], yconv[:, :, tok], ACT.Copy)
                act.activation(yTs[b][:, PAIRS:KT, :], yT[:, :, tok], ACT.Copy).then_inc(y_tile_ready, 1)

            def h_norm(n):
                act.wait_ge(h_ready, n + 3)
                mine.link(act.activation(osq[:, :], h[:, bass.ds(n, 1), :].rearrange("p o d -> p (o d)"), ACT.Square,
                                         accum_out=ssq2[:, bass.ds(n, 1)]))
                act.activation(std2[:, bass.ds(n, 1)], ssq2[:, bass.ds(n, 1)], ACT.Sqrt, scale=1.0 / D,
                               bias=eps_rms[:, :]).then_inc(h_rms_ready, 1)

            def u2_turned(n):
                act.wait_ge(u2_turned_psum, n + 1)
                act.activation(flat(u2T), ps[:, 4:6, :].rearrange("p a c -> p (a c)"), ACT.Copy).then_inc(u2T_ready, 1)

            y_tile(0, 0)
            y_tile(1, 1)
            h_norm(0)
            y_tile(2, 0)
            with act.Fori(0, TT // 2 - 2) as i:
                mine.enter(i, 2)
                for b in range(2):
                    n = 2 * i + b + 1
                    u2_turned(n - 1)
                    h_norm(n)
                    y_tile(n + 2, 1 - b)
            mine.leave(TT // 2 - 2)
            u2_turned(TT - 4)
            h_norm(TT - 3)
            y_tile(TT - 1, 1)
            for n in (TT - 2, TT - 1):
                u2_turned(n - 1)
                h_norm(n)
            u2_turned(TT - 1)
            act.wait_ge(route_steps, 1)
            act.activation(flat(gl2), flat(gl2), ACT.Exp).then_inc(route_exps, 1)
            act.wait_ge(route_steps, 2)
            act.activation(dm[:, :], dm[:, :], ACT.Exp).then_inc(route_exps, 1)

            act.sem_inc(xTs_ready, 1)
            act.sem_inc(rows_evacuated, 1)
            for b in range(2):
                act.sem_inc(rows_stored[b], 16)
            act.wait_ge(ctl_ready, 1)

            def rows_turned(n):
                act.wait_ge(rows_turned_psum, n + 1)
                act.activation(flat(xTs), ps[:, 4:6, :].rearrange("p a c -> p (a c)"), ACT.Copy).then_inc(xTs_ready, 1)

            def hidden_tanh(n):
                act.wait_ge(gate_up_product, n + 1)
                act.activation(th[:, :], ps[:, 0, :], ACT.Tanh, scale=0.5).then_inc(tanh_ready, 1)

            def hidden_turned(n):
                act.wait_ge(hidden_turned_psum, n + 1)
                act.activation(flat(hTs), ps[:, 6, :], ACT.Copy).then_inc(hTs_ready, 1)

            def rows_out(n, b, q):
                act.wait_ge(down_product, n + 1)
                act.wait_ge(rows_stored[b], 16 * q + 16)
                act.activation(ys[b][:, :], ps[:, 2:4, :].rearrange("p a c -> p (a c)"), ACT.Copy).then_inc(rows_evacuated, 1)
                act.wait_ge(rows_evacuated, n + 2)
                act.dma_start(t["ybuf"][bass.ds(n * BLK, BLK), :], ys[b][:, :]).then_inc(rows_stored[b], 16)

            rows_turned(0)
            hidden_tanh(0)
            rows_turned(1)
            with act.Fori(0, E // 2 - 1) as i:
                for b in range(2):
                    n = 2 * i + b
                    hidden_turned(n)
                    hidden_tanh(n + 1)
                    rows_turned(n + 2)
                    rows_out(n, b, i)
            hidden_turned(E - 2)
            hidden_tanh(E - 1)
            rows_out(E - 2, 0, E // 2 - 1)
            hidden_turned(E - 1)
            rows_out(E - 1, 1, E // 2 - 1)
            novf = act.value_load(ctl[0:1, OVF:OVF + 1], min_val=0, max_val=OVF)
            with act.Fori(0, OVF2) as i:
                for b in range(2):
                    n = 2 * i + b + E
                    with act.If(novf > 2 * i + b):
                        rows_turned(n)
                        hidden_tanh(n)
                        hidden_turned(n)
                        rows_out(n, b, i + E // 2)
                        act.nop()
                    with act.Else():
                        act.sem_inc(rows_evacuated, 1)
                        act.sem_inc(rows_stored[b], 16)

            act.sem_inc(out_stored[0], 16)
            act.sem_inc(out_stored[1], 16)
            act.sem_inc(pT_ready, 1)
            rows_of_out = t["out"].rearrange("(t p) d -> t p d", p=P)

            def moe_norm(n, b):
                col = bass.ds(n, 1)
                act.wait_ge(hs_ready, 2 * n + 2)
                mine.link(act.activation(oq[b][:, :], hs[b][:, :], ACT.Square, accum_out=ssq[:, col]))
                act.activation(std[:, col], ssq[:, col], ACT.Sqrt, scale=1.0 / D, bias=eps_rms[:, :]).then_inc(hs_rms_ready, 1)

            def embedding_turned(n):
                act.wait_ge(p_turned, n + 1)
                act.activation(flat(pT), ps[:, 0, 0:PLE], ACT.Copy).then_inc(pT_ready, 1)

            def gate_and_out(n, b):
                col = bass.ds(n, 1)
                act.wait_ge(ple_gate_product, n + 1)
                act.activation(th2[b][:, :], ps[:, 2 * b + 2:2 * b + 4, :].rearrange("p a c -> p (a c)"), ACT.Tanh,
                               scale=0.5).then_inc(ple_tanh_ready, 1)
                act.wait_ge(sum_ready, n + 2)
                mine.link(act.activation(oq[b][:, :], ob[b][:, :], ACT.Square, accum_out=ssq2[:, col]))
                act.activation(std2[:, col], ssq2[:, col], ACT.Sqrt, scale=1.0 / D, bias=eps_rms[:, :]).then_inc(sum_rms_ready, 1)
                act.wait_ge(out_rows_ready, n + 1)
                act.dma_start(rows_of_out[n], ob[b][:, :]).then_inc(out_stored[b], 16)

            moe_norm(0, 0)
            with act.Fori(0, TT // 2 - 1) as i:
                mine.enter(i, 4)
                for b in range(2):
                    embedding_turned(2 * i + b)
                    moe_norm(2 * i + b + 1, 1 - b)
                    gate_and_out(2 * i + b, b)
            mine.leave(TT // 2 - 1)
            embedding_turned(TT - 2)
            moe_norm(TT - 1, 1)
            gate_and_out(TT - 2, 0)
            embedding_turned(TT - 1)
            gate_and_out(TT - 1, 1)

        @block.gpsimd
        def _(pool):
            pool.memset(glu[:, 0:TAPS - 1], 0.0).then_inc(pool_steps, 1)
            pool.memset(reset[:, :], 1.0).then_inc(pool_steps, 1)
            pool.wait_ge(pool_steps, 2)
            pool.memset(reset[:, :].rearrange("p (n c) -> p n c", c=C)[:, :, 0:1], 0.0).then_inc(pool_steps, 1)
            pool.wait_ge(pair_packed, PAIRS + 1)
            pool.wait_ge(conv_stored, 16 * (PAIRS + 1))
            for x in bdar[0] + X2 + bdar[1]:
                pool.memset(x, 0.0).then_inc(bd_zeroed, 1)
            pool.memset(zero[:, :], 0.0).then_inc(zeros_ready, 1)
            pool.memset(S[0][:, :, :], 0.0).then_inc(state_ready, 1)
            own = Chain(pool, pool_steps)
            own.n = 3

            def prepare(i, u):
                for b in range(2):
                    pool.wait_ge(masked[b], 3 * i + 1)
                    own.link(pool.tensor_tensor(TiT2[u][b], twice(LT[b][:, :, :]), over_pairs2(K("first2")), ALU.mult))
                    pool.tensor_tensor(TiT2[u][b], TiT2[u][b], over_pairs2(K("ident")), ALU.add).then_inc(tit_started[b], 1)
                for lv in range(NL):
                    for b in range(2):
                        if lv >= 2:
                            pool.wait_ge(x_product[b], NL * i + lv - 1)
                        mask = cst[:, CCOL["levels2"] + lv * P:CCOL["levels2"] + (lv + 1) * P]
                        pool.tensor_tensor(Loff[b][lv % 2][:, :, :, :], twice(LT[b][:, :, :]), over_pairs2(mask),
                                           ALU.mult).then_inc(loff_ready[b], 1)

            with pool.Fori(0, NCH // 4) as i:
                own.enter(i, 4)
                prepare(2 * i, 0)
                prepare(2 * i + 1, 1)
            own.leave(NCH // 4)
            pool.wait_ge(y_ready, NCH + 2)
            pool.wait_ge(state_ready, NCH + 1)
            for q in range(2):
                pool.memset(Ybd[q], 0.0).then_inc(bd_zeroed, 1)

            pool.sem_inc(u2_kept, 2)
            with pool.Fori(0, TT // 2) as i:
                for b in range(2):
                    pool.wait_ge(u2_ready, 2 * i + b + 1)
                    pool.tensor_copy(u2[:, bass.ds(2 * i + b, 1), :].rearrange("p o d -> p (o d)"), u2s[b][:, :])\
                        .then_inc(u2_kept, 1)
            pool.wait_ge(slots_ready, 2)
            pool.wait_ge(zeros_stored, 16 * ZEROS)
            pool.wait_ge(u2_kept, TT + 2)
            for n in range(TT):
                for k in range(2):
                    pool.indirect_dma_start(out=t["xbuf"][:, :], out_offset=bass.IndirectOffsetOnAxis(ap=slot[k][:, n:n + 1], axis=0),
                                            in_=u2[:, n, :], in_offset=None).then_inc(rows_scattered, 16)
            for b in range(2):
                pool.wait_ge(rows_stored[b], 16 * (E // 2 + OVF2 + 1))
            for n in range(TT):
                b = n % 2
                if n >= 2:
                    pool.wait_ge(hs_ready, 2 * (n - 2) + 2)
                for k in range(2):
                    pool.indirect_dma_start(out=yg[b][k][:, :], out_offset=None, in_=t["ybuf"][:, :],
                                            in_offset=bass.IndirectOffsetOnAxis(ap=slot[k][:, n:n + 1], axis=0))\
                        .then_inc(rows_gathered[b], 16)

        @block.vector
        def _(dve):
            own = Chain(dve, dve_steps)
            dve.sem_inc(u_ready, 2)
            dve.sem_inc(kk_ready, 1)
            dve.sem_inc(pair_packed, 1)
            dve.memset(ndecay[:, :], -DECAY)
            dve.memset(half[:, :], 0.5)
            dve.memset(eps_rms[:, :], 1e-6)
            dve.memset(eps_ln[:, :], 1e-5)
            dve.memset(eps_gn[:, :], 64e-5)
            dve.wait_ge(consts_loaded, 32)
            for out, name, n in ((w0h, "w0", 4), (a0h, "a0", 4), (lngh, "lng", 4), (lnbh, "lnb", 4),
                                 (convwh, "convw", PAIRS * TAPS)):
                dve.tensor_scalar(out[:, :], V(name, 0, n), 0.5, None, ALU.mult)
            last = dve.tensor_scalar(omu[:, :], V("mu_r", 0, 3 * PAIRS), -1.0, 1.0, ALU.mult, ALU.add)
            last.then_inc(vectors_ready, 1)
            def scaled(n):
                if n % 4 == 0:
                    dve.wait_ge(x_rms_ready, n // 4 + 1)
                    own.link(dve.reciprocal(rstd[:, n:n + 4], std[:, n:n + 4]))
                dve.tensor_scalar(xn[n % 2][:, 0:D], xall[:, n, :], rstd[:, n:n + 1], None, ALU.mult).then_inc(x_scaled, 1)

            scaled(0)
            scaled(1)
            for n in range(TT):
                dve.wait_ge(x_turned, n + 1)
                for q in range(2):
                    gain = V("mixg", 4 * q, 4).unsqueeze(2).to_broadcast([P, 4, P])
                    last = dve.tensor_tensor(uT[:, 4 * q:4 * q + 4, n * P:(n + 1) * P],
                                             ps[:, 2 * (n % 2) + q, :].rearrange("p (k c) -> p k c", k=4), gain, ALU.mult)
                last.then_inc(u_ready, 1)
                if n + 2 < TT:
                    scaled(n + 2)
            for z in (zr, zk, zv):
                last = dve.memset(z[:, 0:1], 0.0)
            own.link(last)

            def shift(z, out, mu, rows=P):
                own.link(dve.tensor_tensor(out, z[0:rows, 0:T], z[0:rows, 1:T + 1], ALU.subtract))
                return dve.scalar_tensor_tensor(out=out, in0=out, scalar=mu, in1=z[0:rows, 1:T + 1],
                                                op0=ALU.mult, op1=ALU.add)

            dve.wait_ge(z_evacuated[0], 1)
            shift(zr, lora[:, :], V("mu_wa", rows=64), 64).then_inc(lora_ready, 1)
            dve.wait_ge(z_evacuated[1], 1)
            shift(zk, sg_lo[:, :], V("mu_g", rows=96), 96).then_inc(gate_low_ready, 1)
            dve.wait_ge(gate_low_ready, 2)
            dve.tensor_scalar(sg_lo[:, :], sg_lo[:, :], 0.5, 0.5, ALU.mult, ALU.add).then_inc(gate_low_ready, 1)

            dve.wait_ge(pool_steps, 3)

            def chunked(x):
                return x.rearrange("p (n c) -> p n c", c=C)

            def pair(j):
                def packed(kind):
                    return pk[:, :, bass.ds(j, 1), kind, :].rearrange("p n o c -> p n (o c)")

                dve.wait_ge(decay_ready, j + 1)
                dve.tensor_tensor_scan(b_c[:, :], reset[:, :], b_ld[:, :], 0.0, ALU.mult, ALU.add).then_inc(decay_sums, 1)
                dve.wait_ge(decay_sums, 2 * j + 1)
                dve.tensor_tensor(b_ld[:, :], b_c[:, :], b_ld[:, :], ALU.subtract).then_inc(decay_sums, 1)
                dve.wait_ge(z_evacuated[0], 2 * j + 3)
                own.link(dve.scalar_tensor_tensor(out=b_rs[:, :], in0=zr[:, 0:T], scalar=VD("mu_r", j), in1=b_rs[:, :],
                                                  op0=ALU.mult, op1=ALU.add))
                dve.wait_ge(a_ready, j + 1)
                dve.wait_ge(z_evacuated[1], 2 * j + 3)
                dve.scalar_tensor_tensor(out=b_ks[:, :], in0=zk[:, 0:T], scalar=VD("mu_k", j), in1=b_ks[:, :],
                                         op0=ALU.mult, op1=ALU.add).then_inc(k_shifted, 1)
                dve.wait_ge(k_shifted, j + 1)
                dve.wait_ge(z_evacuated[2], j + 2)
                own.link(dve.scalar_tensor_tensor(out=packed(4), in0=chunked(zv[:, 0:T]), scalar=VD("mu_v", j),
                                                  in1=chunked(b_t[:, :]), op0=ALU.mult, op1=ALU.add))
                own.link(dve.tensor_scalar(b_t[:, :], b_a[:, :], -1.0, VD("ka", j), ALU.add, ALU.mult))
                own.link(dve.scalar_tensor_tensor(out=b_t[:, :], in0=b_t[:, :], scalar=1.0, in1=b_ks[:, :],
                                                  op0=ALU.add, op1=ALU.mult))
                dve.wait_ge(exps_ready, j + 1)
                dve.tensor_tensor(packed(1), chunked(b_rs[:, :]), chunked(b_e1[:, :]), ALU.mult)
                dve.tensor_tensor(packed(3), chunked(b_t[:, :]), chunked(b_c[:, :]), ALU.mult)
                dve.tensor_copy(PCH[:, :, bass.ds(j, 1)], chunked(b_e1[:, :])[:, :, C - 1:C])
                dve.wait_ge(norms_ready, j + 1)
                own.link(dve.tensor_scalar(nrm[:, :], nrm[:, :], 1e-12, None, ALU.max))
                dve.reciprocal(nrm[:, :], nrm[:, :]).then_inc(norms_inverted, 1)
                dve.wait_ge(norms_spread, j + 1)
                dve.tensor_tensor(b_kk[:, :], b_kk[:, :], ps[:, 6:8, :].rearrange("p a c -> p (a c)"), ALU.mult)\
                    .then_inc(kk_ready, 1)
                dve.wait_ge(kk_ready, j + 2)
                own.link(dve.tensor_tensor(b_a[:, :], b_kk[:, :], b_a[:, :], ALU.mult))
                dve.tensor_tensor(packed(2), chunked(b_a[:, :]), chunked(b_c[:, :]), ALU.mult)
                dve.scalar_tensor_tensor(out=packed(0), in0=chunked(b_kk[:, :]), scalar=-1.0, in1=chunked(b_ld[:, :]),
                                         op0=ALU.mult, op1=ALU.mult).then_inc(pair_packed, 1)

            def conv(j):
                dve.wait_ge(z_evacuated[0], 2 * j + 2)
                dve.wait_ge(z_evacuated[1], 2 * j + 2)
                own.link(dve.scalar_tensor_tensor(out=glu[:, TAPS - 1:TAPS - 1 + T], in0=b_sq[:, :], scalar=1.0,
                                                  in1=zval[:, :], op0=ALU.add, op1=ALU.mult))
                dve.wait_ge(conv_stored, 16 * j + 16)

                def tap(s):
                    return convwh[:, bass.ds(j * TAPS + s, 1)]

                for k in range(TAPS):
                    for t0 in (0, HALF):
                        out, x = yc[:, t0:t0 + HALF], glu[:, k + t0:k + t0 + HALF]
                        if k == 0:
                            ins = dve.tensor_scalar(out, x, tap(0), VD("convb", j), ALU.mult, ALU.add)
                        else:
                            ins = dve.scalar_tensor_tensor(out=out, in0=x, scalar=tap(k), in1=out, op0=ALU.mult,
                                                           op1=ALU.add)
                        if k < TAPS - 1:
                            own.link(ins, 1)
                        elif t0 == 0:
                            own.link(ins, 0)
                ins.then_inc(conv_done, 1)

            conv(0)
            with dve.Fori(0, PAIRS - 1) as j:
                own.enter(j, 68)
                pair(j)
                conv(j + 1)
            own.leave(PAIRS - 1)
            pair(PAIRS - 1)

            dve.wait_ge(conv_stored, 16 * (PAIRS + 1))
            dve.wait_ge(pair_packed, PAIRS + 1)
            for x in bdbkv:
                dve.memset(x, 0.0).then_inc(bd_zeroed, 1)
            def bank(b, q, w):
                return ps[:, 3 * b + q, 0:PAIRS * w].rearrange("p (a w) -> p a w", a=PAIRS)

            def scan_r(i, b):
                dve.wait_ge(scan_products, 8 * i + 4 * b + 1)
                dve.tensor_copy(flat(R), ps[:, 6, 0:256]).then_inc(ru_ready, 1)

            def scan_u(i, b):
                dve.wait_ge(scan_products, 8 * i + 4 * b + 2)
                dve.tensor_copy(flat(U), ps[:, 6, 256:512]).then_inc(ru_ready, 1)

            def scan_s(i, b):
                dve.wait_ge(scan_products, 8 * i + 4 * b + 3)
                own.link(dve.tensor_tensor(flat(Stmp), ps[:, 7, 0:256], flat(S[b]), ALU.add))
                decay = PCH[:, bass.ds(2 * i + b, 1), :].rearrange("p o a -> p (o a)").unsqueeze(2)\
                    .to_broadcast([P, PAIRS, HD])
                dve.tensor_tensor(S[1 - b][:, :, :], Stmp[:, :, :], decay, ALU.mult).then_inc(state_ready, 1)

            def prepare(i, u, scan):
                def step(f, b):
                    if scan:
                        f(i - 1, b)

                for b in range(2):
                    dve.wait_ge(gram_products[b], 2 * i + 1)
                    g1, g2 = bank(b, 0, P), bank(b, 1, P)
                    dve.tensor_tensor(LT[b][:, :, :], g1[:, :, 0:C], over_pairs(K("strict")), ALU.mult)\
                        .then_inc(masked[b], 1)
                    dve.tensor_tensor(arb[u][b], twice(g1[:, :, C:P]), over_pairs2(K("incl2")), ALU.mult)\
                        .then_inc(masked[b], 1)
                    dve.wait_ge(gram_products[b], 2 * i + 2)
                    dve.tensor_tensor(aak[u][b], twice(g2[:, :, 0:C]), over_pairs2(K("strict2")), ALU.mult)
                    dve.tensor_tensor(ark[u][b], twice(g2[:, :, C:P]), over_pairs2(K("incl2")), ALU.mult)\
                        .then_inc(masked[b], 1)
                step(scan_r, 0)
                for b in range(2):
                    dve.wait_ge(t_products[b], 2 * NL * i + 1)
                    dve.tensor_copy(Ti[b][:, :, :], bank(b, 2, C)).then_inc(ti_ready[b], 1)
                step(scan_u, 0)
                for lv in range(NL):
                    if lv == 2:
                        step(scan_u, 1)
                    for b in range(2):
                        if lv < NL - 1:
                            dve.wait_ge(t_products[b], 2 * NL * i + 2 * lv + 2)
                            dve.tensor_tensor(Ti[b][:, :, :], Ti[b][:, :, :], bank(b, 1, C), ALU.add)\
                                .then_inc(ti_ready[b], 1)
                        dve.wait_ge(t_products[b], 2 * NL * i + min(2 * lv + 3, 2 * NL))
                        dve.tensor_tensor(flat2(TiT2[u][b]), flat2(TiT2[u][b]), ps[:, 3 * b + 2, :], ALU.add)\
                            .then_inc(tit_ready[b], 1)
                    if lv < 3:
                        step((scan_s, scan_r, scan_s)[lv], (0, 1, 1)[lv])

            prepare(0, 0, False)
            with dve.Fori(0, NCH // 4 - 1) as i:
                own.enter(i, 4)
                prepare(2 * i + 1, 1, True)
                prepare(2 * i + 2, 0, True)
            own.leave(NCH // 4 - 1)
            prepare(NCH // 2 - 1, 1, True)
            for b in range(2):
                for f in (scan_r, scan_u, scan_s):
                    f(NCH // 2 - 1, b)

            low = ps[:, 6:8, :].rearrange("p a c -> p (a c)")
            banks = lambda q: ps[:, q:q + 2, :].rearrange("p a c -> p (a c)")
            one = lambda p, kind: pk[:, :, p, kind, :]
            wide = lambda x: x.unsqueeze(2).to_broadcast([x.shape[0], NCH, HD])

            def centre(p):
                q, yv = p % 2, Yall[:, :, p, :]
                own.link(dve.tensor_reduce(gst[:, q, 0, :], yv, AX_X, ALU.add))
                own.link(dve.tensor_scalar(gst[:, q, 0, :], gst[:, q, 0, :], -1.0 / HD, None, ALU.mult))
                dve.tensor_tensor(chunked(Yc[q][:, :]), yv, wide(gst[:, q, 0, :]), ALU.add).then_inc(gn_centred, 1)
                dve.tensor_scalar(bonesrk[q][:, :], K("bones"), V("rk", p), None, ALU.mult)
                dve.tensor_tensor(chunked(bonus[q][:, :]), one(p, 1), one(p, 3), ALU.mult).then_inc(bonus_ready, 1)

            def normalise(p):
                q = p % 2
                dve.wait_ge(gn_squared, p + 1)
                dve.tensor_reduce(gst[:, q, 1, :], chunked(ysq[q][:, :]), AX_X, ALU.add).then_inc(gn_vars, 1)
                dve.wait_ge(gn_std_ready, p + 1)
                own.link(dve.reciprocal(gst[:, q, 3, :], gst[:, q, 2, :]))
                dve.wait_ge(gn_centred, p + 1)
                for h2 in range(2):
                    rows = slice(64 * h2, 64 * h2 + 64)
                    last = dve.tensor_tensor(Ybd[q][rows, :, h2, :], chunked(Yc[q][rows, :]), wide(gst[rows, q, 3, :]),
                                             ALU.mult)
                last.then_inc(ybd_ready, 1)

            def gated(p):
                b2 = bonus[p % 2]
                dve.wait_ge(heads_product, p + 1)
                own.link(dve.tensor_scalar(b1[:, :], banks(0), V("gng", p), V("gnb", p), ALU.mult, ALU.add))
                dve.wait_ge(bonus_product, p + 1)
                own.link(dve.tensor_tensor(chunked(b2[:, :]), chunked(banks(2)), one(p, 4), ALU.mult))
                own.link(dve.tensor_tensor(b1[:, :], b1[:, :], b2[:, :], ALU.add))
                dve.wait_ge(gate_product, p + 1)
                dve.tensor_tensor(yT[:, p, :], b1[:, :], banks(4), ALU.mult).then_inc(heads_half_ready, 1)

            dve.wait_ge(y_ready, NCH + 2)
            dve.wait_ge(state_ready, NCH + 1)
            dve.wait_ge(zeros_stored, 16 * ZEROS)
            centre(0)
            dve.wait_ge(ln_sums, 1)
            for j in range(PAIRS):
                dve.scalar_tensor_tensor(out=yconv[:, j, :], in0=low, scalar=-1.0 / 512, in1=yconv[:, j, :],
                                         op0=ALU.mult, op1=ALU.add).then_inc(ln_centred, 1)
            dve.wait_ge(bd_zeroed, 10)
            normalise(0)
            centre(1)
            dve.wait_ge(ln_std_ready, 1)
            own.link(dve.reciprocal(lnstd[:, :], lnstd[:, :]))
            dve.wait_ge(ln_centred, PAIRS)
            dve.wait_ge(ln_squared, PAIRS)
            for j in range(PAIRS):
                dve.tensor_tensor(yconv[:, j, :], yconv[:, j, :], lnstd[:, :], ALU.mult).then_inc(ln_normed, 1)
            gated(0)
            normalise(1)
            centre(2)
            for j in range(PAIRS):
                dve.wait_ge(ln_act_steps, 2 * j + 2)
                dve.scalar_tensor_tensor(out=yconv[:, j, :], in0=squares[j][:, :], scalar=1.0, in1=yconv[:, j, :],
                                         op0=ALU.add, op1=ALU.mult).then_inc(conv_half_ready, 1)
            gated(1)
            normalise(2)
            centre(3)
            gated(2)
            normalise(3)
            gated(3)
            dve.sem_inc(h_ready, 2)
            dve.sem_inc(logits_ready, 1)


            dve.wait_ge(router_loaded, 48)

            def residual(n, b, i):
                row = h[:, bass.ds(n, 1), :].rearrange("p o d -> p (o d)")
                dve.wait_ge(out_product_done, n + 3)
                dve.wait_ge(xo_loaded[b], 16 * i + 16)
                dve.tensor_tensor(row, banks(2 * b), xo[b][:, :], ALU.add).then_inc(h_ready, 1)
                dve.wait_ge(h_rms_ready, n + 1)
                own.link(dve.reciprocal(rstd2[:, bass.ds(n, 1)], std2[:, bass.ds(n, 1)]))
                dve.wait_ge(u2_kept, n + 1)
                dve.scalar_tensor_tensor(out=u2s[b][:, :], in0=row, scalar=rstd2[:, bass.ds(n, 1)], in1=fgain[:, :],
                                         op0=ALU.mult, op1=ALU.mult).then_inc(u2_ready, 1)

            def keep_logits(n):
                dve.wait_ge(logit_product, n + 1)
                dve.tensor_tensor(lg[:, bass.ds(n, 1), :].rearrange("p o d -> p (o d)"), ps[:, 6, 0:G + E], rbias[:, :],
                                  ALU.add).then_inc(logits_ready, 1)

            residual(0, 0, 0)
            with dve.Fori(0, TT // 2 - 1) as i:
                own.enter(i, 2)
                for b in range(2):
                    residual(2 * i + b + 1, 1 - b, i + b)
                    keep_logits(2 * i + b)
            own.leave(TT // 2 - 1)
            residual(TT - 1, 1, TT // 2 - 1)
            keep_logits(TT - 2)
            keep_logits(TT - 1)
            dve.wait_ge(logits_ready, TT + 1)

            def bc(x, n):
                return x.unsqueeze(2).to_broadcast([P, TT, n])

            def first_max(x, n, top, work, onehot, prefer):
                own.link(dve.tensor_reduce(top[:, :], x, AX_X, ALU.max))
                own.link(dve.tensor_tensor(work[:, :, :], x, bc(top, n), ALU.is_equal))
                own.link(dve.tensor_tensor(work[:, :, :], work[:, :, :], prefer.unsqueeze(1).to_broadcast([P, TT, n]),
                                           ALU.mult))
                own.link(dve.tensor_reduce(gtop[:, :], work[:, :, :], AX_X, ALU.max))
                own.link(dve.tensor_tensor(onehot[:, :, :], work[:, :, :], bc(gtop, n), ALU.is_equal))

            gl = lg[:, :, 0:G]
            el = lg[:, :, G:G + E].rearrange("p t (g e) -> p t g e", g=G)
            first_max(gl, G, gmax, gl1, og, K("prefer4"))
            dve.tensor_tensor(gl2[:, :, :], gl, bc(gmax, G), ALU.subtract).then_inc(route_steps, 1)
            four = lambda x: x.rearrange("p t (g e) -> p t g e", g=G)
            by_group = og.unsqueeze(3).to_broadcast([P, TT, G, EPG])
            by_expert = lambda x: x.unsqueeze(2).to_broadcast([P, TT, G, EPG])
            own.link(dve.tensor_tensor(four(r_a), el, by_group, ALU.mult))
            own.link(dve.tensor_reduce(esel[:, :, :], r_a.rearrange("p t (g e) -> p t e g", g=G), AX_X, ALU.add))
            first_max(esel, EPG, m1, ew, o1, K("prefer8"))
            own.link(dve.scalar_tensor_tensor(out=flat(e2nd), in0=flat(o1), scalar=-1e30, in1=flat(esel),
                                              op0=ALU.mult, op1=ALU.add))
            first_max(e2nd, EPG, m2, ew, o2, K("prefer8"))
            dve.tensor_tensor(dm[:, :], m2[:, :], m1[:, :], ALU.subtract).then_inc(route_steps, 1)
            dve.tensor_tensor(four(O1), by_group, by_expert(o1), ALU.mult)
            own.link(dve.tensor_tensor(four(O2), by_group, by_expert(o2), ALU.mult))
            dve.tensor_tensor(flat(Os), flat(O1), flat(O2), ALU.add).then_inc(route_steps, 1)
            dve.wait_ge(route_exps, 2)
            own.link(dve.tensor_reduce(gsum[:, :], gl2[:, :, :], AX_X, ALU.add))
            own.link(dve.reciprocal(gp[:, :], gsum[:, :]))
            own.link(dve.tensor_scalar(m1[:, :], dm[:, :], 1.0, None, ALU.add))
            own.link(dve.reciprocal(m2[:, :], m1[:, :]))
            own.link(dve.tensor_tensor(gate[0][:, :], m2[:, :], gp[:, :], ALU.mult))
            own.link(dve.tensor_tensor(gate[1][:, :], gate[0][:, :], dm[:, :], ALU.mult))
            dve.wait_ge(count_products, 1)
            own.link(dve.memset(tbase[:, 0, :], 0.0))
            own.link(dve.tensor_copy(flat(r_b), ps[:, 1, 0:TT * E]))
            for n in range(1, TT):
                own.link(dve.tensor_tensor(tbase[:, n, :], tbase[:, n - 1, :], r_b[:, n - 1, :], ALU.add))
            own.link(dve.tensor_tensor(cnt[:, :], tbase[:, TT - 1, :], r_b[:, TT - 1, :], ALU.add))
            own.link(dve.tensor_tensor(flat(rank), ps[:, 0, 0:TT * E], flat(tbase), ALU.add))
            own.link(dve.tensor_scalar(nb[:, :], cnt[:, :], float(BLK), None, ALU.is_gt))
            for q in range(2, T // BLK):
                own.link(dve.scalar_tensor_tensor(out=nb[:, :], in0=cnt[:, :], scalar=float(q * BLK), in1=nb[:, :],
                                                  op0=ALU.is_gt, op1=ALU.add))
            own.link(dve.tensor_tensor_scan(incl[:, :], K("ones", E), nb[:, :], 0.0, ALU.mult, ALU.add))
            own.link(dve.tensor_tensor(excl[:, :], incl[:, :], nb[:, :], ALU.subtract))
            own.link(dve.tensor_scalar(excl[:, :], excl[:, :], float(BLK), float((E - 1) * BLK), ALU.mult, ALU.add))
            own.link(dve.tensor_tensor(excl[:, :], excl[:, :], K("ebase"), ALU.subtract))
            over_tiles = lambda x: x.unsqueeze(1).to_broadcast([P, TT, E])
            own.link(dve.tensor_scalar(flat(r_a), flat(rank), float(BLK), None, ALU.is_ge))
            own.link(dve.tensor_tensor(r_a[:, :, :], r_a[:, :, :], over_tiles(excl), ALU.mult))
            own.link(dve.tensor_tensor(r_b[:, :, :], rank[:, :, :], over_tiles(K("ebase")), ALU.add))
            own.link(dve.tensor_tensor(flat(slotm), flat(r_a), flat(r_b), ALU.add))
            for k, O in enumerate((O1, O2)):
                own.link(dve.tensor_tensor(flat(r_a), flat(slotm), flat(O), ALU.mult))
                own.link(dve.tensor_reduce(gsum[:, :], r_a[:, :, :], AX_X, ALU.add))
                dve.tensor_copy(slot[k][:, :], gsum[:, :]).then_inc(slots_ready, 1)
                dve.wait_ge(slots_ready, k + 1)
            own.link(dve.tensor_tensor(ovc[0:1, :, :], incl[0:1, :].unsqueeze(1).to_broadcast([1, OVF, E]),
                                       cst[0:1, CCOL["iotam"]:CCOL["iotam"] + OVF].unsqueeze(2).to_broadcast([1, OVF, E]),
                                       ALU.is_le))
            own.link(dve.tensor_reduce(ov[0:1, 0:OVF], ovc[0:1, :, :], AX_X, ALU.add))
            own.link(dve.tensor_scalar(ov[0:1, 0:OVF], ov[0:1, 0:OVF], float(E - 1), None, ALU.min))
            own.link(dve.tensor_copy(ov[0:1, OVF:OVF + 1], incl[0:1, E - 1:E]))
            dve.tensor_copy(ctl[:, :], ov[0:1, :]).then_inc(ctl_ready, 1)

            dve.sem_inc(hidden_ready, 1)
            dve.wait_ge(ctl_ready, 1)
            novf = dve.value_load(ctl[0:1, OVF:OVF + 1], min_val=0, max_val=OVF)

            def hidden(n):
                dve.wait_ge(tanh_ready, n + 1)
                own.link(dve.scalar_tensor_tensor(out=th[:, :], in0=th[:, :], scalar=1.0, in1=ps[:, 0, :],
                                                  op0=ALU.add, op1=ALU.mult))
                dve.scalar_tensor_tensor(out=hid[:, :], in0=th[:, :], scalar=0.5, in1=ps[:, 1, :],
                                         op0=ALU.mult, op1=ALU.mult).then_inc(hidden_ready, 1)

            with dve.Fori(0, E) as e:
                own.enter(e, 1)
                hidden(e)
            own.leave(E)
            with dve.Fori(0, OVF2) as i:
                own.enter(i, 2)
                for b in range(2):
                    with dve.If(novf > 2 * i + b):
                        hidden(2 * i + b + E)
                        dve.nop()
                    with dve.Else():
                        dve.sem_inc(dve_steps, 1)
                        own.n = b + 1
            own.leave(OVF2)

            dve.sem_inc(sum_ready, 1)
            dve.wait_ge(rows_evacuated, E + 2 * OVF2 + 1)
            dve.wait_ge(ple_loaded, 48)
            def add_experts(n, b, i):
                col = bass.ds(n, 1)
                dve.wait_ge(rows_gathered[b], 32 * i + 32)
                dve.scalar_tensor_tensor(out=hs[b][:, :], in0=yg[b][0][:, :], scalar=gate[0][:, col],
                                         in1=h[:, col, :].rearrange("p o d -> p (o d)"), op0=ALU.mult,
                                         op1=ALU.add).then_inc(hs_ready, 1)
                dve.wait_ge(hs_ready, 2 * n + 1)
                dve.scalar_tensor_tensor(out=hs[b][:, :], in0=yg[b][1][:, :], scalar=gate[1][:, col],
                                         in1=hs[b][:, :], op0=ALU.mult, op1=ALU.add).then_inc(hs_ready, 1)
                dve.wait_ge(hs_rms_ready, n + 1)
                own.link(dve.reciprocal(rstd[:, col], std[:, col]))
                dve.tensor_scalar(ns[b][:, :], hs[b][:, :], rstd[:, col], None, ALU.mult).then_inc(ns_ready, 1)

            def turned(n):
                dve.wait_ge(ns_turned, n + 1)
                for q in range(2):
                    last = dve.tensor_tensor(nT[:, 4 * q:4 * q + 4, :], ps[:, q, :].rearrange("p (k c) -> p k c", k=4),
                                             V("pleg", 4 * q, 4).unsqueeze(2).to_broadcast([P, 4, P]), ALU.mult)
                last.then_inc(nT_ready, 1)

            def finish(n, b, i):
                col = bass.ds(n, 1)
                dve.wait_ge(ple_tanh_ready, n + 1)
                dve.wait_ge(p_product, n + 1)
                own.link(dve.scalar_tensor_tensor(out=th2[b][:, :], in0=th2[b][:, :], scalar=1.0, in1=banks(6),
                                                  op0=ALU.add, op1=ALU.mult))
                dve.wait_ge(out_stored[b], 16 * i + 16)
                dve.scalar_tensor_tensor(out=ob[b][:, :], in0=th2[b][:, :], scalar=0.5, in1=hs[b][:, :],
                                         op0=ALU.mult, op1=ALU.add).then_inc(sum_ready, 1)
                dve.wait_ge(sum_rms_ready, n + 1)
                own.link(dve.reciprocal(rstd2[:, col], std2[:, col]))
                dve.scalar_tensor_tensor(out=ob[b][:, :], in0=ob[b][:, :], scalar=rstd2[:, col], in1=lastg[:, :],
                                         op0=ALU.mult, op1=ALU.mult).then_inc(out_rows_ready, 1)

            add_experts(0, 0, 0)
            turned(0)
            with dve.Fori(0, TT // 2 - 1) as i:
                own.enter(i, 6)
                for b in range(2):
                    add_experts(2 * i + b + 1, 1 - b, i + b)
                    turned(2 * i + b + 1)
                    finish(2 * i + b, b, i)
            own.leave(TT // 2 - 1)
            add_experts(TT - 1, 1, TT // 2 - 1)
            turned(TT - 1)
            finish(TT - 2, 0, TT // 2 - 1)
            finish(TT - 1, 1, TT // 2 - 1)


def kernel(**inputs):
    import concourse.bacc as bacc
    from concourse.bass_utils import run_bass_kernel_spmd as run

    a = {k: np.ascontiguousarray(v) for k, v in inputs.items()}
    f = lambda x: np.ascontiguousarray(x)

    def cols(x):
        return x.reshape(-1, P).T

    def padded(x):
        out = np.zeros((P, x.shape[1]), x.dtype)
        out[:x.shape[0]] = x
        return out

    mu = a["rwkv_mu"][0]
    convw = a["conv_w"][0].reshape(TAPS, PAIRS, P).transpose(2, 1, 0).reshape(P, PAIRS * TAPS)
    parts = {"mixg": cols(a["mix_norm"][0]), "mu_r": cols(mu[0:512]), "mu_k": cols(mu[512:1024]),
             "mu_v": cols(mu[1024:1536]), "w0": cols(a["rwkv_w0"][0]), "a0": cols(a["rwkv_a0"][0]),
             "kk": cols(a["rwkv_kk"][0]), "ka": cols(a["rwkv_ka"][0]), "rk": cols(a["rwkv_rk"][0].reshape(-1)),
             "gng": cols(a["rwkv_gn_g"][0]), "gnb": cols(a["rwkv_gn_b"][0]), "convb": cols(a["conv_b"][0]),
             "lng": cols(a["conv_ln_g"][0]), "lnb": cols(a["conv_ln_b"][0]), "convw": convw,
             "mu_wa": padded(mu[1536:1600, None]), "mu_g": padded(mu[1600:1696, None]),
             "pleg": cols(a["ple_norm"][0])}
    vec = f(np.concatenate([parts[n] for n, _ in _cols], axis=1))

    def coltile(w):
        return w.reshape(KT, P, -1).transpose(1, 0, 2).reshape(P, -1)

    w_in = a["w_in"][0]
    z0 = D
    w_conv = f(np.stack([coltile(w_in[:, g * 512 + P * j:g * 512 + P * j + P]) for j in range(4) for g in range(2)]))
    w_rkv = f(np.stack([coltile(w_in[:, z0 + g * 512 + P * j:z0 + g * 512 + P * j + P])
                        for j in range(4) for g in range(3)]))
    arrays = {
        "x": a["x"][0], "cst": constants(), "vec": vec, "w_conv": w_conv, "w_rkv": w_rkv,
        "w_wa": f(coltile(w_in[:, z0 + 1536:z0 + 1600])), "w_g": f(coltile(w_in[:, z0 + 1600:z0 + 1696])),
        "wa2": f(np.concatenate([a["rwkv_w2"][0], a["rwkv_a2"][0]], axis=0).reshape(64, 4, P).transpose(1, 0, 2)),
    }
    arrays |= {
        "g2": a["rwkv_g2"][0], "w_out": a["w_out"][0],
        "rw": f(np.concatenate([a["router_group_w"][0], a["router_expert_w"][0].transpose(1, 0, 2).reshape(D, E)], axis=1)),
        "rb": f(np.concatenate([a["router_group_b"][0], a["router_expert_b"][0].reshape(E)])),
        "ffg": a["ffn_norm"][0], "wg": a["expert_w_gate"][0], "wu": a["expert_w_up"][0], "wd": a["expert_w_down"][0],
        "plew": a["ple_gate_w"][0], "projw": a["ple_proj_w"][0], "lastg": a["final_norm"], "p": a["p"][0, 0],
    }
    nc = bacc.Bacc("TRN2", target_bir_lowering=False, num_devices=1)
    t = {k: nc.dram_tensor("in_" + k, v.shape, mybir.dt.from_np(v.dtype), kind="ExternalInput").ap() for k, v in arrays.items()}
    t["out"] = nc.dram_tensor("out", (T, D), F32, kind="ExternalOutput").ap()
    t["yconv"] = nc.dram_tensor("dr_yconv", (PAIRS, P, T), F32, kind="Internal").ap()
    t["xbuf"] = nc.dram_tensor("dr_xbuf", (NBLK * BLK, D), F32, kind="Internal").ap()
    t["ybuf"] = nc.dram_tensor("dr_ybuf", (NBLK * BLK, D), F32, kind="Internal").ap()
    program(nc, t)
    r = run(nc, [{"in_" + k: v for k, v in arrays.items()}], core_ids=[0])
    return r.results[0]["out"].reshape(1, T, D)
```
